# Optimizing a Trainium2 kernel written in Bass

```python
import math
import jax, jax.numpy as jnp
from jax import lax
import numpy as np

D_MODEL = 1024
BATCH = 1
SEQ = 1024
DEPTH = 1

N_META = 16
DN_HEAD_DIM = 128
DN_HEADS = D_MODEL // DN_HEAD_DIM
DN_KEY_DIM = DN_HEADS * DN_HEAD_DIM
DN_VAL_DIM = DN_HEADS * DN_HEAD_DIM
QKV_DIM = 2 * DN_KEY_DIM + DN_VAL_DIM
DN_CONV = 4
CHUNK = 64
LEAD_PAD = (-N_META) % CHUNK
POOL_GROUPS = 4
POOL_WINDOWS = (2, 4, 8, 16)
POOL_GROUP_DIM = D_MODEL // 8
POOL_WIDTH = POOL_GROUPS * POOL_GROUP_DIM
POOL_OUT_GROUP = D_MODEL // POOL_GROUPS
N_BRANCHES = 2
SPLIT_SIZES = (QKV_DIM, DN_VAL_DIM, DN_HEADS, DN_HEADS, POOL_WIDTH, N_BRANCHES * D_MODEL)
IN_DIM = QKV_DIM + DN_VAL_DIM + 2 * DN_HEADS + POOL_WIDTH + N_BRANCHES * D_MODEL
D_FF = 256 * ((8 * D_MODEL // 3 + 255) // 256)
FFN_CONV = 3
NORM_EPS = 1e-6

kernel_name = 'hybrid_gdn_pool_meta_block'

def rms_norm(x, gain):
    xf = x.astype(jnp.float32)
    y = xf * lax.rsqrt(jnp.mean(xf * xf, axis=-1, keepdims=True) + NORM_EPS) * gain.astype(jnp.float32)
    return y.astype(x.dtype)

def l2_normalize(x):
    xf = x.astype(jnp.float32)
    return xf * lax.rsqrt(jnp.sum(xf * xf, axis=-1, keepdims=True) + NORM_EPS)

def causal_depthwise_conv(x, w):
    k_width = w.shape[0]
    length = x.shape[1]
    xp = jnp.pad(x, ((0, 0), (k_width - 1, 0), (0, 0)))
    out = xp[:, 0:length] * w[0]
    for j in range(1, k_width):
        out = out + xp[:, j:j + length] * w[j]
    return out

def chunk_gated_delta_rule(q, k, v, g, beta):
    b, t, h, dk = k.shape
    dv = v.shape[-1]
    n = t // CHUNK

    def chunks(a):
        a = a.reshape((b, n, CHUNK, h) + a.shape[3:])
        return jnp.moveaxis(a, 3, 1)

    q = chunks(q) * (dk ** -0.5)
    k = chunks(k)
    v = chunks(v)
    beta = chunks(beta)
    g = lax.cumsum(chunks(g), axis=3)
    idx = jnp.arange(CHUNK)
    causal = idx[:, None] >= idx[None, :]
    strict = idx[:, None] > idx[None, :]
    decay = jnp.exp(jnp.where(causal, g[..., :, None] - g[..., None, :], -jnp.inf))
    kb = k * beta[..., None]
    lower = jnp.where(strict, jnp.einsum('bhncd,bhnsd->bhncs', kb, k) * decay, 0.0)
    eye = jnp.eye(CHUNK, dtype=lower.dtype)
    tinv = lax.linalg.triangular_solve(lower + eye, jnp.broadcast_to(eye, lower.shape),
                                       left_side=True, lower=True, unit_diagonal=True)
    u = jnp.einsum('bhncs,bhnsv->bhncv', tinv, v * beta[..., None])
    w = jnp.einsum('bhncs,bhnsd->bhncd', tinv, kb * jnp.exp(g)[..., None])
    qk = jnp.where(causal, jnp.einsum('bhncd,bhnsd->bhncs', q, k) * decay, 0.0)
    q_dec = q * jnp.exp(g)[..., None]
    k_dec = k * jnp.exp(g[..., -1:] - g)[..., None]
    g_tot = jnp.exp(g[..., -1])

    def step(state, inp):
        q_i, k_i, u_i, w_i, qk_i, gt_i = inp
        v_new = u_i - jnp.einsum('bhck,bhkv->bhcv', w_i, state)
        o_i = jnp.einsum('bhck,bhkv->bhcv', q_i, state) + jnp.einsum('bhcs,bhsv->bhcv', qk_i, v_new)
        state = state * gt_i[..., None, None] + jnp.einsum('bhck,bhcv->bhkv', k_i, v_new)
        return state, o_i

    xs = (jnp.moveaxis(q_dec, 2, 0), jnp.moveaxis(k_dec, 2, 0), jnp.moveaxis(u, 2, 0),
          jnp.moveaxis(w, 2, 0), jnp.moveaxis(qk, 2, 0), jnp.moveaxis(g_tot, 2, 0))
    state0 = jnp.zeros((b, h, dk, dv), jnp.float32)
    _, o = lax.scan(step, state0, xs)
    o = jnp.moveaxis(o, 0, 2)
    return jnp.moveaxis(o, 1, 3).reshape(b, t, h, dv)

def multiscale_causal_pool(p, w_pool, pool_scale):
    b, l, _ = p.shape
    pg = p.astype(jnp.float32).reshape(b, l, POOL_GROUPS, POOL_GROUP_DIM)
    csum = lax.cumsum(pg, axis=1)
    pos = jnp.arange(l)
    outs = []
    for gi, win in enumerate(POOL_WINDOWS):
        c = csum[:, :, gi]
        lagged = jnp.pad(c, ((0, 0), (win, 0), (0, 0)))[:, :l]
        count = jnp.minimum(pos + 1, win).astype(jnp.float32)[None, :, None]
        outs.append((c - lagged) / count - pg[:, :, gi])
    pooled = jnp.stack(outs, axis=2)
    y = jnp.einsum('blgc,gcd->blgd', pooled, w_pool.astype(jnp.float32)).reshape(b, l, D_MODEL)
    return (y * pool_scale.astype(jnp.float32)).astype(p.dtype)

def hybrid_mixer(u, w_in, conv_qkv, a_log, dt_bias, head_norm, w_pool, pool_scale, w_out):
    b, l, _ = u.shape
    proj = jnp.einsum('bld,dp->blp', u, w_in)
    offsets = [int(o) for o in np.cumsum(SPLIT_SIZES)[:-1]]
    qkv, z, b_raw, a_raw, pool_in, gate_pre = jnp.split(proj, offsets, axis=-1)
    qkv = jax.nn.silu(causal_depthwise_conv(qkv, conv_qkv))
    q, k, v = jnp.split(qkv, [DN_KEY_DIM, 2 * DN_KEY_DIM], axis=-1)
    q = l2_normalize(q.reshape(b, l, DN_HEADS, DN_HEAD_DIM))
    k = l2_normalize(k.reshape(b, l, DN_HEADS, DN_HEAD_DIM))
    v = v.reshape(b, l, DN_HEADS, DN_HEAD_DIM).astype(jnp.float32)
    beta = jax.nn.sigmoid(b_raw.astype(jnp.float32))
    g = -jnp.exp(a_log.astype(jnp.float32)) * jax.nn.softplus(
        a_raw.astype(jnp.float32) + dt_bias.astype(jnp.float32))
    pad_r = (-(LEAD_PAD + l)) % CHUNK

    def pad_t(a):
        return jnp.pad(a, [(0, 0), (LEAD_PAD, pad_r)] + [(0, 0)] * (a.ndim - 2))

    o = chunk_gated_delta_rule(pad_t(q), pad_t(k), pad_t(v), pad_t(g), pad_t(beta))
    o = o[:, LEAD_PAD:LEAD_PAD + l]
    zf = z.astype(jnp.float32).reshape(b, l, DN_HEADS, DN_HEAD_DIM)
    o = (o * lax.rsqrt(jnp.mean(o * o, axis=-1, keepdims=True) + NORM_EPS)
         * head_norm.astype(jnp.float32) * jax.nn.silu(zf))
    y_a = o.reshape(b, l, DN_VAL_DIM).astype(u.dtype)
    y_b = multiscale_causal_pool(pool_in, w_pool, pool_scale)
    g_a, g_b = jnp.split(jax.nn.sigmoid(gate_pre), 2, axis=-1)
    y = g_a * y_a + g_b * y_b
    return jnp.einsum('bld,de->ble', y, w_out)

def conv_gated_mlp(u, w_up, conv_ffn, w_down):
    hid = jnp.einsum('bld,df->blf', u, w_up)
    hid = causal_depthwise_conv(hid, conv_ffn)
    gate, val = jnp.split(hid, 2, axis=-1)
    return jnp.einsum('blf,fd->bld', jax.nn.silu(gate) * val, w_down)

def setup_inputs(seed: int = 0) -> dict:
    key = jax.random.key(seed)
    ks = jax.random.split(key, 16)
    f32 = jnp.float32

    def normal(k, shape, scale):
        return jax.random.normal(k, shape, f32) * scale

    x = normal(ks[0], (BATCH, SEQ, D_MODEL), 1.0)
    meta_tokens = normal(ks[1], (N_META, D_MODEL), 1.0)
    norm_mix = 1.0 + normal(ks[2], (DEPTH, D_MODEL), 0.02)
    w_in = normal(ks[3], (DEPTH, D_MODEL, IN_DIM), D_MODEL ** -0.5)
    conv_qkv = normal(ks[4], (DEPTH, DN_CONV, QKV_DIM), DN_CONV ** -0.5)
    a_log = jnp.log(jax.random.uniform(ks[5], (DEPTH, DN_HEADS), f32, 1.0, 16.0))
    dt = jnp.exp(jax.random.uniform(ks[6], (DEPTH, DN_HEADS), f32, math.log(1e-3), math.log(1e-1)))
    dt_bias = dt + jnp.log(-jnp.expm1(-dt))
    head_norm = 1.0 + normal(ks[7], (DEPTH, DN_HEAD_DIM), 0.02)
    w_pool = normal(ks[8], (DEPTH, POOL_GROUPS, POOL_GROUP_DIM, POOL_OUT_GROUP), POOL_GROUP_DIM ** -0.5)
    pool_scale = 1.0 + normal(ks[9], (DEPTH, D_MODEL), 0.02)
    w_out = normal(ks[10], (DEPTH, D_MODEL, D_MODEL), D_MODEL ** -0.5)
    norm_ffn = 1.0 + normal(ks[11], (DEPTH, D_MODEL), 0.02)
    w_up = normal(ks[12], (DEPTH, D_MODEL, 2 * D_FF), D_MODEL ** -0.5)
    conv_ffn = normal(ks[13], (DEPTH, FFN_CONV, 2 * D_FF), FFN_CONV ** -0.5)
    w_down = normal(ks[14], (DEPTH, D_FF, D_MODEL), D_FF ** -0.5)
    norm_final = 1.0 + normal(ks[15], (D_MODEL,), 0.02)
    return {'x': x, 'meta_tokens': meta_tokens, 'norm_mix': norm_mix, 'w_in': w_in,
            'conv_qkv': conv_qkv, 'a_log': a_log, 'dt_bias': dt_bias, 'head_norm': head_norm,
            'w_pool': w_pool, 'pool_scale': pool_scale, 'w_out': w_out, 'norm_ffn': norm_ffn,
            'w_up': w_up, 'conv_ffn': conv_ffn, 'w_down': w_down, 'norm_final': norm_final}

def reference(x, meta_tokens, norm_mix, w_in, conv_qkv, a_log, dt_bias, head_norm, w_pool,
              pool_scale, w_out, norm_ffn, w_up, conv_ffn, w_down, norm_final):
    b = x.shape[0]
    meta = jnp.broadcast_to(meta_tokens.astype(x.dtype)[None], (b, N_META, D_MODEL))
    h = jnp.concatenate([meta, x], axis=1)
    for layer in range(DEPTH):
        h = h + hybrid_mixer(rms_norm(h, norm_mix[layer]), w_in[layer], conv_qkv[layer], a_log[layer],
                             dt_bias[layer], head_norm[layer], w_pool[layer], pool_scale[layer], w_out[layer])
        h = h + conv_gated_mlp(rms_norm(h, norm_ffn[layer]), w_up[layer], conv_ffn[layer], w_down[layer])
    h = rms_norm(h, norm_final)
    return h[:, N_META:]


_drawn_inputs = setup_inputs


def setup_inputs(seed=0):
    import zlib

    import numpy as np

    out = dict(_drawn_inputs(seed))
    spreads = {}
    factors = {'norm_mix': 3.842,
     'head_norm': 27.535,
     'pool_scale': 22.164,
     'norm_ffn': 15.14,
     'norm_final': 8.173}
    for name, (base, spread) in spreads.items():
        noise = np.random.default_rng([zlib.crc32(name.encode()), seed]).standard_normal(out[name].shape)
        drawn = base * np.exp(spread * noise) if base else spread * noise
        out[name] = __import__('jax').numpy.asarray(drawn.astype(out[name].dtype))
    for name, factor in factors.items():
        out[name] = (out[name] * factor).astype(out[name].dtype)
    return out
```

```python
from contextlib import ExitStack

import numpy as np

import concourse.bass as bass
from concourse import mybir

F32 = mybir.dt.float32
F32R = mybir.dt.float32r
ACT = mybir.ActivationFunctionType
ALU = mybir.AluOpType
AX_X = mybir.AxisListType.X

P = 128
D = 1024
SEQ = 1024
META = 16
KT = D // P
T = META + SEQ
HEADS = 8
CH = 128
NCH = -(-T // CH)
PAD = NCH * CH - T
TP = NCH * CH
HALO = 2
TO = SEQ + HALO
OFF = META - HALO
QKV_TILES = 3 * HEADS
DFF = 2816
FT = DFF // P
EPS = 1e-6
NEG = -1e30
WINDOWS = (2, 4, 8, 16)
Z_COL = QKV_TILES * P
AB_COL = Z_COL + D
POOL_COL = AB_COL + 2 * HEADS
GA_COL = POOL_COL + 4 * P
GB_COL = GA_COL + D
IN_DIM = GB_COL + D

BLOCKS = [(0, 346), (346, 346), (692, T - 692)]
OBLOCKS = [(i * (TO // 3), TO // 3) for i in range(3)]

SUB = 16
BLKS = CH // SUB
LEVELS = [16, 32, 64]

C_ID, C_CUM, C_NEG = 0, P, 2 * P
C_LV = 3 * P
C_INV = C_LV + len(LEVELS) * P
C_ALL = C_INV + 4 * 16

W_AB = 0
W_QKV = 1
W_POOL = W_QKV + QKV_TILES
W_WPOOL = W_POOL + 4
W_ZG = W_WPOOL + 1
W_OUT = W_ZG + 3 * HEADS
W_UP0 = W_OUT + KT
W_FFN = W_UP0 + 4
FFN_ITERS = FT // 2
W_LAST = W_FFN + 6 * (FFN_ITERS - 1)
W_ALL = W_LAST + 2
SLOTS = 3

U_QKV = 3
U_POOL = U_QKV + 3 * QKV_TILES
U_WPOOL = U_POOL + 12
U_ZG = U_WPOOL + 24
U_OUT = U_ZG + 6 * HEADS
U_UP0 = U_OUT + 24
U_FFN = U_UP0 + 12

FQ, FQD, FK, FKB, FKG, FKD, FV, EGT, GCUM = range(9)

R_CONV, R_NMIX, R_NFFN, R_PSC, R_HN = 0, 96, 104, 112, 120
R_CF = 121


def constants():
    c = np.zeros((P, C_ALL), np.float32)
    r = np.arange(P)
    c[:, C_ID:C_ID + P] = np.eye(P)
    c[:, C_CUM:C_CUM + P] = r[:, None] <= r[None, :]
    c[:, C_NEG:C_NEG + P] = np.where(r[:, None] > r[None, :], -NEG, 0.0)

    def level(z):
        return ((r[:, None] // z % 2 == 1) & (r[None, :] // z == r[:, None] // z - 1)).astype(np.float32)

    for n, z in enumerate(LEVELS):
        c[:, C_LV + n * P:C_LV + (n + 1) * P] = level(z)
    for g, w in enumerate(WINDOWS):
        c[:, C_INV + g * 16:C_INV + g * 16 + w] = np.float32(w) / np.arange(1, w + 1, dtype=np.float32)
        c[:, C_INV + g * 16 + w:C_INV + (g + 1) * 16] = 1.0
    return c


REC = ["P1", "V", "O", "SU", "OT"]
STEPS = ["P1", "TKN", "V", "TKB", "GROW", "KK", "TQ", "TKG", "O", "SU", "QK", "TQD", "OT", "TT0"]
DOUBLING = ["TT0"]
for _n in range(len(LEVELS)):
    DOUBLING += [f"X{_n}", f"Y{_n}"] + ([f"T{_n}"] if _n < len(LEVELS) - 1 else [])
STEPS += DOUBLING[1:]
LAST_Y = DOUBLING[-1]
PREP_STEPS = [s for s in STEPS if s not in REC and s not in DOUBLING]
FORM = {"TKN": ("kn", 0), "TKB": ("kb", 1), "TQ": ("qn", 0), "TKG": ("kg", 1), "TQD": ("qd", 0)}
PIECES = [(0, 3), (3, 6), (6, 8)]
FILLS = {"P1": 1, "TKN": 1, "V": 1, "TKB": 1, "GROW": 1, "KK": 1, "TQ": 2, "TKG": 2, "O": 3, "SU": 2, "QK": 2,
         "TQD": 1, "OT": 2, "TT0": 1, "X0": 1, "Y0": 1, "T0": 1, "X1": 0, "Y1": 1, "T1": 1, "X2": 0, "Y2": 1}
assert sum(FILLS.values()) == 9 * len(PIECES)


def pieces_after(name):
    first = sum(FILLS[s] for s in STEPS[:STEPS.index(name)])
    return range(first, first + FILLS[name])


def units_after(name):
    return [p // len(PIECES) for p in pieces_after(name) if p % len(PIECES) == len(PIECES) - 1]


def hybrid_block(nc, x, meta_tokens, norm_mix, w_in, conv_qkv, a_log, dt_bias, head_norm, w_pool,
                 pool_scale, w_out, norm_ffn, w_up, conv_ffn, w_down, norm_final, consts, out):
    with ExitStack() as ctx:
        def sem(name):
            return ctx.enter_context(nc.semaphore(name))

        base = -(-nc.sbuf_base // 64) * 64
        room = nc.sbuf_usable_end - base
        top = [0]

        def at(name, shape, dt, offset=None):
            size = 4 * int(np.prod(shape[1:]))
            size += -size % 32
            if offset is None:
                offset = top[0]
                top[0] += size
            assert offset + size <= room, (name, offset + size, room)
            return nc.alloc_sbuf_tensor_at(name, shape, dt, offset=base + offset)

        u_hi = at("u_hi", [P, KT, T], F32R)
        u_lo = at("u_lo", [P, KT, T], F32R)
        w_raw = at("w_raw", [P, SLOTS, D], F32)
        w_hi = at("w_hi", [P, SLOTS, D], F32R)
        w_lo = at("w_lo", [P, SLOTS, D], F32R)
        cst = at("cst", [P, C_ALL], F32)
        prm = at("prm", [P, R_CF + 3 * 2 * FT], F32)
        fac = at("fac", [P, 9, NCH, HEADS], F32)
        ssq = at("ssq", [P, QKV_TILES, NCH], F32)
        tiny = at("tiny", [P, 64], F32)
        eps_t = tiny[:, 0:1]
        nss = tiny[:, 8:24]
        oss = tiny[:, 24:32]
        orr = tiny[:, 32:40]
        hdp = tiny[0:16, 40:44]
        gcur = tiny[:, 48:56]
        region = top[0]
        end = [region]

        def plan(items, start=region):
            made, offset = [], start
            for name, shape, dt in items:
                size = 4 * int(np.prod(shape[1:]))
                made.append(at(name, shape, dt, offset))
                offset += size + (-size % 32)
            end[0] = offset
            return made

        xt, xs, ntmp, prow = plan([
            ("xt", [P, 3, D], F32), ("xs", [P, 2, D], F32), ("ntmp", [P, 2, KT, P], F32),
            ("prow", [P, 3, P], F32)])
        xb, cacc, sl, tm, sq = plan([
            ("xb", [P, 3, 3 + T + 1], F32), ("cacc", [P, T], F32), ("sl", [P, TP], F32),
            ("tm", [P, NCH, P], F32), ("sq", [P, NCH, P], F32)])
        px, pa, pb, p_hi, p_lo, ab_beta, ab_g, ab_t, gtok, gtmp = plan([
            ("px", [P, 16 + T], F32), ("pa", [P, 16 + T], F32), ("pb", [P, 16 + T], F32),
            ("p_hi", [P, 4, T], F32R), ("p_lo", [P, 4, T], F32R),
            ("ab_beta", [16, TP], F32), ("ab_g", [16, TP], F32), ("ab_t", [16, TP], F32),
            ("gtok", [P, NCH * HEADS], F32), ("gtmp", [P, 3, NCH * HEADS], F32)],
            end[0])
        (ybs,) = plan([("ybs", [P, 2, TO], F32)])
        (tk, form, qnt, knt, kbt, qdt, kgt, kd, vb, nmx, ex, qkm, rr, at_m, bd, vv, st, ots, zs, gs, yl,
         blk, sol, upd) = plan([
            ("tk", [P, QKV_TILES, P], F32), ("form", [P, 2, HEADS, P], F32),
            ("qnt", [P, HEADS, P], F32), ("knt", [P, HEADS, P], F32), ("kbt", [P, HEADS, P], F32),
            ("qdt", [P, HEADS, P], F32), ("kgt", [P, HEADS, P], F32), ("kd", [P, HEADS, P], F32),
            ("vb", [P, HEADS, P], F32), ("nmx", [P, HEADS, P], F32), ("ex", [P, HEADS, P], F32),
            ("qkm", [P, HEADS, P], F32), ("rr", [P, HEADS, P], F32), ("at_m", [P, HEADS, P], F32), ("bd", [P, HEADS, P], F32),
            ("vv", [P, HEADS, P], F32), ("st", [P, HEADS, P], F32), ("ots", [P, HEADS, P], F32),
            ("zs", [P, TO], F32), ("gs", [P, TO], F32), ("yl", [P, TO], F32),
            ("blk", [BLKS * HEADS, SUB * SUB], F32), ("sol", [BLKS * HEADS, SUB * SUB], F32),
            ("upd", [BLKS * HEADS, SUB * SUB // 4], F32)])
        orx = vb
        tt_m = kbt
        bw = OBLOCKS[0][1]
        yo, yz, yg, ht = plan([
            ("yo", [P, 2, KT, bw], F32), ("yz", [P, 2, KT, bw], F32), ("yg", [P, 2, KT, bw], F32),
            ("ht", [P, KT, TO], F32)])
        h2, h2m = plan([("h2", [P, KT, D], F32), ("h2m", [HALO, D], F32)])
        after_h2 = end[0]
        hx, htmp = plan([("hx", [P, 2, D], F32), ("htmp", [P, 2, KT, P], F32)], after_h2)
        xg, xv, cg, cv, sg, a_hi, a_lo, fing, fino = plan([
            ("xg", [P, TO], F32), ("xv", [P, TO], F32), ("cg", [P, SEQ], F32), ("cv", [P, SEQ], F32),
            ("sg", [P, SEQ], F32), ("a_hi", [P, 2, SEQ], F32R), ("a_lo", [P, 2, SEQ], F32R),
            ("fing", [P, D], F32), ("fino", [P, 2, D], F32)], after_h2)

        gb = ctx.enter_context(nc.psum_tensor("gb", [P, 3, 512], F32))
        db = ctx.enter_context(nc.psum_tensor("db", [P, 4, 512], F32))
        mb = ctx.enter_context(nc.psum_tensor("mb", [P, 512], F32))

        qkv_d = nc.dram_tensor("qkv_d", [NCH * P, QKV_TILES * P], F32, kind="Internal").ap()
        yb_d = nc.dram_tensor("yb_d", [D, TO], F32, kind="Internal").ap()
        za_d = nc.dram_tensor("za_d", [D, TO], F32, kind="Internal").ap()
        yg_d = nc.dram_tensor("yg_d", [D, TO], F32, kind="Internal").ap()
        blk_d = nc.dram_tensor("blk_d", [BLKS * HEADS, SUB * SUB], F32, kind="Internal").ap()
        sol_d = nc.dram_tensor("sol_d", [BLKS * HEADS, SUB * SUB], F32, kind="Internal").ap()
        ot_d = nc.dram_tensor("ot_d", [D, PAD + T], F32, kind="Internal").ap()

        ident = cst[:, C_ID:C_ID + P]

        def lvl(n):
            return cst[:, C_LV + n * P:C_LV + (n + 1) * P]

        def over_heads(m, n=HEADS):
            return m.unsqueeze(1).broadcast_to([P, n, P])

        def per_head(f, n=HEADS):
            return f.unsqueeze(2).broadcast_to([P, n, P])

        def factor(kind, c):
            return fac[:, kind, bass.ds(c, 1), :].rearrange("p o h -> p (o h)")

        s_const = sem("s_const")
        s_zero = sem("s_zero")
        s_prow = sem("s_prow")
        s_hd = sem("s_hd")
        s_prmT = sem("s_prmT")
        s_prm = sem("s_prm")
        s_x = [sem(f"s_x{i}") for i in range(3)]
        s_nsq = sem("s_nsq")
        s_xs = sem("s_xs")
        s_nt = sem("s_nt")
        s_ntmp = sem("s_ntmp")
        s_uhi = sem("s_uhi")
        s_u = sem("s_u")
        s_w = [sem(f"s_w{i}") for i in range(SLOTS)]
        s_whi = sem("s_whi")
        s_wlo = sem("s_wlo")
        s_g = sem("s_g")
        s_gfree = sem("s_gfree")
        s_z = sem("s_z")
        s_zsig = sem("s_zsig")
        s_zfree = sem("s_zfree")
        s_na = sem("s_na")
        s_ab = sem("s_ab")
        s_abT = sem("s_abT")
        s_gtok = sem("s_gtok")
        s_gcum = sem("s_gcum")
        s_gsb = sem("s_gsb")
        s_exp = sem("s_exp")
        s_conv = sem("s_conv")
        s_sl = sem("s_sl")
        s_tmps = sem("s_tmps")
        s_tm = sem("s_tm")
        s_sq = sem("s_sq")
        s_ssq = sem("s_ssq")
        s_spill = sem("s_spill")
        s_fac = sem("s_fac")
        s_pw = sem("s_pw")
        s_phi = sem("s_phi")
        s_plo = sem("s_plo")
        s_yb = [sem(f"s_yb{i}") for i in range(2)]
        s_tk = sem("s_tk")
        s_form = {f: sem(f"s_form_{f}") for f in ("qn", "kn", "kb", "qd", "kg")}
        s_kd = sem("s_kd")
        s_vb = sem("s_vb")
        s_nm = sem("s_nm")
        s_gcp = sem("s_gcp")
        s_dec = sem("s_dec")
        s_ps = {n: sem(f"s_ps_{n}") for n in STEPS}
        s_ev = {n: sem(f"s_ev_{n}") for n in STEPS}
        s_bst = sem("s_bst")
        s_blk = sem("s_blk")
        s_sol = sem("s_sol")
        s_sst = sem("s_sst")
        s_bd = sem("s_bd")
        s_osq = sem("s_osq")
        s_oss = sem("s_oss")
        s_ort = sem("s_ort")
        s_on = sem("s_on")
        s_ot = sem("s_ot")
        s_za = sem("s_za")
        s_yg = sem("s_yg")
        s_yl = sem("s_yl")
        s_zg = sem("s_zg")
        s_gg = sem("s_gg")
        s_yin = [sem(f"s_yin{i}") for i in range(2)]
        s_y1 = sem("s_y1")
        s_yhi = sem("s_yhi")
        s_y = sem("s_y")
        s_h2x = sem("s_h2x")
        s_h2T = sem("s_h2T")
        s_h2 = sem("s_h2")
        s_h2sq = sem("s_h2sq")
        s_hx = sem("s_hx")
        s_hnt = sem("s_hnt")
        s_htmp = sem("s_htmp")
        s_u2hi = sem("s_u2hi")
        s_u2 = sem("s_u2")
        s_cg = sem("s_cg")
        s_cv = sem("s_cv")
        s_sg = sem("s_sg")
        s_act = sem("s_act")
        s_ahi = sem("s_ahi")
        s_alo = sem("s_alo")
        s_dn = sem("s_dn")
        s_dnfree = sem("s_dnfree")
        s_fg = sem("s_fg")
        s_fsq = sem("s_fsq")
        s_fin = sem("s_fin")
        s_out = [sem(f"s_out{i}") for i in range(2)]

        def gain(row, n=KT):
            return prm[:, row:row + n]

        def gflat(kind):
            return fac[:, kind, :, :].rearrange("p c h -> p (c h)")

        def pool_out(g):
            return (pb, pa)[g % 2]

        def heads(m, h):
            return m[:, h * HEADS // 2:(h + 1) * HEADS // 2, :]

        def dbank(name, h):
            return db[:, 2 * (STEPS.index(name) % 2) + h, :].rearrange("p (m c) -> p m c", m=HEADS // 2)

        block = ctx.enter_context(nc.Block())

        @block.sync
        def _(sp):
            def load_w(n, src, i=0, per=3, wide=False):
                if n >= SLOTS:
                    sp.wait_ge(s_wlo, n - SLOTS + 1 + per * i)
                dst = w_raw[:, n % SLOTS, :]
                if not wide:
                    dst = dst.rearrange("p (k c) -> p k c", k=KT)
                sp.dma_start(dst, src).then_inc(s_w[n % SLOTS], 16)

            def cols(w, c0):
                return w[0, :, bass.ds(c0, P)].rearrange("(k p) c -> p k c", p=P)

            sp.dma_start(xt[0:META, 0, :], meta_tokens).then_inc(s_x[0], 16)
            sp.dma_start(cst[:, :], consts).then_inc(s_const, 16)
            for j in range(1, 3):
                sp.dma_start(xt[:, j, :], x[0, (j - 1) * P:j * P, :]).then_inc(s_x[j], 16)
            load_w(W_AB, cols(w_in, AB_COL))
            for j in range(3, KT + 1):
                sp.wait_ge(s_xs, j - 2)
                sp.dma_start(xt[:, j % 3, :], x[0, (j - 1) * P:j * P, :]).then_inc(s_x[j % 3], 16)
            for j in range(2):
                load_w(W_QKV + j, cols(w_in, j * P))
            with sp.Fori(0, QKV_TILES // 3 - 1) as i:
                for j in range(3):
                    load_w(W_QKV + 2 + j, cols(w_in, (2 + j) * P + 3 * P * i), i)
            load_w(W_QKV + QKV_TILES - 1, cols(w_in, (QKV_TILES - 1) * P))
            for g in range(4):
                load_w(W_POOL + g, cols(w_in, POOL_COL + g * P))
            sp.wait_ge(s_wlo, W_WPOOL - SLOTS + 1)
            sp.dma_start(w_raw[:, W_WPOOL % SLOTS, :].rearrange("p (g d) -> p g d", g=4),
                         w_pool[0].rearrange("g p d -> p g d")).then_inc(s_w[W_WPOOL % SLOTS], 16)

            def load_tk(c):
                sp.dma_start(tk[:, :, :].rearrange("p t d -> p (t d)"),
                             qkv_d[bass.ds(c * P, P), :]).then_inc(s_tk, 16)

            def invert(c, n=BLKS):
                def block(b, m):
                    return m[SUB * b:SUB * (b + 1), :, SUB * b:SUB * (b + 1)]

                def rows(m, b):
                    return m[HEADS * b:HEADS * (b + 1), :].rearrange("h (r c) -> r h c", r=SUB)

                stored = 16 * c * BLKS if n < BLKS else 16 + 16 * BLKS * (c - 1)
                sp.wait_ge(s_ev["KK"], 2 * c + 2)
                for b in range(n):
                    sp.dma_start(rows(blk_d, b), block(BLKS - n + b, at_m)).then_inc(s_bst, 16)
                sp.wait_ge(s_bst, stored + 16 * n)
                sp.dma_start(blk[0:HEADS * n, :], blk_d[0:HEADS * n, :]).then_inc(s_blk, 16)
                sp.wait_ge(s_sol, c + 1)
                sp.dma_start(sol_d[0:HEADS * n, :], sol[0:HEADS * n, :]).then_inc(s_sst, 16)
                sp.wait_ge(s_sst, 16 * c + 16)
                if n < BLKS:
                    sp.wait_ge(s_zero, 4)
                for b in range(n):
                    sp.dma_start(block(BLKS - n + b, bd), rows(sol_d, b)).then_inc(s_bd, 16)

            for j, c0 in enumerate((Z_COL, GA_COL, GB_COL)):
                load_w(W_ZG + j, cols(w_in, c0))
            sp.wait_ge(s_spill, 16 * QKV_TILES)
            sp.wait_ge(s_gfree, U_ZG)
            sp.wait_ge(s_yb[0], 16 * 4)
            sp.wait_ge(s_yb[1], 16 * 4)
            sp.wait_ge(s_fac, 1)
            load_tk(0)
            sp.dma_start(yl[:, :], yb_d[0:P, :]).then_inc(s_yl, 16)
            invert(0, 1)
            sp.wait_ge(s_form["qd"], 1)
            sp.wait_ge(s_vb, 1)
            load_tk(1)
            with sp.Fori(0, HEADS - 1) as i:
                for j, c0 in enumerate((Z_COL, GA_COL, GB_COL)):
                    load_w(W_ZG + 3 + j, cols(w_in, c0 + P + P * i), i)
                invert(i + 1)
                sp.wait_ge(s_form["qd"], i + 2)
                sp.wait_ge(s_vb, i + 2)
                load_tk(i + 2)
                sp.wait_ge(s_gg, i + 1)
                sp.dma_start(yl[:, :], yb_d[bass.ds(P + P * i, P), :]).then_inc(s_yl, 16)
            for n in range(3):
                load_w(W_OUT + n, cols(w_out, n * P))
            invert(NCH - 1)
            sp.wait_ge(s_za, 16 * HEADS)
            sp.wait_ge(s_yg, 16 * (HEADS + 1))
            sp.wait_ge(s_ot, 16 * NCH)
            sp.wait_ge(s_ps["OT"], 2 * NCH)
            for b, (o, w) in enumerate(OBLOCKS):
                if b >= 2:
                    sp.wait_ge(s_y, b - 1)
                for src, dst in ((ot_d[:, PAD + OFF + o:PAD + OFF + o + w], yo), (za_d[:, o:o + w], yz),
                                 (yg_d[:, o:o + w], yg)):
                    sp.dma_start(dst[:, b % 2, :, :],
                                 src.rearrange("(k p) t -> p k t", p=P)).then_inc(s_yin[b % 2], 16)
            sp.wait_ge(s_y, 3)
            sp.dma_start(h2m[:, :], meta_tokens[OFF:META, :]).then_inc(s_h2x, 16)
            sp.dma_start(h2[:, :, :], x[0].rearrange("(t p) d -> p t d", p=P)).then_inc(s_h2x, 16)
            for n in range(3, KT):
                load_w(W_OUT + n, cols(w_out, n * P))

            def up_cols(j):
                return (j % 2) * DFF + (j // 2) * P

            for j in range(4):
                load_w(W_UP0 + j, cols(w_up, up_cols(j)))
            with sp.Fori(0, FFN_ITERS - 1) as i:
                for j in range(6):
                    if j in (2, 3):
                        load_w(W_FFN + j, w_down[0, bass.ds(2 * P * i + (j - 2) * P, P), :], i, 6, wide=True)
                    else:
                        jj = j if j < 2 else j - 2
                        load_w(W_FFN + j, cols(w_up, up_cols(jj) + 2 * P + 2 * P * i), i, 6)
            for k in range(2):
                load_w(W_LAST + k, w_down[0, (FT - 2 + k) * P:(FT - 1 + k) * P, :], wide=True)
            sp.dma_start(fing[:, :], norm_final.rearrange("(o d) -> o d", o=1).broadcast_to([P, D])
                         ).then_inc(s_fg, 16)
            for t in range(KT):
                sp.wait_ge(s_fin, t + 1)
                sp.dma_start(out[0, t * P:(t + 1) * P, :], fino[:, t % 2, :]).then_inc(s_out[t % 2], 16)
            sp.wait_ge(s_out[0], 16 * KT // 2)
            sp.wait_ge(s_out[1], 16 * KT // 2)

        @block.gpsimd
        def _(pool):
            pool.memset(prow[:, :, :], 0.0)
            pool.memset(tiny[:, :], 0.0)
            pool.memset(ab_beta[:, :], 0.0)
            pool.memset(ab_g[:, :], 0.0).then_inc(s_zero, 1)
            pool.wait_ge(s_zero, 1)
            pool.memset(eps_t, EPS).then_inc(s_zero, 1)
            with nc.allow_non_contiguous_dma(reason="sixteen words"):
                pool.dma_start(hdp[8:16, 0:1], dt_bias.rearrange("o h -> h o")).then_inc(s_hd, 16)
                pool.dma_start(hdp[8:16, 1:2], a_log.rearrange("o h -> h o")).then_inc(s_hd, 16)

            def rows(v):
                return v.rearrange("o (i p) -> (o i) p", p=P)

            cf = conv_ffn.rearrange("o j (i p) -> (o j i) p", p=P)
            for dst, src in ((prow[0:R_NMIX, 0, :], conv_qkv.rearrange("o j (i p) -> (o j i) p", p=P)),
                             (prow[R_NMIX:R_NMIX + 8, 0, :], rows(norm_mix)),
                             (prow[R_NFFN:R_NFFN + 8, 0, :], rows(norm_ffn)),
                             (prow[R_PSC:R_PSC + 8, 0, :], rows(pool_scale)),
                             (prow[R_HN:R_HN + 1, 0, :], head_norm),
                             (prow[0:88, 1, :], cf[0:88, :]), (prow[0:44, 2, :], cf[88:132, :])):
                pool.dma_start(dst, src).then_inc(s_prow, 16)

            def w_low(n, i=0, per=3):
                pool.wait_ge(s_whi, n + 1 + per * i)
                pool.tensor_tensor(w_lo[:, n % SLOTS, :], w_raw[:, n % SLOTS, :],
                                   w_hi[:, n % SLOTS, :].bitcast(F32), ALU.subtract).then_inc(s_wlo, 1)

            w_low(W_AB)
            w_low(W_QKV)
            w_low(W_QKV + 1)
            pool.wait_ge(s_u, KT + 1)
            pool.memset(xb[:, :, 0:3], 0.0)
            pool.memset(sl[:, 0:PAD], 0.0)
            pool.memset(px[:, 0:16], 0.0)
            pool.memset(pa[:, 0:16], 0.0)
            pool.memset(pb[:, 0:16], 0.0).then_inc(s_zero, 1)

            def squares(j, i=0):
                w_low(W_QKV + 2 + j, i)
                pool.wait_ge(s_tm, 3 * i + j + 1)
                if j > 0:
                    pool.wait_ge(s_ssq, 3 * i + j)
                pool.tensor_tensor(sq[:, :, :], tm[:, :, :], tm[:, :, :], ALU.mult).then_inc(s_sq, 1)

            for j in range(3):
                squares(j)
            with pool.Fori(0, QKV_TILES // 3 - 1) as i:
                for j in range(3, 6):
                    squares(j, i)
            for n in range(W_QKV + QKV_TILES + 2, W_ZG + 3):
                w_low(n)

            def mask(c):
                pool.tensor_tensor(nmx[:, :, :], per_head(factor(GCUM, c)),
                                   over_heads(cst[:, C_NEG:C_NEG + P]), ALU.add).then_inc(s_nm, 1)

            def state_parts(c):
                pool.tensor_tensor(kd[:, :, :], tk[:, HEADS:2 * HEADS, :], per_head(factor(FKD, c)),
                                   ALU.mult).then_inc(s_kd, 1)
                pool.tensor_tensor(vb[:, :, :], tk[:, 2 * HEADS:, :], per_head(factor(FV, c)),
                                   ALU.mult).then_inc(s_vb, 1)

            def substitute(c, n=BLKS):
                n *= HEADS
                low = blk[0:n, :].rearrange("p (r c) -> p r c", c=SUB)
                inv = sol[0:n, :].rearrange("p (r c) -> p r c", c=SUB)
                pool.memset(sol[0:n, :], 0.0)
                pool.drain()
                pool.memset(sol[0:n, ::SUB + 1], 1.0)
                pool.drain()
                pool.wait_ge(s_blk, 16 * c + 16)
                for j in range(SUB - 1):
                    rest = SUB - 1 - j
                    out = upd[0:n, 0:rest * (j + 1)].rearrange("p (r c) -> p r c", c=j + 1)
                    pool.tensor_tensor(out, low[:, j, j + 1:].unsqueeze(2).broadcast_to([n, rest, j + 1]),
                                       inv[:, j, 0:j + 1].unsqueeze(1).broadcast_to([n, rest, j + 1]), ALU.mult)
                    pool.drain()
                    t = pool.tensor_tensor(inv[:, j + 1:, 0:j + 1], inv[:, j + 1:, 0:j + 1], out, ALU.subtract)
                    if j < SUB - 2:
                        pool.drain()
                t.then_inc(s_sol, 1)

            pool.wait_ge(s_fac, 1)
            pool.wait_ge(s_gfree, U_ZG)
            pool.wait_ge(s_yb[0], 16 * 4)
            pool.wait_ge(s_yb[1], 16 * 4)
            mask(0)
            pool.memset(bd[:, :, :], 0.0).then_inc(s_zero, 1)
            pool.memset(gs[:, 0:1], 0.0).then_inc(s_yg, 16)
            pool.wait_ge(s_tk, 16)
            substitute(0, 1)
            state_parts(0)
            for h in range(2):
                pool.memset(heads(st, h), 0.0).then_inc(s_ev["SU"], 1)
            with pool.Fori(0, HEADS) as i:
                pool.wait_ge(s_ev[LAST_Y], 2 * i + 2)
                mask(i + 1)
                substitute(i + 1)
                pool.wait_ge(s_ps["SU"], 2 * i + 2)
                pool.wait_ge(s_ps["OT"], 2 * i + 2)
                pool.wait_ge(s_tk, 16 * i + 32)
                state_parts(i + 1)
                for j in range(3):
                    w_low(W_ZG + 3 + j, i)
            for n in range(3, KT):
                w_low(W_OUT + n)
            for j in range(4):
                w_low(W_UP0 + j)
            with pool.Fori(0, FFN_ITERS - 1) as i:
                for j in range(6):
                    w_low(W_FFN + j, i, 6)
            w_low(W_LAST)
            w_low(W_LAST + 1)

        @block.tensor
        def _(pe):
            def w_ready(n, i=0, per=3):
                pe.wait_ge(s_wlo, n + 1 + per * i)

            def unit(n, bank, o, w, k0=0, k1=KT):
                for k in range(k0, k1):
                    w1, w2 = (v[:, n % SLOTS, k * P:(k + 1) * P] for v in (w_hi, w_lo))
                    u1, u2 = (v[:, k, o:o + w] for v in (u_hi, u_lo))
                    for m, (wt, u) in enumerate(((w1, u1), (w1, u2), (w2, u1))):
                        mm = pe.matmul(gb[:, bank, 0:w], wt, u, start=(k == 0 and m == 0),
                                       stop=(k == KT - 1 and m == 2))
                return mm

            pe.wait_ge(s_const, 16)
            pe.wait_ge(s_prow, 16 * 7)
            for r, n in enumerate((P, 88, 44)):
                pe.transpose(mb[:, r * P:r * P + n], prow[0:n, r, :], cst[0:n, C_ID:C_ID + n]).then_inc(s_prmT, 1)

            for j in range(KT + 1):
                pe.wait_ge(s_xs, j + 1)
                n = META if j == 0 else P
                for h in range(2):
                    if j >= 2:
                        pe.wait_ge(s_ntmp, 2 * (j - 2) + h + 1)
                    for k in range(4 * h, 4 * h + 4):
                        t = pe.transpose(db[:, 2 * (j % 2) + h, k % 4 * P:k % 4 * P + n],
                                         xs[0:n, j % 2, k * P:(k + 1) * P], cst[0:n, C_ID:C_ID + n])
                    t.then_inc(s_nt, 1)

            pe.wait_ge(s_u, KT + 1)
            w_ready(W_AB)
            for b, (o, w) in enumerate(BLOCKS):
                unit(W_AB, b, o, w).then_inc(s_g, 1)

            def project(n, before, i=0):
                w_ready(n, i)
                for b, (o, w) in enumerate(BLOCKS):
                    pe.wait_ge(s_gfree, before + b - 2 + 3 * 3 * i)
                    unit(n, b, o, w).then_inc(s_g, 1)

            def turn(n, first=False):
                pe.wait_ge(s_sl, n + 1)
                if not first:
                    pe.wait_ge(s_tm, n)
                for r, (c0, c1) in enumerate(((0, 4), (4, 8), (8, NCH))):
                    for c in range(c0, c1):
                        t = pe.transpose(db[:, r, (c - c0) * P:(c - c0 + 1) * P], sl[:, c * P:(c + 1) * P], ident)
                    t.then_inc(s_tmps, 1)

            for n in range(3):
                project(W_QKV + n, U_QKV + 3 * n)
                if n:
                    turn(n - 1, n == 1)
            with pe.Fori(0, QKV_TILES // 3 - 1) as i:
                for j in range(3, 6):
                    project(W_QKV + j, U_QKV + 3 * j, i)
                    turn(3 * i + j - 1)
            for g in range(4):
                project(W_POOL + g, U_POOL + 3 * g)
                if g == 0:
                    turn(QKV_TILES - 1)
            pe.wait_ge(s_ab, 1)
            pe.wait_ge(s_prm, 3)
            for c in range(NCH):
                for m, src in enumerate((ab_beta, ab_g)):
                    t = pe.transpose(mb[:, (m * NCH + c) * 16:(m * NCH + c + 1) * 16],
                                     src[:, c * P:(c + 1) * P], cst[0:16, C_ID:C_ID + 16])
            t.then_inc(s_abT, 1)
            pe.wait_ge(s_gtok, 1)
            pe.matmul(mb[:, 288:288 + NCH * HEADS], cst[:, C_CUM:C_CUM + P], gtok[:, :], start=True, stop=True)
            pe.matmul(mb[:, 360:360 + NCH * HEADS], cst[:, C_CUM + P - 1:C_CUM + P].broadcast_to([P, P]),
                      gtok[:, :], start=True, stop=True).then_inc(s_gcum, 1)
            w_ready(W_WPOOL)
            for j in range(KT):
                g = j // 2
                pe.wait_ge(s_plo, g + 1)
                ws = slice(g * 2 * P + (j % 2) * P, g * 2 * P + (j % 2 + 1) * P)
                w1, w2 = (v[:, W_WPOOL % SLOTS, ws] for v in (w_hi, w_lo))
                for b, (o, w) in enumerate(OBLOCKS):
                    pe.wait_ge(s_gfree, U_WPOOL - 3 + 3 * j + b + 1)
                    u1, u2 = (v[:, g, OFF + o:OFF + o + w] for v in (p_hi, p_lo))
                    for m, (wt, u) in enumerate(((w1, u1), (w1, u2), (w2, u1))):
                        mm = pe.matmul(gb[:, b, 0:w], wt, u, start=(m == 0), stop=(m == 2))
                    mm.then_inc(s_g, 1)

            def step(name, c, freed):
                bank = 2 * (STEPS.index(name) % 2)

                def each(inputs, op):
                    for h in range(2):
                        if freed:
                            pe.wait_ge(s_ev[freed[0]], freed[1] + h + 1)
                        for s, v in inputs:
                            pe.wait_ge(s, v + h + 1)
                        for m in range(4):
                            t = op(db[:, bank + h, m * P:(m + 1) * P], 4 * h + m)
                        t.then_inc(s_ps[name], 1)

                def turned(src):
                    return lambda o, m: pe.transpose(o, src[:, m, :], ident)

                def product(a, b):
                    return lambda o, m: pe.matmul(o, a[:, m, :], b[:, m, :], start=True, stop=True)

                done = {n: (s_ev[n], 2 * (c - 1) if n in DOUBLING and n != LAST_Y else 2 * c) for n in STEPS}
                if name in FORM:
                    f, n = FORM[name]
                    pe.wait_ge(s_form[f], c + 1)
                    each([], turned(form[:, n]))
                elif name == "GROW":
                    pe.wait_ge(s_gcp, c + 1)
                    each([], lambda o, m: pe.transpose(o, gcur[:, m:m + 1].broadcast_to([P, P]), ident))
                elif name == "KK":
                    each([done["TKN"], done["TKB"]], product(knt, kbt))
                elif name == "QK":
                    each([done["TQ"]], product(knt, qnt))
                elif name == "TT0":
                    pe.wait_ge(s_bd, 16 + 16 * BLKS * c)
                    each([], turned(bd))
                elif name[0] == "X":
                    each([done["KK" if name == "X0" else f"T{int(name[1]) - 1}"]],
                         product(at_m, bd if name == "X0" else tt_m))
                elif name == "Y0":
                    each([done["X0"], done["TT0"]], product(nmx, rr))
                elif name[0] == "Y":
                    each([done["X" + name[1]]], product(nmx, rr))
                elif name[0] == "T":
                    each([done["Y" + name[1]]], turned(rr))
                elif name == "P1":
                    pe.wait_ge(s_ev["SU"], 2 * c + 2)
                    each([done["TKG"]], product(kgt, st))
                elif name == "V":
                    each([done["P1"], done[LAST_Y]], product(rr, orx))
                elif name == "O":
                    def both(o, m):
                        pe.matmul(o, qdt[:, m, :], st[:, m, :], start=True, stop=False)
                        return pe.matmul(o, qkm[:, m, :], vv[:, m, :], start=False, stop=True)
                    each([done["V"], done["QK"], done["TQD"]], both)
                elif name == "SU":
                    pe.wait_ge(s_kd, c + 1)
                    each([done["V"]], product(kd, vv))
                elif name == "OT":
                    pe.wait_ge(s_on, c + 1)
                    each([], turned(orx))

            def same_banks(name, among):
                return [n for n in among if STEPS.index(n) % 2 == STEPS.index(name) % 2]

            pe.wait_ge(s_tm, QKV_TILES)
            for k, name in enumerate(PREP_STEPS):
                held = same_banks(name, PREP_STEPS[:k])
                step(name, 0, (held[-1], 0) if held else None)
            step("TT0", 0, (same_banks("TT0", PREP_STEPS)[-1], 0))
            pe.wait_ge(s_ev["QK"], 2)

            def piece(p, i):
                u, part = divmod(p, 3)
                t, b = divmod(u, 3)
                o, w = OBLOCKS[b]
                if part == 0:
                    if b == 0:
                        w_ready(W_ZG + t, i)
                    if t == 1:
                        pe.wait_ge(s_zfree, 3 * i + b + 1)
                    else:
                        pe.wait_ge(s_gfree, U_ZG - 3 + b + 1 + 6 * i + (3 if t == 2 else 0))
                mm = unit(W_ZG + t, b, OFF + o, w, *PIECES[part])
                if part == 2:
                    mm.then_inc(s_z if t == 0 else s_g, 1)

            with pe.Fori(0, HEADS) as i:
                for k, name in enumerate(STEPS):
                    held = same_banks(name, STEPS[:k])
                    c = i if name in REC else i + 1
                    if not held:
                        freed = (LAST_Y, 2 * i)
                    elif held[-1] in REC:
                        freed = (held[-1], 2 * i + 2 if held[-1] == "SU" else 2 * i)
                    else:
                        freed = (held[-1], 2 * i if held[-1] in DOUBLING else 2 * i + 2)
                    step(name, c, freed)
                    for p in pieces_after(name):
                        piece(p, i)
            for name, prev in (("P1", LAST_Y), ("V", "P1"), ("O", "V"), ("OT", "O")):
                step(name, NCH - 1, (prev, 2 * (NCH - 1)))

            for n in range(KT):
                w_ready(W_OUT + n)
                for b, (o, w) in enumerate(OBLOCKS):
                    pe.wait_ge(s_gfree, U_OUT - 3 + 3 * n + b + 1)
                    if n == 0:
                        pe.wait_ge(s_y, b + 1)
                    unit(W_OUT + n, b, o, w).then_inc(s_g, 1)

            def back(j):
                n, c0 = (HALO, 0) if j == 0 else (P, HALO + (j - 1) * P)
                for h in range(2):
                    if j >= 1:
                        pe.wait_ge(s_h2, 2 * (j - 1) + h + 1)
                    for k in range(4):
                        t = pe.transpose(db[0:n, h, k * P:(k + 1) * P], ht[:, 4 * h + k, c0:c0 + n], ident)
                    t.then_inc(s_h2T, 1)

            def forth(j):
                n = HALO if j == 0 else P
                pe.wait_ge(s_hx, j + 1)
                for h in range(2):
                    if j >= 1:
                        pe.wait_ge(s_htmp, 2 * (j - 1) + h + 1)
                    for k in range(4 * h, 4 * h + 4):
                        t = pe.transpose(db[:, 2 + h, k % 4 * P:k % 4 * P + n], hx[0:n, j % 2, k * P:(k + 1) * P],
                                         cst[0:n, C_ID:C_ID + n])
                    t.then_inc(s_hnt, 1)

            pe.wait_ge(s_ev["OT"], 2 * NCH)
            pe.wait_ge(s_ev["O"], 2 * NCH)
            pe.wait_ge(s_gfree, U_UP0)
            back(0)
            for j in range(KT + 1):
                if j < KT:
                    back(j + 1)
                forth(j)

            def up(n, before, i=0):
                w_ready(n, i, 6)
                for b, (o, w) in enumerate(OBLOCKS):
                    pe.wait_ge(s_gfree, before + b - 2 + 12 * i)
                    unit(n, b, o, w).then_inc(s_g, 1)

            def down(n, i):
                w_ready(n + 1, 0 if n == W_LAST else i, 6)
                pe.wait_ge(s_alo, 2 * i + 2)
                for u in range(2 * KT):
                    t, half = divmod(u, 2)
                    if u > 3:
                        pe.wait_ge(s_dnfree, 16 * i + u - 3)
                    for q in range(2):
                        a1, a2 = (v[:, q, t * P:(t + 1) * P] for v in (a_hi, a_lo))
                        w1, w2 = (v[:, (n + q) % SLOTS, half * 512:(half + 1) * 512] for v in (w_hi, w_lo))
                        for m, (a, wt) in enumerate(((a1, w1), (a1, w2), (a2, w1))):
                            mm = pe.matmul(db[:, u % 4, :], a, wt, start=(q == 0 and m == 0),
                                           stop=(q == 1 and m == 2))
                    mm.then_inc(s_dn, 1)

            pe.wait_ge(s_u2, KT + 1)
            for j in range(4):
                up(W_UP0 + j, U_UP0 + 3 * j)
            with pe.Fori(0, FFN_ITERS - 1) as i:
                up(W_FFN, U_FFN, i)
                up(W_FFN + 1, U_FFN + 3, i)
                down(W_FFN + 2, i)
                up(W_FFN + 4, U_FFN + 6, i)
                up(W_FFN + 5, U_FFN + 9, i)
                pe.wait_ge(s_dnfree, 16 * i + 2 * KT)
            down(W_LAST, FFN_ITERS - 1)

        @block.scalar
        def _(act):
            def w_high(n, i=0, per=3):
                act.wait_ge(s_w[n % SLOTS], 16 * (n // SLOTS + 1) + 16 * (per // 3) * i)
                act.activation(w_hi[:, n % SLOTS, :], w_raw[:, n % SLOTS, :], ACT.Copy).then_inc(s_whi, 1)

            def root(j, n, src, junk, done):
                act.activation(junk, src, ACT.Square, accum_out=nss[0:n, j:j + 1])
                act.drain()
                act.activation(nss[0:n, j:j + 1], nss[0:n, j:j + 1], ACT.Sqrt, bias=eps_t[0:n, :],
                               scale=1.0 / D).then_inc(done, 1)

            def norm_root(j):
                n = META if j == 0 else P
                act.wait_ge(s_x[j % 3], 16 * (j // 3 + 1))
                if j >= 2:
                    act.wait_ge(s_nt, 2 * (j - 1))
                root(j, n, xt[0:n, j % 3, :], xs[0:n, j % 2, :], s_nsq)

            act.wait_ge(s_zero, 2)
            norm_root(0)
            for r, (c0, n) in enumerate(((0, R_CF), (R_CF, 88), (R_CF + 88, 44))):
                act.wait_ge(s_prmT, 3)
                act.activation(prm[:, c0:c0 + n], mb[:, r * P:r * P + n], ACT.Copy).then_inc(s_prm, 1)
            for j in range(KT + 1):
                if j < KT:
                    norm_root(j + 1)
                n, c0 = (META, 0) if j == 0 else (P, META + (j - 1) * P)
                act.wait_ge(s_ntmp, 2 * j + 2)
                act.activation(u_hi[:, :, c0:c0 + n], ntmp[:, j % 2, :, 0:n], ACT.Copy).then_inc(s_uhi, 1)
                if j in (2, 4, 6):
                    w_high(W_AB + (j - 2) // 2)

            act.wait_ge(s_hd, 32)
            for b, (o, w) in enumerate(BLOCKS):
                act.wait_ge(s_g, b + 1)
                act.activation(ab_beta[:, PAD + o:PAD + o + w], gb[0:16, b, 0:w], ACT.Sigmoid)
                act.activation(ab_t[:, PAD + o:PAD + o + w], gb[0:16, b, 0:w], ACT.Identity,
                               bias=hdp[:, 0:1]).then_inc(s_gfree, 1)
            w_high(W_QKV + 2)
            act.drain()
            act.activation(ab_g[:, PAD:], ab_t[:, PAD:], ACT.Abs)
            act.activation(hdp[:, 2:3], hdp[:, 1:2], ACT.Exp)
            act.drain()
            act.activation(ab_g[:, PAD:], ab_g[:, PAD:], ACT.Exp, scale=-1.0)
            act.activation(ab_t[:, PAD:], ab_t[:, PAD:], ACT.Relu)
            act.drain()
            act.activation(ab_g[:, PAD:], ab_g[:, PAD:], ACT.Ln, bias=1.0).then_inc(s_na, 1)

            def silu(n):
                act.wait_ge(s_conv, n + 1)
                act.wait_ge(s_tmps, 3 * n)
                act.activation(sl[:, PAD:], cacc[:, :], ACT.Silu).then_inc(s_sl, 1)

            def by_tokens(n):
                act.wait_ge(s_sq, n)
                act.wait_ge(s_spill, 16 * n)
                for r, (c0, c1) in enumerate(((0, 4), (4, 8), (8, NCH))):
                    act.wait_ge(s_tmps, 3 * n + r + 1)
                    t = act.activation(tm[:, c0:c1, :].rearrange("p c d -> p (c d)"), db[:, r, 0:(c1 - c0) * P],
                                       ACT.Copy)
                t.then_inc(s_tm, 1)
                act.wait_ge(s_tm, n + 1)
                act.dma_start(qkv_d[:, bass.ds(n * P, P)].rearrange("(c p) d -> p c d", p=P),
                              tm[:, :, :]).then_inc(s_spill, 16)

            def qkv_tile(j, i=0):
                n = j + 3 * i
                if j > 0:
                    act.wait_ge(s_g, 3 * n + 3)
                    w_high(W_QKV + j + 2, i)
                for b, (o, w) in enumerate(BLOCKS):
                    if b == 0 and j >= 3:
                        act.wait_ge(s_conv, n - 2)
                    act.wait_ge(s_g, U_QKV + 3 * n + b + 1)
                    act.activation(xb[:, j % 3, 3 + o:3 + o + w], gb[:, b, 0:w], ACT.Copy).then_inc(s_gfree, 1)
                    if b == 1 and j > 0:
                        silu(n - 1)
                if j > 0:
                    by_tokens(n - 1)

            act.wait_ge(s_zero, 3)
            for j in range(3):
                qkv_tile(j)
            with act.Fori(0, QKV_TILES // 3 - 1) as i:
                for j in range(3, 6):
                    qkv_tile(j, i)

            for g in range(4):
                act.wait_ge(s_g, 3 * (W_POOL + g))
                w_high(W_POOL + g + 2)
                for b, (o, w) in enumerate(BLOCKS):
                    if g and b == 0:
                        act.wait_ge(s_pw, g)
                    act.wait_ge(s_g, U_POOL + 3 * g + b + 1)
                    act.activation(px[:, 16 + o:16 + o + w], gb[:, b, 0:w], ACT.Copy).then_inc(s_gfree, 1)
                    if g == 0 and b == 1:
                        silu(QKV_TILES - 1)
                if g == 0:
                    by_tokens(QKV_TILES - 1)
                act.wait_ge(s_pw, g + 1)
                act.activation(p_hi[:, g, :], pool_out(g)[:, 16:], ACT.Copy).then_inc(s_phi, 1)
            act.wait_ge(s_g, U_WPOOL)
            w_high(W_WPOOL + 2)

            act.wait_ge(s_gsb, 1)
            act.activation(gtmp[:, 1, :], gflat(GCUM), ACT.Exp)
            act.activation(gtmp[:, 2, :], gtmp[:, 0, :], ACT.Exp)
            act.activation(gflat(EGT), mb[:, 360:360 + NCH * HEADS], ACT.Exp)
            act.wait_ge(s_ssq, QKV_TILES)
            act.activation(ssq[:, 0:2 * HEADS, :], ssq[:, 0:2 * HEADS, :], ACT.Sqrt, bias=eps_t).then_inc(s_exp, 1)

            for j in range(KT):
                if j >= 2:
                    act.wait_ge(s_yb[j % 2], 16 * (j // 2))
                for b, (o, w) in enumerate(OBLOCKS):
                    act.wait_ge(s_g, U_WPOOL + 3 * j + b + 1)
                    act.activation(ybs[:, j % 2, o:o + w], gb[:, b, 0:w], ACT.Copy,
                                   scale=gain(R_PSC + j, 1)).then_inc(s_gfree, 1)
                act.wait_ge(s_gfree, U_WPOOL + 3 * j + 3)
                act.dma_start(yb_d[j * P:(j + 1) * P, :], ybs[:, j % 2, :]).then_inc(s_yb[j % 2], 16)
            w_high(W_ZG + 2)

            def copy_halves(name, dst, c, turns=None):
                for h in range(2):
                    act.wait_ge(s_ps[name], 2 * (c if turns is None else turns) + h + 1)
                    act.activation(heads(dst, h), dbank(name, h), ACT.Copy).then_inc(s_ev[name], 1)

            def act_step(name, c):
                if name == "TQ":
                    copy_halves(name, qnt, c)
                elif name == "TKN":
                    copy_halves(name, knt, c)
                elif name == "TQD":
                    copy_halves(name, qdt, c)
                elif name == "TKG":
                    copy_halves(name, kgt, c)
                elif name == "GROW":
                    for h in range(2):
                        act.wait_ge(s_ev[name], 2 * c + h + 1)
                        act.activation(heads(ex, h), heads(ex, h), ACT.Exp).then_inc(s_dec, 1)
                elif name == "TT0":
                    copy_halves(name, rr, c - 1, turns=c)
                elif name in DOUBLING and name[0] == "T":
                    copy_halves(name, tt_m, c - 1)
                elif name == "V":
                    copy_halves(name, vv, c)
                elif name == "O":
                    for h in range(2):
                        act.wait_ge(s_ps[name], 2 * c + h + 1)
                        act.activation(heads(ots, h), dbank(name, h), ACT.Square).then_inc(s_osq, 1)
                        act.activation(heads(orx, h), dbank(name, h), ACT.Copy).then_inc(s_ev[name], 1)
                elif name == "SU":
                    act.wait_ge(s_oss, c + 1)
                    act.activation(orr, oss, ACT.Sqrt, bias=eps_t, scale=1.0 / P).then_inc(s_ort, 1)
                elif name == "OT":
                    copy_halves(name, ots, c)
                    act.wait_ge(s_ev[name], 2 * c + 2)
                    act.dma_start(ot_d[:, bass.ds(c * P, P)].rearrange("(h d) t -> d h t", d=P),
                                  ots[:, :, :]).then_inc(s_ot, 16)

            for name in PREP_STEPS:
                act_step(name, 0)
            for h in range(2):
                act.wait_ge(s_ps["TT0"], h + 1)
                act.activation(heads(rr, h), dbank("TT0", h), ACT.Copy).then_inc(s_ev[LAST_Y], 1)

            def gates(u, i):
                t, b = divmod(u, 3)
                o, w = OBLOCKS[b]
                if t == 0:
                    act.wait_ge(s_z, 3 * i + b + 1)
                    act.activation(zs[:, o:o + w], gb[:, b, 0:w], ACT.Sigmoid).then_inc(s_zsig, 1)
                else:
                    if t == 1:
                        act.wait_ge(s_yg, 16 * i + 16)
                    elif b == 0:
                        act.wait_ge(s_zg, i + 1)
                        act.dma_start(za_d[bass.ds(i * P, P), :], zs[:, :]).then_inc(s_za, 16)
                    act.wait_ge(s_g, U_ZG + 6 * i + 3 * (t - 1) + b + 1)
                    act.activation(gs[:, o:o + w], gb[:, b, 0:w], ACT.Sigmoid).then_inc(s_gfree, 1)
                if b == 2:
                    w_high(W_ZG + 3 + t, i)
                if u == 8:
                    act.wait_ge(s_gg, i + 1)
                    act.dma_start(yg_d[bass.ds(i * P, P), :], gs[:, :]).then_inc(s_yg, 16)

            with act.Fori(0, HEADS) as i:
                for name in STEPS:
                    act_step(name, i if name in REC else i + 1)
                    for u in units_after(name):
                        gates(u, i)
                act.wait_ge(s_ot, 16 * i + 16)
                act.wait_ge(s_za, 16 * i + 16)
            for name in REC:
                act_step(name, NCH - 1)

            for b, (o, w) in enumerate(OBLOCKS):
                act.wait_ge(s_y1, b + 1)
                act.activation(u_hi[:, :, o:o + w], yo[:, b % 2, :, :], ACT.Copy).then_inc(s_yhi, 1)

            for n in range(KT):
                for b, (o, w) in enumerate(OBLOCKS):
                    act.wait_ge(s_g, U_OUT + 3 * n + b + 1)
                    act.activation(ht[:, n, o:o + w], gb[:, b, 0:w], ACT.Copy).then_inc(s_gfree, 1)
                w_high(W_OUT + n + 3)

            def high2(j):
                n, c0 = (HALO, 0) if j == 0 else (P, HALO + (j - 1) * P)
                act.wait_ge(s_htmp, 2 * j + 2)
                act.activation(u_hi[:, :, c0:c0 + n], htmp[:, j % 2, :, 0:n], ACT.Copy).then_inc(s_u2hi, 1)

            for j in range(KT + 1):
                n = HALO if j == 0 else P
                act.wait_ge(s_h2, 2 * j + 2)
                if j >= 2:
                    act.wait_ge(s_hnt, 2 * (j - 1))
                root(j, n, h2m[:, :] if j == 0 else h2[:, j - 1, :], hx[0:n, j % 2, :], s_h2sq)
                if j >= 1:
                    high2(j - 1)
            high2(KT)

            def take(j, before, i=0):
                dst = xg if j % 2 == 0 else xv
                for b, (o, w) in enumerate(OBLOCKS):
                    act.wait_ge(s_g, before + b + 1 + 12 * i)
                    act.activation(dst[:, o:o + w], gb[:, b, 0:w], ACT.Copy).then_inc(s_gfree, 1)

            def gate(p):
                act.wait_ge(s_cg, p + 1)
                act.wait_ge(s_act, p)
                act.activation(sg[:, :], cg[:, :], ACT.Silu).then_inc(s_sg, 1)

            def high(p, q, turns):
                act.wait_ge(s_dn, 16 * turns)
                act.wait_ge(s_act, p + 1)
                act.activation(a_hi[:, q, :], cv[:, :], ACT.Copy).then_inc(s_ahi, 1)

            for q in range(2):
                if q:
                    act.wait_ge(s_cg, 1)
                take(0, U_UP0 + 6 * q)
                w_high(W_UP0 + 3 + 2 * q)
                if q:
                    act.wait_ge(s_cv, 1)
                take(1, U_UP0 + 3 + 6 * q)
                if q == 0:
                    w_high(W_UP0 + 4)
                gate(q)
                high(q, q, 0)
            with act.Fori(0, FFN_ITERS - 1) as i:
                act.wait_ge(s_g, U_FFN + 12 * i)
                w_high(W_FFN + 2, i, 6)
                act.wait_ge(s_cg, 2 * i + 2)
                take(0, U_FFN, i)
                w_high(W_FFN + 3, i, 6)
                act.wait_ge(s_cv, 2 * i + 2)
                take(1, U_FFN + 3, i)
                w_high(W_FFN + 4, i, 6)
                gate(2 * i + 2)
                high(2 * i + 2, 0, i + 1)
                w_high(W_FFN + 5, i, 6)
                w_high(W_FFN + 6, i, 6)
                act.wait_ge(s_cg, 2 * i + 3)
                take(0, U_FFN + 6, i)
                w_high(W_FFN + 7, i, 6)
                act.wait_ge(s_cv, 2 * i + 3)
                take(1, U_FFN + 9, i)
                gate(2 * i + 3)
                high(2 * i + 3, 1, i + 1)

            for t in range(KT):
                act.wait_ge(s_dnfree, 16 * (FFN_ITERS - 1) + 2 * t + 2)
                if t >= 2:
                    act.wait_ge(s_out[t % 2], 16 * (t // 2))
                root(t, P, h2[:, t, :], fino[:, t % 2, :], s_fsq)

        @block.vector
        def _(dve):
            def drain():
                dve.drain()

            def scale(j):
                n = META if j == 0 else P
                dve.wait_ge(s_nsq, j + 1)
                dve.reciprocal(nss[0:n, j:j + 1], nss[0:n, j:j + 1])
                drain()
                dve.tensor_scalar(xs[0:n, j % 2, :], xt[0:n, j % 3, :], nss[0:n, j:j + 1], None,
                                  ALU.mult).then_inc(s_xs, 1)

            scale(0)
            dve.wait_ge(s_prm, 3)
            for j in range(KT + 1):
                if j < KT:
                    scale(j + 1)
                n, c0 = (META, 0) if j == 0 else (P, META + (j - 1) * P)
                if j >= 2:
                    dve.wait_ge(s_uhi, j - 1)
                for h in range(2):
                    dve.wait_ge(s_nt, 2 * j + h + 1)
                    ps = db[:, 2 * (j % 2) + h, :].rearrange("p (k c) -> p k c", k=4)[:, :, 0:n]
                    dve.tensor_tensor(ntmp[:, j % 2, 4 * h:4 * h + 4, 0:n], ps,
                                      gain(R_NMIX + 4 * h, 4).unsqueeze(2).broadcast_to([P, 4, n]),
                                      ALU.mult).then_inc(s_ntmp, 1)
                dve.wait_ge(s_uhi, j + 1)
                dve.tensor_tensor(u_lo[:, :, c0:c0 + n], ntmp[:, j % 2, :, 0:n],
                                  u_hi[:, :, c0:c0 + n].bitcast(F32), ALU.subtract).then_inc(s_u, 1)

            dve.wait_ge(s_na, 1)
            dve.tensor_tensor(ab_g[:, PAD:], ab_g[:, PAD:], ab_t[:, PAD:], ALU.add)
            drain()
            dve.tensor_scalar(ab_g[:, PAD:], ab_g[:, PAD:], hdp[:, 2:3], -1.0, ALU.mult, ALU.mult).then_inc(s_ab, 1)

            taps = 4

            def conv(n, slot):
                dve.wait_ge(s_gfree, U_QKV + 3 * n + 3)
                dve.wait_ge(s_sl, n)

                def tap(j):
                    return prm[:, bass.ds(R_CONV + j * QKV_TILES + n, 1)]

                dve.tensor_scalar(cacc[:, :], xb[:, slot, 3:3 + T], tap(taps - 1), None, ALU.mult)
                for j in range(taps - 2, -1, -1):
                    drain()
                    t = dve.scalar_tensor_tensor(cacc[:, :], xb[:, slot, j:j + T], tap(j), cacc[:, :],
                                                 ALU.mult, ALU.add)
                t.then_inc(s_conv, 1)

            def sums(n):
                dve.wait_ge(s_sq, n + 1)
                dve.tensor_reduce(ssq[:, bass.ds(n, 1), :].rearrange("p o c -> p (o c)"), sq[:, :, :], AX_X,
                                  ALU.add).then_inc(s_ssq, 1)

            dve.wait_ge(s_zero, 3)
            conv(0, 0)
            with dve.Fori(0, QKV_TILES // 3 - 1) as i:
                for j in range(3):
                    conv(1 + 3 * i + j, (1 + j) % 3)
                    sums(3 * i + j)
            for n in (QKV_TILES - 2, QKV_TILES - 1):
                conv(n, n % 3)
                sums(n - 1)

            for g in range(4):
                if g:
                    dve.wait_ge(s_phi, g)
                dve.wait_ge(s_gfree, U_POOL + 3 * g + 3)
                src = px
                for k in range(g + 1):
                    dst = (pa, pb)[k % 2]
                    dve.tensor_tensor(dst[:, 16:], src[:, 16:], src[:, 16 - 2 ** k:16 + T - 2 ** k], ALU.add)
                    drain()
                    src = dst
                dst = pool_out(g)
                dve.tensor_scalar(dst[:, 16:], src[:, 16:], 1.0 / WINDOWS[g], None, ALU.mult)
                drain()
                dve.tensor_tensor(dst[:, 16:32], dst[:, 16:32], cst[:, C_INV + 16 * g:C_INV + 16 * g + 16], ALU.mult)
                drain()
                dve.tensor_tensor(dst[:, 16:], dst[:, 16:], px[:, 16:], ALU.subtract).then_inc(s_pw, 1)
                dve.wait_ge(s_phi, g + 1)
                dve.tensor_tensor(p_lo[:, g, :], dst[:, 16:], p_hi[:, g, :].bitcast(F32),
                                  ALU.subtract).then_inc(s_plo, 1)
                drain()
                if g == 0:
                    sums(QKV_TILES - 1)

            def by_chunk(m):
                return mb[:, m * NCH * 16:(m + 1) * NCH * 16].rearrange("p (c k) -> p c k", k=16)

            dve.wait_ge(s_abT, 1)
            dve.tensor_copy(fac[:, FV, :, :], by_chunk(0)[:, :, 0:8])
            dve.tensor_copy(gtok[:, :].rearrange("p (c h) -> p c h", h=HEADS), by_chunk(1)[:, :, 8:16]).then_inc(s_gtok, 1)
            dve.wait_ge(s_gcum, 1)
            dve.tensor_copy(gflat(GCUM), mb[:, 288:288 + NCH * HEADS])
            drain()
            dve.tensor_tensor(gtmp[:, 0, :], mb[:, 360:360 + NCH * HEADS], gflat(GCUM), ALU.subtract).then_inc(s_gsb, 1)
            dve.wait_ge(s_exp, 1)
            dve.reciprocal(ssq[:, 0:2 * HEADS, :], ssq[:, 0:2 * HEADS, :])
            drain()
            rq = ssq[:, 0:HEADS, :].rearrange("p h c -> p c h")
            rk = ssq[:, HEADS:2 * HEADS, :].rearrange("p h c -> p c h")
            eg = gtmp[:, 1, :].rearrange("p (c h) -> p c h", h=HEADS)
            el = gtmp[:, 2, :].rearrange("p (c h) -> p c h", h=HEADS)
            dve.tensor_scalar(fac[:, FQ], rq, float(P) ** -0.5, None, ALU.mult)
            dve.tensor_copy(fac[:, FK], rk)
            dve.tensor_tensor(fac[:, FKD], rk, el, ALU.mult)
            dve.tensor_tensor(fac[:, FKB], rk, fac[:, FV], ALU.mult)
            drain()
            dve.tensor_tensor(fac[:, FQD], fac[:, FQ], eg, ALU.mult)
            dve.tensor_tensor(fac[:, FKG], fac[:, FKB], eg, ALU.mult).then_inc(s_fac, 1)
            drain()

            def scaled(f, n, src, kind, c):
                dve.tensor_tensor(form[:, n], tk[:, src * HEADS:(src + 1) * HEADS, :], per_head(factor(kind, c)),
                                  ALU.mult).then_inc(s_form[f], 1)

            def halves(name, turns, op, out_sem):
                for h in range(2):
                    dve.wait_ge(s_ps[name], 2 * turns + h + 1)
                    op(h).then_inc(out_sem, 1)

            def dve_step(name, c):
                if name == "TKN":
                    dve.wait_ge(s_ps[name], 2 * c + 2)
                elif name == "TKB":
                    halves(name, c, lambda h: dve.tensor_copy(heads(kbt, h), dbank(name, h)), s_ev[name])
                elif name == "GROW":
                    dve.wait_ge(s_nm, c + 1)
                    halves(name, c, lambda h: dve.tensor_tensor(heads(ex, h), dbank(name, h), heads(nmx, h),
                                                                ALU.subtract), s_ev[name])
                elif name == "KK":
                    for h in range(2):
                        dve.wait_ge(s_dec, 2 * c + h + 1)
                        dve.wait_ge(s_ps[name], 2 * c + h + 1)
                        dve.tensor_tensor(heads(at_m, h), dbank(name, h), heads(ex, h), ALU.mult).then_inc(s_ev[name], 1)
                    scaled("qn", 0, 0, FQ, c)
                    scaled("kg", 1, 1, FKG, c)
                elif name == "TQ":
                    dve.wait_ge(s_ps[name], 2 * c + 2)
                    scaled("qd", 0, 0, FQD, c)
                elif name == "QK":
                    halves(name, c, lambda h: dve.tensor_tensor(heads(qkm, h), dbank(name, h), heads(ex, h),
                                                                ALU.mult), s_ev[name])
                elif name[0] == "X":
                    halves(name, c - 1, lambda h: dve.tensor_tensor(
                        heads(nmx, h), dbank(name, h), over_heads(lvl(int(name[1])), HEADS // 2), ALU.mult), s_ev[name])
                elif name[0] == "Y":
                    halves(name, c - 1, lambda h: dve.tensor_tensor(heads(rr, h), heads(rr, h), dbank(name, h),
                                                                    ALU.subtract), s_ev[name])
                elif name == "P1":
                    dve.wait_ge(s_vb, c + 1)
                    halves(name, c, lambda h: dve.tensor_tensor(heads(orx, h), heads(vb, h), dbank(name, h),
                                                                ALU.subtract), s_ev[name])
                elif name == "O":
                    dve.wait_ge(s_ps[name], 2 * c + 2)
                    dve.tensor_tensor(st[:, :, :], st[:, :, :], per_head(factor(EGT, c)), ALU.mult)
                    dve.wait_ge(s_osq, 2 * c + 2)
                    dve.tensor_reduce(oss, ots[:, :, :], AX_X, ALU.add).then_inc(s_oss, 1)
                elif name == "SU":
                    drain()
                    halves(name, c, lambda h: dve.tensor_tensor(heads(st, h), heads(st, h), dbank(name, h),
                                                                ALU.add), s_ev[name])
                elif name == "TQD":
                    output_scale(c - 1)

            def output_scale(c):
                dve.wait_ge(s_ort, c + 1)
                dve.reciprocal(orr, orr)
                drain()
                dve.wait_ge(s_ev["O"], 2 * c + 2)
                dve.tensor_tensor(orx[:, :, :], orx[:, :, :], per_head(orr), ALU.mult).then_inc(s_on, 1)

            def forms_first(c):
                dve.tensor_copy(gcur, factor(GCUM, c)).then_inc(s_gcp, 1)
                dve.wait_ge(s_tk, 16 * c + 16)
                scaled("kn", 0, 1, FK, c)
                scaled("kb", 1, 1, FKB, c)

            forms_first(0)
            for name in PREP_STEPS:
                if name != "TQD":
                    dve_step(name, 0)

            def gated(u, i):
                t, b = divmod(u, 3)
                o, w = OBLOCKS[b]
                if t == 0:
                    dve.wait_ge(s_zsig, 3 * i + b + 1)
                    dve.scalar_tensor_tensor(zs[:, o:o + w], zs[:, o:o + w], gain(R_HN, 1), gb[:, b, 0:w],
                                             ALU.mult, ALU.mult).then_inc(s_zfree, 1)
                elif u == 5:
                    dve.wait_ge(s_gfree, U_ZG + 6 * i + 3)
                    dve.tensor_tensor(zs[:, :], zs[:, :], gs[:, :], ALU.mult).then_inc(s_zg, 1)
                elif u == 8:
                    dve.wait_ge(s_gfree, U_ZG + 6 * i + 6)
                    dve.wait_ge(s_yl, 16 * i + 16)
                    dve.tensor_tensor(gs[:, :], gs[:, :], yl[:, :], ALU.mult).then_inc(s_gg, 1)

            dve.wait_ge(s_ev["SU"], 2)
            with dve.Fori(0, HEADS) as i:
                dve_step("P1", i)
                forms_first(i + 1)
                for name in STEPS[1:]:
                    dve_step(name, i if name in REC else i + 1)
                    for u in units_after(name):
                        gated(u, i)
            dve_step("P1", NCH - 1)
            dve.wait_ge(s_osq, 2 * NCH)
            dve.tensor_reduce(oss, ots[:, :, :], AX_X, ALU.add).then_inc(s_oss, 1)
            output_scale(NCH - 1)

            for b, (o, w) in enumerate(OBLOCKS):
                dve.wait_ge(s_yin[b % 2], 48 * (b // 2 + 1))
                s = b % 2
                dve.tensor_tensor(yo[:, s], yo[:, s], yz[:, s], ALU.mult)
                drain()
                dve.tensor_tensor(yo[:, s], yo[:, s], yg[:, s], ALU.add).then_inc(s_y1, 1)
                dve.wait_ge(s_yhi, b + 1)
                dve.tensor_tensor(u_lo[:, :, o:o + w], yo[:, s], u_hi[:, :, o:o + w].bitcast(F32),
                                  ALU.subtract).then_inc(s_y, 1)

            dve.wait_ge(s_h2x, 32)

            def residual(j):
                n = HALO if j == 0 else P
                for h in range(2):
                    dst = h2m[:, h * 512:(h + 1) * 512] if j == 0 else h2[:, j - 1, h * 512:(h + 1) * 512]
                    dve.wait_ge(s_h2T, 2 * j + h + 1)
                    dve.tensor_tensor(dst, dst, db[0:n, h, :], ALU.add).then_inc(s_h2, 1)

            def scale2(j):
                n = HALO if j == 0 else P
                dve.wait_ge(s_h2sq, j + 1)
                dve.reciprocal(nss[0:n, j:j + 1], nss[0:n, j:j + 1])
                drain()
                dve.tensor_scalar(hx[0:n, j % 2, :], h2m[:, :] if j == 0 else h2[:, j - 1, :], nss[0:n, j:j + 1], None,
                                  ALU.mult).then_inc(s_hx, 1)

            residual(0)
            for j in range(KT + 1):
                if j < KT:
                    residual(j + 1)
                scale2(j)
                n, c0 = (HALO, 0) if j == 0 else (P, HALO + (j - 1) * P)
                if j >= 2:
                    dve.wait_ge(s_u2hi, j - 1)
                for h in range(2):
                    dve.wait_ge(s_hnt, 2 * j + h + 1)
                    ps = db[:, 2 + h, :].rearrange("p (k c) -> p k c", k=4)[:, :, 0:n]
                    dve.tensor_tensor(htmp[:, j % 2, 4 * h:4 * h + 4, 0:n], ps,
                                      gain(R_NFFN + 4 * h, 4).unsqueeze(2).broadcast_to([P, 4, n]),
                                      ALU.mult).then_inc(s_htmp, 1)
                dve.wait_ge(s_u2hi, j + 1)
                dve.tensor_tensor(u_lo[:, :, c0:c0 + n], htmp[:, j % 2, :, 0:n],
                                  u_hi[:, :, c0:c0 + n].bitcast(F32), ALU.subtract).then_inc(s_u2, 1)

            def conv3(dst, src, f, done):
                def tap(j):
                    return prm[:, bass.ds(R_CF + j * 2 * FT + f, 1)]
                dve.tensor_scalar(dst[:, :], src[:, 2:2 + SEQ], tap(2), None, ALU.mult)
                drain()
                dve.scalar_tensor_tensor(dst[:, :], src[:, 1:1 + SEQ], tap(1), dst[:, :], ALU.mult, ALU.add)
                drain()
                dve.scalar_tensor_tensor(dst[:, :], src[:, 0:SEQ], tap(0), dst[:, :], ALU.mult,
                                         ALU.add).then_inc(done, 1)

            def hidden(p, taken):
                dve.wait_ge(s_gfree, taken)
                dve.wait_ge(s_sg, p)
                conv3(cg, xg, p, s_cg)
                dve.wait_ge(s_gfree, taken + 3)
                conv3(cv, xv, FT + p, s_cv)
                drain()
                dve.wait_ge(s_sg, p + 1)
                dve.tensor_tensor(cv[:, :], cv[:, :], sg[:, :], ALU.mult).then_inc(s_act, 1)

            def low(p, q):
                dve.wait_ge(s_ahi, p + 1)
                dve.tensor_tensor(a_lo[:, q, :], cv[:, :], a_hi[:, q, :].bitcast(F32), ALU.subtract).then_inc(s_alo, 1)

            def add_down(i):
                for u in range(2 * KT):
                    t, half = divmod(u, 2)
                    dve.wait_ge(s_dn, 16 * i + u + 1)
                    dst = h2[:, t, half * 512:(half + 1) * 512]
                    dve.tensor_tensor(dst, dst, db[:, u % 4, :], ALU.add).then_inc(s_dnfree, 1)

            for q in range(2):
                hidden(q, U_UP0 + 3 + 6 * q)
                low(q, q)
            with dve.Fori(0, FFN_ITERS - 1) as i:
                hidden(2 * i + 2, U_FFN + 3 + 12 * i)
                add_down(i)
                low(2 * i + 2, 0)
                hidden(2 * i + 3, U_FFN + 9 + 12 * i)
                low(2 * i + 3, 1)
            add_down(FFN_ITERS - 1)
            dve.wait_ge(s_fg, 16)
            for t in range(KT):
                dve.wait_ge(s_fsq, t + 1)
                dve.reciprocal(nss[:, t:t + 1], nss[:, t:t + 1])
                drain()
                dve.scalar_tensor_tensor(fino[:, t % 2, :], h2[:, t, :], nss[:, t:t + 1], fing[:, :],
                                         ALU.mult, ALU.mult).then_inc(s_fin, 1)


def kernel(**inputs):
    import concourse.bacc as bacc
    from concourse.bass_utils import run_bass_kernel_spmd

    names = ["x", "meta_tokens", "norm_mix", "w_in", "conv_qkv", "a_log", "dt_bias", "head_norm", "w_pool",
             "pool_scale", "w_out", "norm_ffn", "w_up", "conv_ffn", "w_down", "norm_final"]
    nc = bacc.Bacc("TRN2", target_bir_lowering=False, num_devices=1)
    arrays = {f"in_{n}": np.ascontiguousarray(inputs[n]) for n in names}
    arrays["in_constants"] = constants()
    args = [nc.dram_tensor(n, a.shape, mybir.dt.from_np(a.dtype), kind="ExternalInput").ap()
            for n, a in arrays.items()]
    args.append(nc.dram_tensor("out_h", (1, SEQ, D), F32, kind="ExternalOutput").ap())
    hybrid_block(nc, *args)
    r = run_bass_kernel_spmd(nc, [arrays], core_ids=[0])
    return r.results[0]["out_h"]
```

```python
from contextlib import ExitStack

import numpy as np

import concourse.bass as bass
from concourse import mybir

F32 = mybir.dt.float32
F32R = mybir.dt.float32r
ACT = mybir.ActivationFunctionType
ALU = mybir.AluOpType
AX_X = mybir.AxisListType.X

P = 128
D = 1024
SEQ = 1024
META = 16
KT = D // P
T = META + SEQ
HEADS = 8
CH = 128
NCH = -(-T // CH)
PAD = NCH * CH - T
TP = NCH * CH
HALO = 2
TO = SEQ + HALO
OFF = META - HALO
QKV_TILES = 3 * HEADS
DFF = 2816
FT = DFF // P
EPS = 1e-6
NEG = -1e30
WINDOWS = (2, 4, 8, 16)
Z_COL = QKV_TILES * P
AB_COL = Z_COL + D
POOL_COL = AB_COL + 2 * HEADS
GA_COL = POOL_COL + 4 * P
GB_COL = GA_COL + D
IN_DIM = GB_COL + D

BLOCKS = [(0, 346), (346, 346), (692, T - 692)]
OBLOCKS = [(i * (TO // 3), TO // 3) for i in range(3)]

SUB = 16
BLKS = CH // SUB
LEVELS = [16, 32, 64]

C_ID, C_CUM, C_NEG = 0, P, 2 * P
C_LV = 3 * P
C_INV = C_LV + len(LEVELS) * P
C_ALL = C_INV + 4 * 16

W_AB = 0
W_QKV = 1
W_POOL = W_QKV + QKV_TILES
W_WPOOL = W_POOL + 4
W_ZG = W_WPOOL + 1
W_OUT = W_ZG + 3 * HEADS
W_UP0 = W_OUT + KT
W_FFN = W_UP0 + 4
FFN_ITERS = FT // 2
W_LAST = W_FFN + 6 * (FFN_ITERS - 1)
W_ALL = W_LAST + 2
SLOTS = 3

U_QKV = 3
U_POOL = U_QKV + 3 * QKV_TILES
U_WPOOL = U_POOL + 12
U_ZG = U_WPOOL + 24
U_OUT = U_ZG + 6 * HEADS
U_UP0 = U_OUT + 24
U_FFN = U_UP0 + 12

FQ, FQD, FK, FKB, FKG, FKD, FV, EGT, GCUM = range(9)

R_CONV, R_PSC, R_HN, R_CF = 0, 96, 104, 105


def constants():
    c = np.zeros((P, C_ALL), np.float32)
    r = np.arange(P)
    c[:, C_ID:C_ID + P] = np.eye(P)
    c[:, C_CUM:C_CUM + P] = r[:, None] <= r[None, :]
    c[:, C_NEG:C_NEG + P] = np.where(r[:, None] > r[None, :], -NEG, 0.0)

    def level(z):
        return ((r[:, None] // z % 2 == 1) & (r[None, :] // z == r[:, None] // z - 1)).astype(np.float32)

    for n, z in enumerate(LEVELS):
        c[:, C_LV + n * P:C_LV + (n + 1) * P] = level(z)
    for g, w in enumerate(WINDOWS):
        c[:, C_INV + g * 16:C_INV + g * 16 + w] = np.float32(w) / np.arange(1, w + 1, dtype=np.float32)
        c[:, C_INV + g * 16 + w:C_INV + (g + 1) * 16] = 1.0
    return c


REC = ["P1", "V", "O", "SU", "OT"]
STEPS = ["P1", "TKN", "V", "TKB", "GROW", "KK", "TQ", "TKG", "O", "SU", "QK", "TQD", "OT", "TT0"]
DOUBLING = ["TT0"]
for _n in range(len(LEVELS)):
    DOUBLING += [f"X{_n}", f"Y{_n}"] + ([f"T{_n}"] if _n < len(LEVELS) - 1 else [])
STEPS += DOUBLING[1:]
LAST_Y = DOUBLING[-1]
PREP_STEPS = [s for s in STEPS if s not in REC and s not in DOUBLING]
FORM = {"TKN": ("kn", 0), "TKB": ("kb", 1), "TQ": ("qn", 0), "TKG": ("kg", 1), "TQD": ("qd", 0)}
PIECES = [(0, 3), (3, 6), (6, 8)]
FILLS = {"P1": 1, "TKN": 1, "V": 1, "TKB": 1, "GROW": 1, "KK": 1, "TQ": 2, "TKG": 2, "O": 3, "SU": 2, "QK": 2,
         "TQD": 1, "OT": 2, "TT0": 1, "X0": 1, "Y0": 1, "T0": 1, "X1": 0, "Y1": 1, "T1": 1, "X2": 0, "Y2": 1}
assert sum(FILLS.values()) == 9 * len(PIECES)


OUT_PLAN = [("unit", n, b) for b in range(3) for n in range(3)]
OUT_PLAN += [("unit", n, b) for n in (3, 4) for b in range(3)]
OUT_PLAN += [("unit", n, 0) for n in (5, 6, 7)]
OUT_PLAN += [("unit", 5, 1), ("back", 0), ("unit", 6, 1), ("forth", 0), ("back", 1)]
for _j, _unit in enumerate([("unit", 7, 1), ("unit", 5, 2), ("unit", 6, 2), ("unit", 7, 2), ("up", 0, 0),
                            ("up", 1, 0), ("up", 0, 1)]):
    OUT_PLAN += [_unit, ("forth", _j + 1), ("back", _j + 2)]
OUT_PLAN += [("up", 1, 1), ("forth", KT), ("up", 0, 2), ("up", 1, 2)]
OUT_UNITS = [s[1:] for s in OUT_PLAN if s[0] == "unit"]
assert sorted(OUT_UNITS) == [(n, b) for n in range(KT) for b in range(3)]
BACK_UNITS = [18, 18, 18, 21, 21, 21, 24, 24, 24]
for _j in range(KT + 1):
    _cols = HALO if _j == 0 else HALO + _j * P
    assert BACK_UNITS[_j] > max(OUT_UNITS.index((n, b)) for n in range(KT) for b in range(3)
                                if OBLOCKS[b][0] < _cols)


NORMED = [-(-(o + w - HALO) // P) + 1 for o, w in OBLOCKS]


def pieces_after(name):
    first = sum(FILLS[s] for s in STEPS[:STEPS.index(name)])
    return range(first, first + FILLS[name])


def units_after(name):
    return [p // len(PIECES) for p in pieces_after(name) if p % len(PIECES) == len(PIECES) - 1]


def hybrid_block(nc, x, meta_tokens, norm_mix, w_in, conv_qkv, a_log, dt_bias, head_norm, w_pool,
                 pool_scale, w_out, norm_ffn, w_up, conv_ffn, w_down, norm_final, consts, out):
    with ExitStack() as ctx:
        def sem(name):
            return ctx.enter_context(nc.semaphore(name))

        base = -(-nc.sbuf_base // 64) * 64
        room = nc.sbuf_usable_end - base
        top = [0]

        def at(name, shape, dt, offset=None):
            size = 4 * int(np.prod(shape[1:]))
            size += -size % 32
            if offset is None:
                offset = top[0]
                top[0] += size
            assert offset + size <= room, (name, offset + size, room)
            return nc.alloc_sbuf_tensor_at(name, shape, dt, offset=base + offset)

        u_hi = at("u_hi", [P, KT, T], F32R)
        u_lo = at("u_lo", [P, KT, T], F32R)
        w_raw = at("w_raw", [P, SLOTS, D], F32)
        w_hi = at("w_hi", [P, SLOTS, D], F32R)
        w_lo = at("w_lo", [P, SLOTS, D], F32R)
        cst = at("cst", [P, C_ALL], F32)
        prm = at("prm", [P, R_CF + 3 * 2 * FT], F32)
        fac = at("fac", [P, 9, NCH, HEADS], F32)
        ssq = at("ssq", [P, QKV_TILES, NCH], F32)
        tiny = at("tiny", [P, 64], F32)
        eps_t = tiny[:, 0:1]
        nss = tiny[:, 8:24]
        oss = tiny[:, 24:32]
        orr = tiny[:, 32:40]
        hdp = tiny[0:16, 40:44]
        gcur = tiny[:, 48:56]
        region = top[0]
        end = [region]

        def plan(items, start=region):
            made, offset = [], start
            for name, shape, dt in items:
                size = 4 * int(np.prod(shape[1:]))
                made.append(at(name, shape, dt, offset))
                offset += size + (-size % 32)
            end[0] = offset
            return made

        xt, xs, gmix, prow = plan([
            ("xt", [P, 3, D], F32), ("xs", [P, 2, D], F32), ("gmix", [P, D], F32), ("prow", [P, 3, P], F32)])
        xb, cacc, sl, tm, sq = plan([
            ("xb", [P, 3, 3 + T + 1], F32), ("cacc", [P, T], F32), ("sl", [P, TP], F32),
            ("tm", [P, NCH, P], F32), ("sq", [P, NCH, P], F32)])
        px, pa, pb, p_hi, p_lo, ab_beta, ab_g, ab_t, gtok, gtmp = plan([
            ("px", [P, 16 + T], F32), ("pa", [P, 16 + T], F32), ("pb", [P, 16 + T], F32),
            ("p_hi", [P, 4, T], F32R), ("p_lo", [P, 4, T], F32R),
            ("ab_beta", [16, TP], F32), ("ab_g", [16, TP], F32), ("ab_t", [16, TP], F32),
            ("gtok", [P, NCH * HEADS], F32), ("gtmp", [P, 3, NCH * HEADS], F32)],
            end[0])
        (ybs,) = plan([("ybs", [P, 2, TO], F32)])
        names = ["knt", "qnt", "kbt", "nmx", "ex", "at_m", "bd"]
        live = ["qdt", "kgt", "kd", "vb", "qkm", "rr", "vv", "st", "ots"]
        (tk, form, knt, qnt, kbt, nmx, ex, at_m, bd, zs, gs, yl, blk, sol, upd, qdt, kgt, kd, vb, qkm, rr, vv,
         st, ots) = plan(
            [("tk", [P, QKV_TILES, P], F32), ("form", [P, 2, HEADS, P], F32)]
            + [(n, [P, HEADS, P], F32) for n in names]
            + [("zs", [P, TO], F32), ("gs", [P, TO], F32), ("yl", [P, TO], F32),
               ("blk", [BLKS * HEADS, SUB * SUB], F32), ("sol", [BLKS * HEADS, SUB * SUB], F32),
               ("upd", [BLKS * HEADS, SUB * SUB // 4], F32)]
            + [(n, [P, HEADS, P], F32) for n in live])
        orx = vb
        tt_m = kbt
        bw = OBLOCKS[0][1]
        yz0, yg0, yo0, yz1, yg1, yo1, ht = plan(
            [(n, [P, KT, bw], F32) for n in ("yz0", "yg0", "yo0", "yz1", "yg1", "yo1")]
            + [("ht", [P, KT, TO], F32)])
        yz, yg, yo = (yz0, yz1), (yg0, yg1), (yo0, yo1)
        h2, h2m = plan([("h2", [P, KT, D], F32), ("h2m", [HALO, D], F32)])
        after_h2 = end[0]
        xg, xv, cg, cv, sg = plan([
            ("xg", [P, TO], F32), ("xv", [P, TO], F32), ("cg", [P, SEQ], F32), ("cv", [P, SEQ], F32),
            ("sg", [P, SEQ], F32)], after_h2)
        gffn = sg
        mlp_end = end[0]
        (hx,) = plan([("hx", [P, 2, D], F32)], mlp_end)
        a_hi, a_lo, fing, fino = plan([
            ("a_hi", [P, 2, SEQ], F32R), ("a_lo", [P, 2, SEQ], F32R), ("fing", [P, D], F32),
            ("fino", [P, 2, D], F32)], mlp_end)

        gb = ctx.enter_context(nc.psum_tensor("gb", [P, 3, 512], F32))
        db = ctx.enter_context(nc.psum_tensor("db", [P, 4, 512], F32))
        mb = ctx.enter_context(nc.psum_tensor("mb", [P, 512], F32))

        qkv_d = nc.dram_tensor("qkv_d", [NCH * P, QKV_TILES * P], F32, kind="Internal").ap()
        yb_d = nc.dram_tensor("yb_d", [D, TO], F32, kind="Internal").ap()
        za_d = nc.dram_tensor("za_d", [D, TO], F32, kind="Internal").ap()
        yg_d = nc.dram_tensor("yg_d", [D, TO], F32, kind="Internal").ap()
        blk_d = nc.dram_tensor("blk_d", [BLKS * HEADS, SUB * SUB], F32, kind="Internal").ap()
        sol_d = nc.dram_tensor("sol_d", [BLKS * HEADS, SUB * SUB], F32, kind="Internal").ap()
        ot_d = nc.dram_tensor("ot_d", [D, PAD + T], F32, kind="Internal").ap()

        ident = cst[:, C_ID:C_ID + P]

        def lvl(n):
            return cst[:, C_LV + n * P:C_LV + (n + 1) * P]

        def over_heads(m, n=HEADS):
            return m.unsqueeze(1).broadcast_to([P, n, P])

        def per_head(f, n=HEADS):
            return f.unsqueeze(2).broadcast_to([P, n, P])

        def factor(kind, c):
            return fac[:, kind, bass.ds(c, 1), :].rearrange("p o h -> p (o h)")

        s_const = sem("s_const")
        s_zero = sem("s_zero")
        s_prow = sem("s_prow")
        s_hd = sem("s_hd")
        s_prmT = sem("s_prmT")
        s_prm = sem("s_prm")
        s_x = [sem(f"s_x{i}") for i in range(3)]
        s_nsq = sem("s_nsq")
        s_xs = sem("s_xs")
        s_nt = sem("s_nt")
        s_gmix = sem("s_gmix")
        s_uhi = sem("s_uhi")
        s_u = sem("s_u")
        s_w = [sem(f"s_w{i}") for i in range(SLOTS)]
        s_whi = sem("s_whi")
        s_wlo = sem("s_wlo")
        s_g = sem("s_g")
        s_gfree = sem("s_gfree")
        s_z = sem("s_z")
        s_zsig = sem("s_zsig")
        s_zfree = sem("s_zfree")
        s_na = sem("s_na")
        s_ab = sem("s_ab")
        s_abT = sem("s_abT")
        s_gtok = sem("s_gtok")
        s_gcum = sem("s_gcum")
        s_gsb = sem("s_gsb")
        s_exp = sem("s_exp")
        s_conv = sem("s_conv")
        s_sl = sem("s_sl")
        s_tmps = sem("s_tmps")
        s_tm = sem("s_tm")
        s_sq = sem("s_sq")
        s_ssq = sem("s_ssq")
        s_spill = sem("s_spill")
        s_fac = sem("s_fac")
        s_pw = sem("s_pw")
        s_phi = sem("s_phi")
        s_plo = sem("s_plo")
        s_yb = [sem(f"s_yb{i}") for i in range(2)]
        s_tk = sem("s_tk")
        s_form = {f: sem(f"s_form_{f}") for f in ("qn", "kn", "kb", "qd", "kg")}
        s_kd = sem("s_kd")
        s_vb = sem("s_vb")
        s_nm = sem("s_nm")
        s_gcp = sem("s_gcp")
        s_dec = sem("s_dec")
        s_ps = {n: sem(f"s_ps_{n}") for n in STEPS}
        s_ev = {n: sem(f"s_ev_{n}") for n in STEPS}
        s_bst = sem("s_bst")
        s_blk = sem("s_blk")
        s_sol = sem("s_sol")
        s_sst = sem("s_sst")
        s_bd = sem("s_bd")
        s_osq = sem("s_osq")
        s_oss = sem("s_oss")
        s_ort = sem("s_ort")
        s_on = sem("s_on")
        s_ot = sem("s_ot")
        s_za = sem("s_za")
        s_yg = sem("s_yg")
        s_yl = sem("s_yl")
        s_zg = sem("s_zg")
        s_gg = sem("s_gg")
        s_yin = [sem(f"s_yin{i}") for i in range(2)]
        s_y1 = sem("s_y1")
        s_yhi = sem("s_yhi")
        s_y = sem("s_y")
        s_h2x = [sem(f"s_h2x{i}") for i in range(3)]
        s_h2T = sem("s_h2T")
        s_h2 = sem("s_h2")
        s_h2sq = sem("s_h2sq")
        s_hx = sem("s_hx")
        s_hnt = sem("s_hnt")
        s_gffn = sem("s_gffn")
        s_u2hi = sem("s_u2hi")
        s_u2 = sem("s_u2")
        s_cg = sem("s_cg")
        s_cv = sem("s_cv")
        s_sg = sem("s_sg")
        s_act = sem("s_act")
        s_ahi = sem("s_ahi")
        s_alo = sem("s_alo")
        s_dn = sem("s_dn")
        s_dnfree = sem("s_dnfree")
        s_fg = sem("s_fg")
        s_fsq = sem("s_fsq")
        s_fin = sem("s_fin")
        s_out = [sem(f"s_out{i}") for i in range(2)]

        def gain(row, n=KT):
            return prm[:, row:row + n]

        def gflat(kind):
            return fac[:, kind, :, :].rearrange("p c h -> p (c h)")

        def pool_out(g):
            return (pb, pa)[g % 2]

        def heads(m, h):
            return m[:, h * HEADS // 2:(h + 1) * HEADS // 2, :]

        def dbank(name, h):
            return db[:, 2 * (STEPS.index(name) % 2) + h, :].rearrange("p (m c) -> p m c", m=HEADS // 2)

        def tbank(b, n):
            return db[:, b, :].rearrange("p (k c) -> p k c", k=4)[:, :, 0:n]

        block = ctx.enter_context(nc.Block())

        @block.sync
        def _(sp):
            def load_w(n, src, i=0, per=3, wide=False):
                if n >= SLOTS:
                    sp.wait_ge(s_wlo, n - SLOTS + 1 + per * i)
                dst = w_raw[:, n % SLOTS, :]
                if not wide:
                    dst = dst.rearrange("p (k c) -> p k c", k=KT)
                sp.dma_start(dst, src).then_inc(s_w[n % SLOTS], 16)

            def cols(w, c0):
                return w[0, :, bass.ds(c0, P)].rearrange("(k p) c -> p k c", p=P)

            sp.dma_start(xt[0:META, 0, :], meta_tokens).then_inc(s_x[0], 16)
            sp.dma_start(cst[:, :], consts).then_inc(s_const, 16)
            sp.dma_start(gmix[:, :], norm_mix.broadcast_to([P, D])).then_inc(s_gmix, 16)
            for j in range(1, 3):
                sp.dma_start(xt[:, j, :], x[0, (j - 1) * P:j * P, :]).then_inc(s_x[j], 16)
            load_w(W_AB, cols(w_in, AB_COL))
            for j in range(3, KT + 1):
                sp.wait_ge(s_xs, j - 2)
                sp.dma_start(xt[:, j % 3, :], x[0, (j - 1) * P:j * P, :]).then_inc(s_x[j % 3], 16)
            for j in range(2):
                load_w(W_QKV + j, cols(w_in, j * P))
            with sp.Fori(0, QKV_TILES // 3 - 1) as i:
                for j in range(3):
                    load_w(W_QKV + 2 + j, cols(w_in, (2 + j) * P + 3 * P * i), i)
            load_w(W_QKV + QKV_TILES - 1, cols(w_in, (QKV_TILES - 1) * P))
            for g in range(4):
                load_w(W_POOL + g, cols(w_in, POOL_COL + g * P))
            sp.wait_ge(s_wlo, W_WPOOL - SLOTS + 1)
            sp.dma_start(w_raw[:, W_WPOOL % SLOTS, :].rearrange("p (g d) -> p g d", g=4),
                         w_pool[0].rearrange("g p d -> p g d")).then_inc(s_w[W_WPOOL % SLOTS], 16)

            def load_tk(c):
                sp.dma_start(tk[:, :, :].rearrange("p t d -> p (t d)"),
                             qkv_d[bass.ds(c * P, P), :]).then_inc(s_tk, 16)

            def invert(c, n=BLKS):
                def block(b, m):
                    return m[SUB * b:SUB * (b + 1), :, SUB * b:SUB * (b + 1)]

                def rows(m, b):
                    return m[HEADS * b:HEADS * (b + 1), :].rearrange("h (r c) -> r h c", r=SUB)

                stored = 16 * c * BLKS if n < BLKS else 16 + 16 * BLKS * (c - 1)
                sp.wait_ge(s_ev["KK"], 2 * c + 2)
                for b in range(n):
                    sp.dma_start(rows(blk_d, b), block(BLKS - n + b, at_m)).then_inc(s_bst, 16)
                sp.wait_ge(s_bst, stored + 16 * n)
                sp.dma_start(blk[0:HEADS * n, :], blk_d[0:HEADS * n, :]).then_inc(s_blk, 16)
                sp.wait_ge(s_sol, c + 1)
                sp.dma_start(sol_d[0:HEADS * n, :], sol[0:HEADS * n, :]).then_inc(s_sst, 16)
                sp.wait_ge(s_sst, 16 * c + 16)
                if n < BLKS:
                    sp.wait_ge(s_zero, 4)
                for b in range(n):
                    sp.dma_start(block(BLKS - n + b, bd), rows(sol_d, b)).then_inc(s_bd, 16)

            for j, c0 in enumerate((Z_COL, GA_COL, GB_COL)):
                load_w(W_ZG + j, cols(w_in, c0))
            sp.wait_ge(s_spill, 16 * QKV_TILES)
            sp.wait_ge(s_gfree, U_ZG)
            sp.wait_ge(s_yb[0], 16 * 4)
            sp.wait_ge(s_yb[1], 16 * 4)
            sp.wait_ge(s_fac, 1)
            load_tk(0)
            sp.dma_start(yl[:, :], yb_d[0:P, :]).then_inc(s_yl, 16)
            invert(0, 1)
            sp.wait_ge(s_form["qd"], 1)
            sp.wait_ge(s_vb, 1)
            load_tk(1)
            with sp.Fori(0, HEADS - 1) as i:
                for j, c0 in enumerate((Z_COL, GA_COL, GB_COL)):
                    load_w(W_ZG + 3 + j, cols(w_in, c0 + P + P * i), i)
                invert(i + 1)
                sp.wait_ge(s_form["qd"], i + 2)
                sp.wait_ge(s_vb, i + 2)
                load_tk(i + 2)
                sp.wait_ge(s_gg, i + 1)
                sp.dma_start(yl[:, :], yb_d[bass.ds(P + P * i, P), :]).then_inc(s_yl, 16)
            for n in range(3):
                load_w(W_OUT + n, cols(w_out, n * P))
            invert(NCH - 1)

            def load_y(b, src, dst):
                o, w = OBLOCKS[b]
                sp.dma_start(dst[b % 2][:, :, :], src[:, o:o + w].rearrange("(k p) t -> p k t", p=P)
                             ).then_inc(s_yin[b % 2], 16)

            ot_from = ot_d[:, PAD + OFF:]
            sp.wait_ge(s_za, 16 * HEADS)
            sp.wait_ge(s_form["qd"], NCH)
            sp.wait_ge(s_vb, NCH)
            load_y(0, za_d, yz)
            sp.wait_ge(s_yg, 16 * (HEADS + 1))
            sp.wait_ge(s_ev["QK"], 2 * NCH)
            load_y(0, yg_d, yg)
            sp.wait_ge(s_ps[LAST_Y], 2 * (NCH - 1))
            sp.wait_ge(s_ot, 16 * (NCH - 1))
            load_y(0, ot_from, yo)
            load_y(1, za_d, yz)
            load_y(1, yg_d, yg)
            sp.wait_ge(s_ps["O"], 2 * NCH)
            load_y(1, ot_from, yo)
            for n in range(3, 6):
                load_w(W_OUT + n, cols(w_out, n * P))
            sp.wait_ge(s_y, 2)
            load_y(2, za_d, yz)
            load_y(2, yg_d, yg)
            sp.wait_ge(s_ot, 16 * NCH)
            load_y(2, ot_from, yo)
            sp.wait_ge(s_y, 6)
            sp.dma_start(gffn[:, :], norm_ffn.broadcast_to([P, D])).then_inc(s_gffn, 16)
            sp.dma_start(h2m[:, :], meta_tokens[OFF:META, :]).then_inc(s_h2x[0], 16)
            for g, (t0, t1) in enumerate(((0, 2), (2, 5), (5, KT))):
                sp.dma_start(h2[:, t0:t1, :], x[0, t0 * P:t1 * P, :].rearrange("(t p) d -> p t d", p=P)
                             ).then_inc(s_h2x[g], 16)
                if g < 2:
                    load_w(W_OUT + 6 + g, cols(w_out, (6 + g) * P))

            def up_cols(j):
                return (j % 2) * DFF + (j // 2) * P

            for j in range(4):
                load_w(W_UP0 + j, cols(w_up, up_cols(j)))
            with sp.Fori(0, FFN_ITERS - 1) as i:
                for j in range(6):
                    if j in (2, 3):
                        load_w(W_FFN + j, w_down[0, bass.ds(2 * P * i + (j - 2) * P, P), :], i, 6, wide=True)
                    else:
                        jj = j if j < 2 else j - 2
                        load_w(W_FFN + j, cols(w_up, up_cols(jj) + 2 * P + 2 * P * i), i, 6)
            for k in range(2):
                load_w(W_LAST + k, w_down[0, (FT - 2 + k) * P:(FT - 1 + k) * P, :], wide=True)
            sp.dma_start(fing[:, :], norm_final.rearrange("(o d) -> o d", o=1).broadcast_to([P, D])
                         ).then_inc(s_fg, 16)
            for t in range(KT):
                sp.wait_ge(s_fin, t + 1)
                sp.dma_start(out[0, t * P:(t + 1) * P, :], fino[:, t % 2, :]).then_inc(s_out[t % 2], 16)
            sp.wait_ge(s_out[0], 16 * KT // 2)
            sp.wait_ge(s_out[1], 16 * KT // 2)

        @block.gpsimd
        def _(pool):
            pool.memset(prow[:, :, :], 0.0)
            pool.memset(tiny[:, :], 0.0)
            pool.memset(ab_beta[:, :], 0.0)
            pool.memset(ab_g[:, :], 0.0).then_inc(s_zero, 1)
            pool.wait_ge(s_zero, 1)
            pool.memset(eps_t, EPS).then_inc(s_zero, 1)
            with nc.allow_non_contiguous_dma(reason="sixteen words"):
                pool.dma_start(hdp[8:16, 0:1], dt_bias.rearrange("o h -> h o")).then_inc(s_hd, 16)
                pool.dma_start(hdp[8:16, 1:2], a_log.rearrange("o h -> h o")).then_inc(s_hd, 16)

            def rows(v):
                return v.rearrange("o (i p) -> (o i) p", p=P)

            cf = conv_ffn.rearrange("o j (i p) -> (o j i) p", p=P)
            for dst, src in ((prow[0:R_PSC, 0, :], conv_qkv.rearrange("o j (i p) -> (o j i) p", p=P)),
                             (prow[R_PSC:R_PSC + 8, 0, :], rows(pool_scale)),
                             (prow[R_HN:R_HN + 1, 0, :], head_norm),
                             (prow[0:88, 1, :], cf[0:88, :]), (prow[0:44, 2, :], cf[88:132, :])):
                pool.dma_start(dst, src).then_inc(s_prow, 16)

            def w_low(n, i=0, per=3):
                pool.wait_ge(s_whi, n + 1 + per * i)
                pool.tensor_tensor(w_lo[:, n % SLOTS, :], w_raw[:, n % SLOTS, :],
                                   w_hi[:, n % SLOTS, :].bitcast(F32), ALU.subtract).then_inc(s_wlo, 1)

            w_low(W_AB)
            w_low(W_QKV)
            w_low(W_QKV + 1)
            pool.wait_ge(s_u, 2 * (KT + 1))
            pool.memset(xb[:, :, 0:3], 0.0)
            pool.memset(sl[:, 0:PAD], 0.0)
            pool.memset(px[:, 0:16], 0.0)
            pool.memset(pa[:, 0:16], 0.0)
            pool.memset(pb[:, 0:16], 0.0).then_inc(s_zero, 1)

            def squares(j, i=0):
                w_low(W_QKV + 2 + j, i)
                pool.wait_ge(s_tm, 3 * i + j + 1)
                if j > 0:
                    pool.wait_ge(s_ssq, 3 * i + j)
                pool.tensor_tensor(sq[:, :, :], tm[:, :, :], tm[:, :, :], ALU.mult).then_inc(s_sq, 1)

            for j in range(3):
                squares(j)
            with pool.Fori(0, QKV_TILES // 3 - 1) as i:
                for j in range(3, 6):
                    squares(j, i)
            for n in range(W_QKV + QKV_TILES + 2, W_ZG + 3):
                w_low(n)

            def mask(c):
                pool.tensor_tensor(nmx[:, :, :], per_head(factor(GCUM, c)),
                                   over_heads(cst[:, C_NEG:C_NEG + P]), ALU.add).then_inc(s_nm, 1)

            def state_parts(c):
                pool.tensor_tensor(kd[:, :, :], tk[:, HEADS:2 * HEADS, :], per_head(factor(FKD, c)),
                                   ALU.mult).then_inc(s_kd, 1)
                pool.tensor_tensor(vb[:, :, :], tk[:, 2 * HEADS:, :], per_head(factor(FV, c)),
                                   ALU.mult).then_inc(s_vb, 1)

            def substitute(c, n=BLKS):
                n *= HEADS
                low = blk[0:n, :].rearrange("p (r c) -> p r c", c=SUB)
                inv = sol[0:n, :].rearrange("p (r c) -> p r c", c=SUB)
                pool.memset(sol[0:n, :], 0.0)
                pool.drain()
                pool.memset(sol[0:n, ::SUB + 1], 1.0)
                pool.drain()
                pool.wait_ge(s_blk, 16 * c + 16)
                for j in range(SUB - 1):
                    rest = SUB - 1 - j
                    out = upd[0:n, 0:rest * (j + 1)].rearrange("p (r c) -> p r c", c=j + 1)
                    pool.tensor_tensor(out, low[:, j, j + 1:].unsqueeze(2).broadcast_to([n, rest, j + 1]),
                                       inv[:, j, 0:j + 1].unsqueeze(1).broadcast_to([n, rest, j + 1]), ALU.mult)
                    pool.drain()
                    t = pool.tensor_tensor(inv[:, j + 1:, 0:j + 1], inv[:, j + 1:, 0:j + 1], out, ALU.subtract)
                    if j < SUB - 2:
                        pool.drain()
                t.then_inc(s_sol, 1)

            pool.wait_ge(s_fac, 1)
            pool.wait_ge(s_gfree, U_ZG)
            pool.wait_ge(s_yb[0], 16 * 4)
            pool.wait_ge(s_yb[1], 16 * 4)
            mask(0)
            pool.memset(bd[:, :, :], 0.0).then_inc(s_zero, 1)
            pool.memset(gs[:, 0:1], 0.0).then_inc(s_yg, 16)
            pool.wait_ge(s_tk, 16)
            substitute(0, 1)
            state_parts(0)
            for h in range(2):
                pool.memset(heads(st, h), 0.0).then_inc(s_ev["SU"], 1)
            with pool.Fori(0, HEADS) as i:
                pool.wait_ge(s_ev[LAST_Y], 2 * i + 2)
                mask(i + 1)
                substitute(i + 1)
                pool.wait_ge(s_ps["SU"], 2 * i + 2)
                pool.wait_ge(s_ps["OT"], 2 * i + 2)
                pool.wait_ge(s_tk, 16 * i + 32)
                state_parts(i + 1)
                for j in range(3):
                    w_low(W_ZG + 3 + j, i)
            for n in range(3, KT):
                w_low(W_OUT + n)
            for j in range(4):
                w_low(W_UP0 + j)
            with pool.Fori(0, FFN_ITERS - 1) as i:
                for j in range(6):
                    w_low(W_FFN + j, i, 6)
            w_low(W_LAST)
            w_low(W_LAST + 1)

        @block.tensor
        def _(pe):
            def w_ready(n, i=0, per=3):
                pe.wait_ge(s_wlo, n + 1 + per * i)

            def unit(n, bank, o, w, k0=0, k1=KT):
                for k in range(k0, k1):
                    w1, w2 = (v[:, n % SLOTS, k * P:(k + 1) * P] for v in (w_hi, w_lo))
                    u1, u2 = (v[:, k, o:o + w] for v in (u_hi, u_lo))
                    for m, (wt, u) in enumerate(((w1, u1), (w1, u2), (w2, u1))):
                        mm = pe.matmul(gb[:, bank, 0:w], wt, u, start=(k == 0 and m == 0),
                                       stop=(k == KT - 1 and m == 2))
                return mm

            pe.wait_ge(s_const, 16)
            for j in range(KT + 1):
                pe.wait_ge(s_xs, j + 1)
                n = META if j == 0 else P
                for h in range(2):
                    if j >= 2:
                        pe.wait_ge(s_u, 2 * (j - 2) + h + 1)
                    for k in range(4 * h, 4 * h + 4):
                        t = pe.transpose(db[:, 2 * (j % 2) + h, k % 4 * P:k % 4 * P + n],
                                         xs[0:n, j % 2, k * P:(k + 1) * P], cst[0:n, C_ID:C_ID + n])
                    t.then_inc(s_nt, 1)
                if j == 4:
                    pe.wait_ge(s_prow, 16 * 5)
                    for r, n in enumerate((R_CF, 88, 44)):
                        t = pe.transpose(mb[:, r * P:r * P + n], prow[0:n, r, :], cst[0:n, C_ID:C_ID + n])
                    t.then_inc(s_prmT, 1)

            pe.wait_ge(s_u, 2 * (KT + 1))
            w_ready(W_AB)
            for b, (o, w) in enumerate(BLOCKS):
                unit(W_AB, b, o, w).then_inc(s_g, 1)

            def project(n, before, i=0):
                w_ready(n, i)
                for b, (o, w) in enumerate(BLOCKS):
                    pe.wait_ge(s_gfree, before + b - 2 + 3 * 3 * i)
                    unit(n, b, o, w).then_inc(s_g, 1)

            def turn(n, first=False):
                pe.wait_ge(s_sl, n + 1)
                if not first:
                    pe.wait_ge(s_tm, n)
                for r, (c0, c1) in enumerate(((0, 4), (4, 8), (8, NCH))):
                    for c in range(c0, c1):
                        t = pe.transpose(db[:, r, (c - c0) * P:(c - c0 + 1) * P], sl[:, c * P:(c + 1) * P], ident)
                    t.then_inc(s_tmps, 1)

            for n in range(3):
                project(W_QKV + n, U_QKV + 3 * n)
                if n:
                    turn(n - 1, n == 1)
            with pe.Fori(0, QKV_TILES // 3 - 1) as i:
                for j in range(3, 6):
                    project(W_QKV + j, U_QKV + 3 * j, i)
                    turn(3 * i + j - 1)
            for g in range(4):
                project(W_POOL + g, U_POOL + 3 * g)
                if g == 0:
                    turn(QKV_TILES - 1)
            pe.wait_ge(s_ab, 1)
            pe.wait_ge(s_prm, 3)
            for c in range(NCH):
                for m, src in enumerate((ab_beta, ab_g)):
                    t = pe.transpose(mb[:, (m * NCH + c) * 16:(m * NCH + c + 1) * 16],
                                     src[:, c * P:(c + 1) * P], cst[0:16, C_ID:C_ID + 16])
            t.then_inc(s_abT, 1)
            pe.wait_ge(s_gtok, 1)
            pe.matmul(mb[:, 288:288 + NCH * HEADS], cst[:, C_CUM:C_CUM + P], gtok[:, :], start=True, stop=True)
            pe.matmul(mb[:, 360:360 + NCH * HEADS], cst[:, C_CUM + P - 1:C_CUM + P].broadcast_to([P, P]),
                      gtok[:, :], start=True, stop=True).then_inc(s_gcum, 1)
            w_ready(W_WPOOL)
            for j in range(KT):
                g = j // 2
                pe.wait_ge(s_plo, g + 1)
                ws = slice(g * 2 * P + (j % 2) * P, g * 2 * P + (j % 2 + 1) * P)
                w1, w2 = (v[:, W_WPOOL % SLOTS, ws] for v in (w_hi, w_lo))
                for b, (o, w) in enumerate(OBLOCKS):
                    pe.wait_ge(s_gfree, U_WPOOL - 3 + 3 * j + b + 1)
                    u1, u2 = (v[:, g, OFF + o:OFF + o + w] for v in (p_hi, p_lo))
                    for m, (wt, u) in enumerate(((w1, u1), (w1, u2), (w2, u1))):
                        mm = pe.matmul(gb[:, b, 0:w], wt, u, start=(m == 0), stop=(m == 2))
                    mm.then_inc(s_g, 1)

            def step(name, c, freed):
                bank = 2 * (STEPS.index(name) % 2)

                def each(inputs, op):
                    for h in range(2):
                        if freed:
                            pe.wait_ge(s_ev[freed[0]], freed[1] + h + 1)
                        for s, v in inputs:
                            pe.wait_ge(s, v + h + 1)
                        for m in range(4):
                            t = op(db[:, bank + h, m * P:(m + 1) * P], 4 * h + m)
                        t.then_inc(s_ps[name], 1)

                def turned(src):
                    return lambda o, m: pe.transpose(o, src[:, m, :], ident)

                def product(a, b):
                    return lambda o, m: pe.matmul(o, a[:, m, :], b[:, m, :], start=True, stop=True)

                done = {n: (s_ev[n], 2 * (c - 1) if n in DOUBLING and n != LAST_Y else 2 * c) for n in STEPS}
                if name in FORM:
                    f, n = FORM[name]
                    pe.wait_ge(s_form[f], c + 1)
                    each([], turned(form[:, n]))
                elif name == "GROW":
                    pe.wait_ge(s_gcp, c + 1)
                    each([], lambda o, m: pe.transpose(o, gcur[:, m:m + 1].broadcast_to([P, P]), ident))
                elif name == "KK":
                    each([done["TKN"], done["TKB"]], product(knt, kbt))
                elif name == "QK":
                    each([done["TQ"]], product(knt, qnt))
                elif name == "TT0":
                    pe.wait_ge(s_bd, 16 + 16 * BLKS * c)
                    each([], turned(bd))
                elif name[0] == "X":
                    each([done["KK" if name == "X0" else f"T{int(name[1]) - 1}"]],
                         product(at_m, bd if name == "X0" else tt_m))
                elif name == "Y0":
                    each([done["X0"], done["TT0"]], product(nmx, rr))
                elif name[0] == "Y":
                    each([done["X" + name[1]]], product(nmx, rr))
                elif name[0] == "T":
                    each([done["Y" + name[1]]], turned(rr))
                elif name == "P1":
                    pe.wait_ge(s_ev["SU"], 2 * c + 2)
                    each([done["TKG"]], product(kgt, st))
                elif name == "V":
                    each([done["P1"], done[LAST_Y]], product(rr, orx))
                elif name == "O":
                    def both(o, m):
                        pe.matmul(o, qdt[:, m, :], st[:, m, :], start=True, stop=False)
                        return pe.matmul(o, qkm[:, m, :], vv[:, m, :], start=False, stop=True)
                    each([done["V"], done["QK"], done["TQD"]], both)
                elif name == "SU":
                    pe.wait_ge(s_kd, c + 1)
                    each([done["V"]], product(kd, vv))
                elif name == "OT":
                    pe.wait_ge(s_on, c + 1)
                    each([], turned(orx))

            def same_banks(name, among):
                return [n for n in among if STEPS.index(n) % 2 == STEPS.index(name) % 2]

            pe.wait_ge(s_tm, QKV_TILES)
            for k, name in enumerate(PREP_STEPS):
                held = same_banks(name, PREP_STEPS[:k])
                step(name, 0, (held[-1], 0) if held else None)
            step("TT0", 0, (same_banks("TT0", PREP_STEPS)[-1], 0))
            pe.wait_ge(s_ev["QK"], 2)

            def piece(p, i):
                u, part = divmod(p, 3)
                t, b = divmod(u, 3)
                o, w = OBLOCKS[b]
                if part == 0:
                    if b == 0:
                        w_ready(W_ZG + t, i)
                    if t == 1:
                        pe.wait_ge(s_zfree, 3 * i + b + 1)
                    else:
                        pe.wait_ge(s_gfree, U_ZG - 3 + b + 1 + 6 * i + (3 if t == 2 else 0))
                mm = unit(W_ZG + t, b, OFF + o, w, *PIECES[part])
                if part == 2:
                    mm.then_inc(s_z if t == 0 else s_g, 1)

            with pe.Fori(0, HEADS) as i:
                for k, name in enumerate(STEPS):
                    held = same_banks(name, STEPS[:k])
                    c = i if name in REC else i + 1
                    if not held:
                        freed = (LAST_Y, 2 * i)
                    elif held[-1] in REC:
                        freed = (held[-1], 2 * i + 2 if held[-1] == "SU" else 2 * i)
                    else:
                        freed = (held[-1], 2 * i if held[-1] in DOUBLING else 2 * i + 2)
                    step(name, c, freed)
                    for p in pieces_after(name):
                        piece(p, i)
            for name, prev in (("P1", LAST_Y), ("V", "P1"), ("O", "V"), ("OT", "O")):
                step(name, NCH - 1, (prev, 2 * (NCH - 1)))

            def back(j):
                n, c0 = (HALO, 0) if j == 0 else (P, HALO + (j - 1) * P)
                for h in range(2):
                    if j >= 1:
                        pe.wait_ge(s_h2, 2 * (j - 1) + h + 1)
                    for k in range(4):
                        t = pe.transpose(db[0:n, h, k * P:(k + 1) * P], ht[:, 4 * h + k, c0:c0 + n], ident)
                    t.then_inc(s_h2T, 1)

            def forth(j):
                n = HALO if j == 0 else P
                pe.wait_ge(s_hx, j + 1)
                for h in range(2):
                    if j >= 1:
                        pe.wait_ge(s_u2, 2 * (j - 1) + h + 1)
                    for k in range(4 * h, 4 * h + 4):
                        t = pe.transpose(db[:, 2 + h, k % 4 * P:k % 4 * P + n], hx[0:n, j % 2, k * P:(k + 1) * P],
                                         cst[0:n, C_ID:C_ID + n])
                    t.then_inc(s_hnt, 1)

            q = 0
            for kind, *at_ in OUT_PLAN:
                if kind == "unit":
                    n, b = at_
                    o, w = OBLOCKS[b]
                    w_ready(W_OUT + n)
                    pe.wait_ge(s_gfree, U_OUT - 3 + q + 1)
                    for hf in range(2):
                        if n == 0:
                            pe.wait_ge(s_y, 2 * b + hf + 1)
                        mm = unit(W_OUT + n, q % 3, o, w, 4 * hf, 4 * hf + 4)
                    mm.then_inc(s_g, 1)
                    q += 1
                elif kind == "up":
                    n, b = at_
                    o, w = OBLOCKS[b]
                    w_ready(W_UP0 + n)
                    pe.wait_ge(s_u2, 2 * NORMED[b])
                    pe.wait_ge(s_gfree, U_OUT - 3 + q + 1)
                    unit(W_UP0 + n, q % 3, o, w).then_inc(s_g, 1)
                    q += 1
                elif kind == "back":
                    if at_[0] == 0:
                        pe.wait_ge(s_ev["OT"], 2 * NCH)
                        pe.wait_ge(s_ev["O"], 2 * NCH)
                    pe.wait_ge(s_gfree, U_OUT + BACK_UNITS[at_[0]])
                    back(at_[0])
                else:
                    forth(at_[0])

            def up(n, before, i=0):
                w_ready(n, i, 6)
                for b, (o, w) in enumerate(OBLOCKS):
                    pe.wait_ge(s_gfree, before + b - 2 + 12 * i)
                    unit(n, b, o, w).then_inc(s_g, 1)

            def down(n, i):
                w_ready(n + 1, 0 if n == W_LAST else i, 6)
                pe.wait_ge(s_alo, 2 * i + 2)
                for u in range(2 * KT):
                    t, half = divmod(u, 2)
                    if u > 3:
                        pe.wait_ge(s_dnfree, 16 * i + u - 3)
                    for q in range(2):
                        a1, a2 = (v[:, q, t * P:(t + 1) * P] for v in (a_hi, a_lo))
                        w1, w2 = (v[:, (n + q) % SLOTS, half * 512:(half + 1) * 512] for v in (w_hi, w_lo))
                        for m, (a, wt) in enumerate(((a1, w1), (a1, w2), (a2, w1))):
                            mm = pe.matmul(db[:, u % 4, :], a, wt, start=(q == 0 and m == 0),
                                           stop=(q == 1 and m == 2))
                    mm.then_inc(s_dn, 1)

            for j in range(2, 4):
                up(W_UP0 + j, U_UP0 + 3 * j)
            with pe.Fori(0, FFN_ITERS - 1) as i:
                up(W_FFN, U_FFN, i)
                up(W_FFN + 1, U_FFN + 3, i)
                down(W_FFN + 2, i)
                up(W_FFN + 4, U_FFN + 6, i)
                up(W_FFN + 5, U_FFN + 9, i)
                pe.wait_ge(s_dnfree, 16 * i + 2 * KT)
            down(W_LAST, FFN_ITERS - 1)

        @block.scalar
        def _(act):
            def w_high(n, i=0, per=3):
                act.wait_ge(s_w[n % SLOTS], 16 * (n // SLOTS + 1) + 16 * (per // 3) * i)
                act.activation(w_hi[:, n % SLOTS, :], w_raw[:, n % SLOTS, :], ACT.Copy).then_inc(s_whi, 1)

            def root(j, n, src, junk, done):
                act.activation(junk, src, ACT.Square, accum_out=nss[0:n, j:j + 1])
                act.drain()
                act.activation(nss[0:n, j:j + 1], nss[0:n, j:j + 1], ACT.Sqrt, bias=eps_t[0:n, :],
                               scale=1.0 / D).then_inc(done, 1)

            def norm_root(j):
                n = META if j == 0 else P
                act.wait_ge(s_x[j % 3], 16 * (j // 3 + 1))
                if j >= 2:
                    act.wait_ge(s_nt, 2 * (j - 1))
                root(j, n, xt[0:n, j % 3, :], xs[0:n, j % 2, :], s_nsq)

            act.wait_ge(s_zero, 2)
            norm_root(0)
            for j in range(KT + 1):
                if j < KT:
                    norm_root(j + 1)
                n, c0 = (META, 0) if j == 0 else (P, META + (j - 1) * P)
                for h in range(2):
                    act.wait_ge(s_nt, 2 * j + h + 1)
                    act.activation(u_hi[:, 4 * h:4 * h + 4, c0:c0 + n], tbank(2 * (j % 2) + h, n),
                                   ACT.Copy).then_inc(s_uhi, 1)
                if j == 5:
                    act.wait_ge(s_prmT, 1)
                    for r, (p0, m) in enumerate(((0, R_CF), (R_CF, 88), (R_CF + 88, 44))):
                        act.activation(prm[:, p0:p0 + m], mb[:, r * P:r * P + m], ACT.Copy).then_inc(s_prm, 1)
                if j in (2, 4, 6):
                    w_high(W_AB + (j - 2) // 2)

            act.wait_ge(s_hd, 32)
            for b, (o, w) in enumerate(BLOCKS):
                act.wait_ge(s_g, b + 1)
                act.activation(ab_beta[:, PAD + o:PAD + o + w], gb[0:16, b, 0:w], ACT.Sigmoid)
                act.activation(ab_t[:, PAD + o:PAD + o + w], gb[0:16, b, 0:w], ACT.Identity,
                               bias=hdp[:, 0:1]).then_inc(s_gfree, 1)
            w_high(W_QKV + 2)
            act.drain()
            act.activation(ab_g[:, PAD:], ab_t[:, PAD:], ACT.Abs)
            act.activation(hdp[:, 2:3], hdp[:, 1:2], ACT.Exp)
            act.drain()
            act.activation(ab_g[:, PAD:], ab_g[:, PAD:], ACT.Exp, scale=-1.0)
            act.activation(ab_t[:, PAD:], ab_t[:, PAD:], ACT.Relu)
            act.drain()
            act.activation(ab_g[:, PAD:], ab_g[:, PAD:], ACT.Ln, bias=1.0).then_inc(s_na, 1)

            def silu(n):
                act.wait_ge(s_conv, n + 1)
                act.wait_ge(s_tmps, 3 * n)
                act.activation(sl[:, PAD:], cacc[:, :], ACT.Silu).then_inc(s_sl, 1)

            def by_tokens(n):
                act.wait_ge(s_sq, n)
                act.wait_ge(s_spill, 16 * n)
                for r, (c0, c1) in enumerate(((0, 4), (4, 8), (8, NCH))):
                    act.wait_ge(s_tmps, 3 * n + r + 1)
                    t = act.activation(tm[:, c0:c1, :].rearrange("p c d -> p (c d)"), db[:, r, 0:(c1 - c0) * P],
                                       ACT.Copy)
                t.then_inc(s_tm, 1)
                act.wait_ge(s_tm, n + 1)
                act.dma_start(qkv_d[:, bass.ds(n * P, P)].rearrange("(c p) d -> p c d", p=P),
                              tm[:, :, :]).then_inc(s_spill, 16)

            def qkv_tile(j, i=0):
                n = j + 3 * i
                if j > 0:
                    act.wait_ge(s_g, 3 * n + 3)
                    w_high(W_QKV + j + 2, i)
                for b, (o, w) in enumerate(BLOCKS):
                    if b == 0 and j >= 3:
                        act.wait_ge(s_conv, n - 2)
                    act.wait_ge(s_g, U_QKV + 3 * n + b + 1)
                    act.activation(xb[:, j % 3, 3 + o:3 + o + w], gb[:, b, 0:w], ACT.Copy).then_inc(s_gfree, 1)
                    if b == 1 and j > 0:
                        silu(n - 1)
                if j > 0:
                    by_tokens(n - 1)

            act.wait_ge(s_zero, 3)
            for j in range(3):
                qkv_tile(j)
            with act.Fori(0, QKV_TILES // 3 - 1) as i:
                for j in range(3, 6):
                    qkv_tile(j, i)

            for g in range(4):
                act.wait_ge(s_g, 3 * (W_POOL + g))
                w_high(W_POOL + g + 2)
                for b, (o, w) in enumerate(BLOCKS):
                    if g and b == 0:
                        act.wait_ge(s_pw, g)
                    act.wait_ge(s_g, U_POOL + 3 * g + b + 1)
                    act.activation(px[:, 16 + o:16 + o + w], gb[:, b, 0:w], ACT.Copy).then_inc(s_gfree, 1)
                    if g == 0 and b == 1:
                        silu(QKV_TILES - 1)
                if g == 0:
                    by_tokens(QKV_TILES - 1)
                act.wait_ge(s_pw, g + 1)
                act.activation(p_hi[:, g, :], pool_out(g)[:, 16:], ACT.Copy).then_inc(s_phi, 1)
            act.wait_ge(s_g, U_WPOOL)
            w_high(W_WPOOL + 2)

            act.wait_ge(s_gsb, 1)
            act.activation(gtmp[:, 1, :], gflat(GCUM), ACT.Exp)
            act.activation(gtmp[:, 2, :], gtmp[:, 0, :], ACT.Exp)
            act.activation(gflat(EGT), mb[:, 360:360 + NCH * HEADS], ACT.Exp)
            act.wait_ge(s_ssq, QKV_TILES)
            act.activation(ssq[:, 0:2 * HEADS, :], ssq[:, 0:2 * HEADS, :], ACT.Sqrt, bias=eps_t).then_inc(s_exp, 1)

            for j in range(KT):
                if j >= 2:
                    act.wait_ge(s_yb[j % 2], 16 * (j // 2))
                for b, (o, w) in enumerate(OBLOCKS):
                    act.wait_ge(s_g, U_WPOOL + 3 * j + b + 1)
                    act.activation(ybs[:, j % 2, o:o + w], gb[:, b, 0:w], ACT.Copy,
                                   scale=gain(R_PSC + j, 1)).then_inc(s_gfree, 1)
                act.wait_ge(s_gfree, U_WPOOL + 3 * j + 3)
                act.dma_start(yb_d[j * P:(j + 1) * P, :], ybs[:, j % 2, :]).then_inc(s_yb[j % 2], 16)
            w_high(W_ZG + 2)

            def copy_halves(name, dst, c, turns=None):
                for h in range(2):
                    act.wait_ge(s_ps[name], 2 * (c if turns is None else turns) + h + 1)
                    act.activation(heads(dst, h), dbank(name, h), ACT.Copy).then_inc(s_ev[name], 1)

            def act_step(name, c):
                if name == "TQ":
                    copy_halves(name, qnt, c)
                elif name == "TKN":
                    copy_halves(name, knt, c)
                elif name == "TQD":
                    copy_halves(name, qdt, c)
                elif name == "TKG":
                    copy_halves(name, kgt, c)
                elif name == "GROW":
                    for h in range(2):
                        act.wait_ge(s_ev[name], 2 * c + h + 1)
                        act.activation(heads(ex, h), heads(ex, h), ACT.Exp).then_inc(s_dec, 1)
                elif name == "TT0":
                    copy_halves(name, rr, c - 1, turns=c)
                elif name in DOUBLING and name[0] == "T":
                    copy_halves(name, tt_m, c - 1)
                elif name == "V":
                    copy_halves(name, vv, c)
                elif name == "O":
                    for h in range(2):
                        act.wait_ge(s_ps[name], 2 * c + h + 1)
                        act.activation(heads(ots, h), dbank(name, h), ACT.Square).then_inc(s_osq, 1)
                        act.activation(heads(orx, h), dbank(name, h), ACT.Copy).then_inc(s_ev[name], 1)
                elif name == "SU":
                    act.wait_ge(s_oss, c + 1)
                    act.activation(orr, oss, ACT.Sqrt, bias=eps_t, scale=1.0 / P).then_inc(s_ort, 1)
                elif name == "OT":
                    copy_halves(name, ots, c)
                    act.wait_ge(s_ev[name], 2 * c + 2)
                    act.dma_start(ot_d[:, bass.ds(c * P, P)].rearrange("(h d) t -> d h t", d=P),
                                  ots[:, :, :]).then_inc(s_ot, 16)

            for name in PREP_STEPS:
                act_step(name, 0)
            for h in range(2):
                act.wait_ge(s_ps["TT0"], h + 1)
                act.activation(heads(rr, h), dbank("TT0", h), ACT.Copy).then_inc(s_ev[LAST_Y], 1)

            def gates(u, i):
                t, b = divmod(u, 3)
                o, w = OBLOCKS[b]
                if t == 0:
                    act.wait_ge(s_z, 3 * i + b + 1)
                    act.activation(zs[:, o:o + w], gb[:, b, 0:w], ACT.Sigmoid).then_inc(s_zsig, 1)
                else:
                    if t == 1:
                        act.wait_ge(s_yg, 16 * i + 16)
                    elif b == 0:
                        act.wait_ge(s_zg, i + 1)
                        act.dma_start(za_d[bass.ds(i * P, P), :], zs[:, :]).then_inc(s_za, 16)
                    act.wait_ge(s_g, U_ZG + 6 * i + 3 * (t - 1) + b + 1)
                    act.activation(gs[:, o:o + w], gb[:, b, 0:w], ACT.Sigmoid).then_inc(s_gfree, 1)
                if b == 2:
                    w_high(W_ZG + 3 + t, i)
                if u == 8:
                    act.wait_ge(s_gg, i + 1)
                    act.dma_start(yg_d[bass.ds(i * P, P), :], gs[:, :]).then_inc(s_yg, 16)

            with act.Fori(0, HEADS) as i:
                for name in STEPS:
                    act_step(name, i if name in REC else i + 1)
                    for u in units_after(name):
                        gates(u, i)
                act.wait_ge(s_ot, 16 * i + 16)
                act.wait_ge(s_za, 16 * i + 16)
            for name in REC:
                act_step(name, NCH - 1)

            def y_high(b):
                o, w = OBLOCKS[b]
                for hf in range(2):
                    ks = slice(4 * hf, 4 * hf + 4)
                    act.wait_ge(s_y1, 2 * b + hf + 1)
                    act.activation(u_hi[:, ks, o:o + w], yo[b % 2][:, ks, :], ACT.Copy).then_inc(s_yhi, 1)

            def high2(j):
                n, c0 = (HALO, 0) if j == 0 else (P, HALO + (j - 1) * P)
                for h in range(2):
                    act.wait_ge(s_hnt, 2 * j + h + 1)
                    act.activation(u_hi[:, 4 * h:4 * h + 4, c0:c0 + n], tbank(2 + h, n), ACT.Copy).then_inc(s_u2hi, 1)

            y_high(0)
            q = 0
            for kind, *at_ in OUT_PLAN:
                if kind == "unit":
                    n, b = at_
                    o, w = OBLOCKS[b]
                    if n == 0 and b < 2:
                        y_high(b + 1)
                    act.wait_ge(s_g, U_OUT + q + 1)
                    act.activation(ht[:, n, o:o + w], gb[:, q % 3, 0:w], ACT.Copy).then_inc(s_gfree, 1)
                    q += 1
                    if b == 2:
                        w_high(W_OUT + n + 3)
                elif kind == "up":
                    n, b = at_
                    o, w = OBLOCKS[b]
                    act.wait_ge(s_g, U_OUT + q + 1)
                    act.activation((xg, xv)[n][:, o:o + w], gb[:, q % 3, 0:w], ACT.Copy).then_inc(s_gfree, 1)
                    q += 1
                elif kind == "back":
                    j = at_[0]
                    n = HALO if j == 0 else P
                    act.wait_ge(s_h2, 2 * j + 2)
                    if j >= 2:
                        act.wait_ge(s_hnt, 2 * (j - 1))
                    root(j, n, h2m[:, :] if j == 0 else h2[:, j - 1, :], hx[0:n, j % 2, :], s_h2sq)
                else:
                    high2(at_[0])

            def take(j, before, i=0):
                dst = xg if j % 2 == 0 else xv
                for b, (o, w) in enumerate(OBLOCKS):
                    act.wait_ge(s_g, before + b + 1 + 12 * i)
                    act.activation(dst[:, o:o + w], gb[:, b, 0:w], ACT.Copy).then_inc(s_gfree, 1)

            def gate(p):
                act.wait_ge(s_cg, p + 1)
                act.wait_ge(s_act, p)
                act.activation(sg[:, :], cg[:, :], ACT.Silu).then_inc(s_sg, 1)

            def high(p, q, turns):
                act.wait_ge(s_dn, 16 * turns)
                act.wait_ge(s_act, p + 1)
                act.activation(a_hi[:, q, :], cv[:, :], ACT.Copy).then_inc(s_ahi, 1)

            for q in range(2):
                if q == 0:
                    w_high(W_UP0 + 3)
                    w_high(W_UP0 + 4)
                else:
                    act.wait_ge(s_cg, 1)
                    take(0, U_UP0 + 6)
                    w_high(W_UP0 + 5)
                    act.wait_ge(s_cv, 1)
                    take(1, U_UP0 + 9)
                gate(q)
                high(q, q, 0)
            with act.Fori(0, FFN_ITERS - 1) as i:
                act.wait_ge(s_g, U_FFN + 12 * i)
                w_high(W_FFN + 2, i, 6)
                act.wait_ge(s_cg, 2 * i + 2)
                take(0, U_FFN, i)
                w_high(W_FFN + 3, i, 6)
                act.wait_ge(s_cv, 2 * i + 2)
                take(1, U_FFN + 3, i)
                w_high(W_FFN + 4, i, 6)
                gate(2 * i + 2)
                high(2 * i + 2, 0, i + 1)
                w_high(W_FFN + 5, i, 6)
                w_high(W_FFN + 6, i, 6)
                act.wait_ge(s_cg, 2 * i + 3)
                take(0, U_FFN + 6, i)
                w_high(W_FFN + 7, i, 6)
                act.wait_ge(s_cv, 2 * i + 3)
                take(1, U_FFN + 9, i)
                gate(2 * i + 3)
                high(2 * i + 3, 1, i + 1)

            for t in range(KT):
                act.wait_ge(s_dnfree, 16 * (FFN_ITERS - 1) + 2 * t + 2)
                if t >= 2:
                    act.wait_ge(s_out[t % 2], 16 * (t // 2))
                root(t, P, h2[:, t, :], fino[:, t % 2, :], s_fsq)

        @block.vector
        def _(dve):
            def drain():
                dve.drain()

            def scale(j):
                n = META if j == 0 else P
                dve.wait_ge(s_nsq, j + 1)
                dve.reciprocal(nss[0:n, j:j + 1], nss[0:n, j:j + 1])
                drain()
                dve.scalar_tensor_tensor(xs[0:n, j % 2, :], xt[0:n, j % 3, :], nss[0:n, j:j + 1], gmix[0:n, :],
                                         ALU.mult, ALU.mult).then_inc(s_xs, 1)

            dve.wait_ge(s_gmix, 16)
            scale(0)
            for j in range(KT + 1):
                if j < KT:
                    scale(j + 1)
                n, c0 = (META, 0) if j == 0 else (P, META + (j - 1) * P)
                for h in range(2):
                    dve.wait_ge(s_uhi, 2 * j + h + 1)
                    dst = slice(4 * h, 4 * h + 4), slice(c0, c0 + n)
                    dve.tensor_tensor(u_lo[:, dst[0], dst[1]], tbank(2 * (j % 2) + h, n),
                                      u_hi[:, dst[0], dst[1]].bitcast(F32), ALU.subtract).then_inc(s_u, 1)
            dve.wait_ge(s_prm, 3)

            dve.wait_ge(s_na, 1)
            dve.tensor_tensor(ab_g[:, PAD:], ab_g[:, PAD:], ab_t[:, PAD:], ALU.add)
            drain()
            dve.tensor_scalar(ab_g[:, PAD:], ab_g[:, PAD:], hdp[:, 2:3], -1.0, ALU.mult, ALU.mult).then_inc(s_ab, 1)

            taps = 4

            def conv(n, slot):
                dve.wait_ge(s_gfree, U_QKV + 3 * n + 3)
                dve.wait_ge(s_sl, n)

                def tap(j):
                    return prm[:, bass.ds(R_CONV + j * QKV_TILES + n, 1)]

                dve.tensor_scalar(cacc[:, :], xb[:, slot, 3:3 + T], tap(taps - 1), None, ALU.mult)
                for j in range(taps - 2, -1, -1):
                    drain()
                    t = dve.scalar_tensor_tensor(cacc[:, :], xb[:, slot, j:j + T], tap(j), cacc[:, :],
                                                 ALU.mult, ALU.add)
                t.then_inc(s_conv, 1)

            def sums(n):
                dve.wait_ge(s_sq, n + 1)
                dve.tensor_reduce(ssq[:, bass.ds(n, 1), :].rearrange("p o c -> p (o c)"), sq[:, :, :], AX_X,
                                  ALU.add).then_inc(s_ssq, 1)

            dve.wait_ge(s_zero, 3)
            conv(0, 0)
            with dve.Fori(0, QKV_TILES // 3 - 1) as i:
                for j in range(3):
                    conv(1 + 3 * i + j, (1 + j) % 3)
                    sums(3 * i + j)
            for n in (QKV_TILES - 2, QKV_TILES - 1):
                conv(n, n % 3)
                sums(n - 1)

            for g in range(4):
                if g:
                    dve.wait_ge(s_phi, g)
                dve.wait_ge(s_gfree, U_POOL + 3 * g + 3)
                src = px
                for k in range(g + 1):
                    dst = (pa, pb)[k % 2]
                    dve.tensor_tensor(dst[:, 16:], src[:, 16:], src[:, 16 - 2 ** k:16 + T - 2 ** k], ALU.add)
                    drain()
                    src = dst
                dst = pool_out(g)
                dve.tensor_scalar(dst[:, 16:], src[:, 16:], 1.0 / WINDOWS[g], None, ALU.mult)
                drain()
                dve.tensor_tensor(dst[:, 16:32], dst[:, 16:32], cst[:, C_INV + 16 * g:C_INV + 16 * g + 16], ALU.mult)
                drain()
                dve.tensor_tensor(dst[:, 16:], dst[:, 16:], px[:, 16:], ALU.subtract).then_inc(s_pw, 1)
                dve.wait_ge(s_phi, g + 1)
                dve.tensor_tensor(p_lo[:, g, :], dst[:, 16:], p_hi[:, g, :].bitcast(F32),
                                  ALU.subtract).then_inc(s_plo, 1)
                drain()
                if g == 0:
                    sums(QKV_TILES - 1)

            def by_chunk(m):
                return mb[:, m * NCH * 16:(m + 1) * NCH * 16].rearrange("p (c k) -> p c k", k=16)

            dve.wait_ge(s_abT, 1)
            dve.tensor_copy(fac[:, FV, :, :], by_chunk(0)[:, :, 0:8])
            dve.tensor_copy(gtok[:, :].rearrange("p (c h) -> p c h", h=HEADS), by_chunk(1)[:, :, 8:16]).then_inc(s_gtok, 1)
            dve.wait_ge(s_gcum, 1)
            dve.tensor_copy(gflat(GCUM), mb[:, 288:288 + NCH * HEADS])
            drain()
            dve.tensor_tensor(gtmp[:, 0, :], mb[:, 360:360 + NCH * HEADS], gflat(GCUM), ALU.subtract).then_inc(s_gsb, 1)
            dve.wait_ge(s_exp, 1)
            dve.reciprocal(ssq[:, 0:2 * HEADS, :], ssq[:, 0:2 * HEADS, :])
            drain()
            rq = ssq[:, 0:HEADS, :].rearrange("p h c -> p c h")
            rk = ssq[:, HEADS:2 * HEADS, :].rearrange("p h c -> p c h")
            eg = gtmp[:, 1, :].rearrange("p (c h) -> p c h", h=HEADS)
            el = gtmp[:, 2, :].rearrange("p (c h) -> p c h", h=HEADS)
            dve.tensor_scalar(fac[:, FQ], rq, float(P) ** -0.5, None, ALU.mult)
            dve.tensor_copy(fac[:, FK], rk)
            dve.tensor_tensor(fac[:, FKD], rk, el, ALU.mult)
            dve.tensor_tensor(fac[:, FKB], rk, fac[:, FV], ALU.mult)
            drain()
            dve.tensor_tensor(fac[:, FQD], fac[:, FQ], eg, ALU.mult)
            dve.tensor_tensor(fac[:, FKG], fac[:, FKB], eg, ALU.mult).then_inc(s_fac, 1)
            drain()

            def scaled(f, n, src, kind, c):
                dve.tensor_tensor(form[:, n], tk[:, src * HEADS:(src + 1) * HEADS, :], per_head(factor(kind, c)),
                                  ALU.mult).then_inc(s_form[f], 1)

            def halves(name, turns, op, out_sem):
                for h in range(2):
                    dve.wait_ge(s_ps[name], 2 * turns + h + 1)
                    op(h).then_inc(out_sem, 1)

            def dve_step(name, c):
                if name == "TKN":
                    dve.wait_ge(s_ps[name], 2 * c + 2)
                elif name == "TKB":
                    halves(name, c, lambda h: dve.tensor_copy(heads(kbt, h), dbank(name, h)), s_ev[name])
                elif name == "GROW":
                    dve.wait_ge(s_nm, c + 1)
                    halves(name, c, lambda h: dve.tensor_tensor(heads(ex, h), dbank(name, h), heads(nmx, h),
                                                                ALU.subtract), s_ev[name])
                elif name == "KK":
                    for h in range(2):
                        dve.wait_ge(s_dec, 2 * c + h + 1)
                        dve.wait_ge(s_ps[name], 2 * c + h + 1)
                        dve.tensor_tensor(heads(at_m, h), dbank(name, h), heads(ex, h), ALU.mult).then_inc(s_ev[name], 1)
                    scaled("qn", 0, 0, FQ, c)
                    scaled("kg", 1, 1, FKG, c)
                elif name == "TQ":
                    dve.wait_ge(s_ps[name], 2 * c + 2)
                    scaled("qd", 0, 0, FQD, c)
                elif name == "QK":
                    halves(name, c, lambda h: dve.tensor_tensor(heads(qkm, h), dbank(name, h), heads(ex, h),
                                                                ALU.mult), s_ev[name])
                elif name[0] == "X":
                    halves(name, c - 1, lambda h: dve.tensor_tensor(
                        heads(nmx, h), dbank(name, h), over_heads(lvl(int(name[1])), HEADS // 2), ALU.mult), s_ev[name])
                elif name[0] == "Y":
                    halves(name, c - 1, lambda h: dve.tensor_tensor(heads(rr, h), heads(rr, h), dbank(name, h),
                                                                    ALU.subtract), s_ev[name])
                elif name == "P1":
                    dve.wait_ge(s_vb, c + 1)
                    halves(name, c, lambda h: dve.tensor_tensor(heads(orx, h), heads(vb, h), dbank(name, h),
                                                                ALU.subtract), s_ev[name])
                elif name == "O":
                    dve.wait_ge(s_ps[name], 2 * c + 2)
                    dve.tensor_tensor(st[:, :, :], st[:, :, :], per_head(factor(EGT, c)), ALU.mult)
                    dve.wait_ge(s_osq, 2 * c + 2)
                    dve.tensor_reduce(oss, ots[:, :, :], AX_X, ALU.add).then_inc(s_oss, 1)
                elif name == "SU":
                    drain()
                    halves(name, c, lambda h: dve.tensor_tensor(heads(st, h), heads(st, h), dbank(name, h),
                                                                ALU.add), s_ev[name])
                elif name == "TQD":
                    output_scale(c - 1)

            def output_scale(c):
                dve.wait_ge(s_ort, c + 1)
                dve.reciprocal(orr, orr)
                drain()
                dve.wait_ge(s_ev["O"], 2 * c + 2)
                dve.tensor_tensor(orx[:, :, :], orx[:, :, :], per_head(orr), ALU.mult).then_inc(s_on, 1)

            def forms_first(c):
                dve.tensor_copy(gcur, factor(GCUM, c)).then_inc(s_gcp, 1)
                dve.wait_ge(s_tk, 16 * c + 16)
                scaled("kn", 0, 1, FK, c)
                scaled("kb", 1, 1, FKB, c)

            forms_first(0)
            for name in PREP_STEPS:
                if name != "TQD":
                    dve_step(name, 0)

            def gated(u, i):
                t, b = divmod(u, 3)
                o, w = OBLOCKS[b]
                if t == 0:
                    dve.wait_ge(s_zsig, 3 * i + b + 1)
                    dve.scalar_tensor_tensor(zs[:, o:o + w], zs[:, o:o + w], gain(R_HN, 1), gb[:, b, 0:w],
                                             ALU.mult, ALU.mult).then_inc(s_zfree, 1)
                elif u == 5:
                    dve.wait_ge(s_gfree, U_ZG + 6 * i + 3)
                    dve.tensor_tensor(zs[:, :], zs[:, :], gs[:, :], ALU.mult).then_inc(s_zg, 1)
                elif u == 8:
                    dve.wait_ge(s_gfree, U_ZG + 6 * i + 6)
                    dve.wait_ge(s_yl, 16 * i + 16)
                    dve.tensor_tensor(gs[:, :], gs[:, :], yl[:, :], ALU.mult).then_inc(s_gg, 1)

            dve.wait_ge(s_ev["SU"], 2)
            with dve.Fori(0, HEADS) as i:
                dve_step("P1", i)
                forms_first(i + 1)
                for name in STEPS[1:]:
                    dve_step(name, i if name in REC else i + 1)
                    for u in units_after(name):
                        gated(u, i)
            dve_step("P1", NCH - 1)
            dve.wait_ge(s_osq, 2 * NCH)
            dve.tensor_reduce(oss, ots[:, :, :], AX_X, ALU.add).then_inc(s_oss, 1)
            output_scale(NCH - 1)

            for b, (o, w) in enumerate(OBLOCKS):
                s = b % 2
                dve.wait_ge(s_yin[s], 48 * (b // 2 + 1))
                halves_k = slice(0, 4), slice(4, 8)
                for ks in halves_k:
                    dve.tensor_tensor(yo[s][:, ks, :], yo[s][:, ks, :], yz[s][:, ks, :], ALU.mult)
                    drain()
                    dve.tensor_tensor(yo[s][:, ks, :], yo[s][:, ks, :], yg[s][:, ks, :], ALU.add).then_inc(s_y1, 1)
                for hf, ks in enumerate(halves_k):
                    dve.wait_ge(s_yhi, 2 * b + hf + 1)
                    dve.tensor_tensor(u_lo[:, ks, o:o + w], yo[s][:, ks, :], u_hi[:, ks, o:o + w].bitcast(F32),
                                      ALU.subtract).then_inc(s_y, 1)

            def residual(j):
                n = HALO if j == 0 else P
                for h in range(2):
                    dst = h2m[:, h * 512:(h + 1) * 512] if j == 0 else h2[:, j - 1, h * 512:(h + 1) * 512]
                    dve.wait_ge(s_h2x[j // 3], 32 if j < 3 else 16)
                    dve.wait_ge(s_h2T, 2 * j + h + 1)
                    dve.tensor_tensor(dst, dst, db[0:n, h, :], ALU.add).then_inc(s_h2, 1)

            def scale2(j):
                n = HALO if j == 0 else P
                dve.wait_ge(s_h2sq, j + 1)
                dve.reciprocal(nss[0:n, j:j + 1], nss[0:n, j:j + 1])
                drain()
                dve.scalar_tensor_tensor(hx[0:n, j % 2, :], h2m[:, :] if j == 0 else h2[:, j - 1, :], nss[0:n, j:j + 1],
                                         gffn[0:n, :], ALU.mult, ALU.mult).then_inc(s_hx, 1)

            dve.wait_ge(s_gffn, 16)

            def low2(j):
                n, c0 = (HALO, 0) if j == 0 else (P, HALO + (j - 1) * P)
                for h in range(2):
                    dve.wait_ge(s_u2hi, 2 * j + h + 1)
                    dst = slice(4 * h, 4 * h + 4), slice(c0, c0 + n)
                    dve.tensor_tensor(u_lo[:, dst[0], dst[1]], tbank(2 + h, n),
                                      u_hi[:, dst[0], dst[1]].bitcast(F32), ALU.subtract).then_inc(s_u2, 1)

            for kind, *at_ in OUT_PLAN:
                if kind == "back":
                    residual(at_[0])
                    if at_[0]:
                        low2(at_[0] - 1)
                elif kind == "forth":
                    scale2(at_[0])
            low2(KT)

            def conv3(dst, src, f, done):
                def tap(j):
                    return prm[:, bass.ds(R_CF + j * 2 * FT + f, 1)]
                dve.tensor_scalar(dst[:, :], src[:, 2:2 + SEQ], tap(2), None, ALU.mult)
                drain()
                dve.scalar_tensor_tensor(dst[:, :], src[:, 1:1 + SEQ], tap(1), dst[:, :], ALU.mult, ALU.add)
                drain()
                dve.scalar_tensor_tensor(dst[:, :], src[:, 0:SEQ], tap(0), dst[:, :], ALU.mult,
                                         ALU.add).then_inc(done, 1)

            def hidden(p, taken, more=3):
                dve.wait_ge(s_gfree, taken)
                dve.wait_ge(s_sg, p)
                conv3(cg, xg, p, s_cg)
                dve.wait_ge(s_gfree, taken + more)
                conv3(cv, xv, FT + p, s_cv)
                drain()
                dve.wait_ge(s_sg, p + 1)
                dve.tensor_tensor(cv[:, :], cv[:, :], sg[:, :], ALU.mult).then_inc(s_act, 1)

            def low(p, q):
                dve.wait_ge(s_ahi, p + 1)
                dve.tensor_tensor(a_lo[:, q, :], cv[:, :], a_hi[:, q, :].bitcast(F32), ALU.subtract).then_inc(s_alo, 1)

            def add_down(i):
                for u in range(2 * KT):
                    t, half = divmod(u, 2)
                    dve.wait_ge(s_dn, 16 * i + u + 1)
                    dst = h2[:, t, half * 512:(half + 1) * 512]
                    dve.tensor_tensor(dst, dst, db[:, u % 4, :], ALU.add).then_inc(s_dnfree, 1)

            hidden(0, U_UP0 + 5, 1)
            low(0, 0)
            hidden(1, U_UP0 + 9)
            low(1, 1)
            with dve.Fori(0, FFN_ITERS - 1) as i:
                hidden(2 * i + 2, U_FFN + 3 + 12 * i)
                add_down(i)
                low(2 * i + 2, 0)
                hidden(2 * i + 3, U_FFN + 9 + 12 * i)
                low(2 * i + 3, 1)
            add_down(FFN_ITERS - 1)
            dve.wait_ge(s_fg, 16)
            for t in range(KT):
                dve.wait_ge(s_fsq, t + 1)
                dve.reciprocal(nss[:, t:t + 1], nss[:, t:t + 1])
                drain()
                dve.scalar_tensor_tensor(fino[:, t % 2, :], h2[:, t, :], nss[:, t:t + 1], fing[:, :],
                                         ALU.mult, ALU.mult).then_inc(s_fin, 1)


def kernel(**inputs):
    import concourse.bacc as bacc
    from concourse.bass_utils import run_bass_kernel_spmd

    names = ["x", "meta_tokens", "norm_mix", "w_in", "conv_qkv", "a_log", "dt_bias", "head_norm", "w_pool",
             "pool_scale", "w_out", "norm_ffn", "w_up", "conv_ffn", "w_down", "norm_final"]
    nc = bacc.Bacc("TRN2", target_bir_lowering=False, num_devices=1)
    arrays = {f"in_{n}": np.ascontiguousarray(inputs[n]) for n in names}
    arrays["in_constants"] = constants()
    args = [nc.dram_tensor(n, a.shape, mybir.dt.from_np(a.dtype), kind="ExternalInput").ap()
            for n, a in arrays.items()]
    args.append(nc.dram_tensor("out_h", (1, SEQ, D), F32, kind="ExternalOutput").ap())
    hybrid_block(nc, *args)
    r = run_bass_kernel_spmd(nc, [arrays], core_ids=[0])
    return r.results[0]["out_h"]
```

```python
from contextlib import ExitStack

import numpy as np

import concourse.bass as bass
from concourse import mybir

F32 = mybir.dt.float32
F32R = mybir.dt.float32r
ACT = mybir.ActivationFunctionType
ALU = mybir.AluOpType
AX_X = mybir.AxisListType.X

P = 128
D = 1024
SEQ = 1024
META = 16
KT = D // P
T = META + SEQ
HEADS = 8
CH = 128
NCH = -(-T // CH)
PAD = NCH * CH - T
TP = NCH * CH
HALO = 2
TO = SEQ + HALO
OFF = META - HALO
QKV_TILES = 3 * HEADS
DFF = 2816
FT = DFF // P
EPS = 1e-6
NEG = -1e30
WINDOWS = (2, 4, 8, 16)
GROUPS = (3, 2, 1, 0)
Z_COL = QKV_TILES * P
AB_COL = Z_COL + D
POOL_COL = AB_COL + 2 * HEADS
GA_COL = POOL_COL + 4 * P
GB_COL = GA_COL + D

BLOCKS = [(0, 346), (346, 346), (692, T - 692)]
OBLOCKS = [(i * (TO // 3), TO // 3) for i in range(3)]

SUB = 16
BLKS = CH // SUB
LEVELS = [16, 32, 64]

C_ID, C_CUM, C_NEG = 0, P, 2 * P
C_LV = 3 * P
C_INV = C_LV + len(LEVELS) * P
C_ALL = C_INV + 4 * 16

W_AB = 0
W_QKV = 1
W_POOL = W_QKV + QKV_TILES
W_WPOOL = W_POOL + 4
W_ZG = W_WPOOL + 1
W_OUT = W_ZG + 3 * HEADS
W_UP0 = W_OUT + KT
W_FFN = W_UP0 + 4
FFN_ITERS = FT // 2
W_LAST = W_FFN + 6 * (FFN_ITERS - 1)
SLOTS = 3
OUT_SLOTS = 4

U_QKV = 3
U_POOL = U_QKV + 3 * QKV_TILES
U_WPOOL = U_POOL + 12
U_ZG = U_WPOOL + 24
U_OUT = U_ZG + 6 * HEADS
U_UP0 = U_OUT + 24
U_FFN = U_UP0 + 12

FQ, FQD, FK, FKB, FKG, FKD, FV, EGT, GCUM = range(9)

R_CONV, R_PSC, R_HN, R_CF = 0, 96, 104, 105


def constants():
    c = np.zeros((P, C_ALL), np.float32)
    r = np.arange(P)
    c[:, C_ID:C_ID + P] = np.eye(P)
    c[:, C_CUM:C_CUM + P] = r[:, None] <= r[None, :]
    c[:, C_NEG:C_NEG + P] = np.where(r[:, None] > r[None, :], -NEG, 0.0)

    def level(z):
        return ((r[:, None] // z % 2 == 1) & (r[None, :] // z == r[:, None] // z - 1)).astype(np.float32)

    for n, z in enumerate(LEVELS):
        c[:, C_LV + n * P:C_LV + (n + 1) * P] = level(z)
    for g, w in enumerate(WINDOWS):
        c[:, C_INV + g * 16:C_INV + g * 16 + w] = np.float32(w) / np.arange(1, w + 1, dtype=np.float32)
        c[:, C_INV + g * 16 + w:C_INV + (g + 1) * 16] = 1.0
    return c


REC = ["P1", "V", "O", "SU", "OT"]
STEPS = ["P1", "TKN", "V", "TKB", "GROW", "KK", "TQ", "TKG", "O", "SU", "QK", "TQD", "OT", "TT0"]
DOUBLING = ["TT0"]
for _n in range(len(LEVELS)):
    DOUBLING += [f"X{_n}", f"Y{_n}"] + ([f"T{_n}"] if _n < len(LEVELS) - 1 else [])
STEPS += DOUBLING[1:]
LAST_Y = DOUBLING[-1]
PREP_STEPS = [s for s in STEPS if s not in REC and s not in DOUBLING]
FORM = {"TKN": ("kn", 0), "TKB": ("kb", 1), "TQ": ("qn", 0), "TKG": ("kg", 1), "TQD": ("qd", 0)}
PIECES = [(0, 3), (3, 6), (6, 8)]
FEATURE_HALVES = slice(0, KT // 2), slice(KT // 2, KT)
FILLS = {"P1": 2, "TKN": 0, "V": 1, "TKB": 0, "GROW": 3, "KK": 2, "TQ": 2, "TKG": 2, "O": 2, "SU": 2, "QK": 1,
         "TQD": 1, "OT": 2, "TT0": 1, "X0": 1, "Y0": 1, "T0": 1, "X1": 0, "Y1": 1, "T1": 1, "X2": 0, "Y2": 1}
assert sum(FILLS.values()) == 9 * len(PIECES) and FILLS["P1"] < len(PIECES)


FIRST_PLAN = ["TKN", ("pool", 0), "TKB", ("pool", 1), "GROW", ("pool", 2), ("pool", 3), "KK", ("pool", 4), "TQ",
              ("pool", 5), ("pool", 6), ("pool", 7), "TKG", "QK", "TQD"]
assert [s for s in FIRST_PLAN if isinstance(s, str)] == PREP_STEPS

OUT_PLAN = [("unit", n, b) for b in range(3) for n in range(3)]
OUT_PLAN += [("unit", n, b) for n in (3, 4) for b in range(3)]
OUT_PLAN += [("unit", n, 0) for n in (5, 6, 7)]
OUT_PLAN += [("unit", 5, 1), ("back", 0), ("unit", 6, 1), ("forth", 0), ("back", 1)]
for _j, _unit in enumerate([("unit", 7, 1), ("unit", 5, 2), ("unit", 6, 2), ("unit", 7, 2), ("up", 0, 0),
                            ("up", 1, 0), ("up", 0, 1)]):
    OUT_PLAN += [_unit, ("forth", _j + 1), ("back", _j + 2)]
OUT_PLAN += [("up", 1, 1), ("forth", KT), ("up", 0, 2), ("up", 1, 2)]
OUT_UNITS = [s[1:] for s in OUT_PLAN if s[0] == "unit"]
assert sorted(OUT_UNITS) == [(n, b) for n in range(KT) for b in range(3)]
BACK_UNITS = [18, 18, 18, 21, 21, 21, 24, 24, 24]
for _j in range(KT + 1):
    _cols = HALO if _j == 0 else HALO + _j * P
    assert BACK_UNITS[_j] > max(OUT_UNITS.index((n, b)) for n in range(KT) for b in range(3)
                                if OBLOCKS[b][0] < _cols)


NORMED = [-(-(o + w - HALO) // P) + 1 for o, w in OBLOCKS]


def pieces_after(name):
    first = sum(FILLS[s] for s in STEPS[:STEPS.index(name)])
    return range(first, first + FILLS[name])


def units_after(name):
    return [p // len(PIECES) for p in pieces_after(name) if p % len(PIECES) == len(PIECES) - 1]


def hybrid_block(nc, x, meta_tokens, norm_mix, w_in, conv_qkv, a_log, dt_bias, head_norm, w_pool,
                 pool_scale, w_out, norm_ffn, w_up, conv_ffn, w_down, norm_final, consts, out):
    with ExitStack() as ctx:
        def sem(name):
            return ctx.enter_context(nc.semaphore(name))

        base = -(-nc.sbuf_base // 64) * 64
        room = nc.sbuf_usable_end - base
        top = [0]

        def at(name, shape, dt, offset=None):
            size = 4 * int(np.prod(shape[1:]))
            size += -size % 32
            if offset is None:
                offset = top[0]
                top[0] += size
            assert offset + size <= room, (name, offset + size, room)
            return nc.alloc_sbuf_tensor_at(name, shape, dt, offset=base + offset)

        u_hi = at("u_hi", [P, KT, T], F32R)
        u_lo = at("u_lo", [P, KT, T], F32R)
        w_raw = at("w_raw", [P, SLOTS, D], F32)
        w_hi = at("w_hi", [P, SLOTS, D], F32R)
        w_lo = at("w_lo", [P, SLOTS, D], F32R)
        cst = at("cst", [P, C_ALL], F32)
        prm = at("prm", [P, R_CF + 3 * 2 * FT], F32)
        fac = at("fac", [P, 9, NCH, HEADS], F32)
        ssq = at("ssq", [P, QKV_TILES, NCH], F32)
        tiny = at("tiny", [P, 64], F32)
        eps_t = tiny[:, 0:1]
        nss = tiny[:, 8:24]
        oss = tiny[:, 24:32]
        orr = tiny[:, 32:40]
        hdp = tiny[0:16, 40:44]
        gcur = tiny[:, 48:56]
        region = top[0]
        end = [region]

        def plan(items, start=region):
            made, offset = [], start
            for name, shape, dt in items:
                size = 4 * int(np.prod(shape[1:]))
                made.append(at(name, shape, dt, offset))
                offset += size + (-size % 32)
            end[0] = offset
            return made

        xt, xs, gmix, prow = plan([
            ("xt", [P, 3, D], F32), ("xs", [P, 2, D], F32), ("gmix", [P, D], F32), ("prow", [P, 3, P], F32)])
        xb, cacc, sl, tm, sq = plan([
            ("xb", [P, 3, 3 + T + 1], F32), ("cacc", [P, T], F32), ("sl", [P, TP], F32),
            ("tm", [P, NCH, P], F32), ("sq", [P, NCH, P], F32)])
        px, pa, pb, ab_beta, ab_g, ab_t, gtok, gtmp, p_hi, p_lo, ybs = plan([
            ("px", [P, 16 + T], F32), ("pa", [P, 16 + T], F32), ("pb", [P, 16 + T], F32),
            ("ab_beta", [16, TP], F32), ("ab_g", [16, TP], F32), ("ab_t", [16, TP], F32),
            ("gtok", [P, NCH * HEADS], F32), ("gtmp", [P, 3, NCH * HEADS], F32),
            ("p_hi", [P, 4, T], F32R), ("p_lo", [P, 4, T], F32R), ("ybs", [P, 2, TO], F32)],
            end[0])
        names = ["knt", "qnt", "kbt", "nmx", "ex", "at_m", "bd"]
        live = ["qdt", "kgt", "kd", "vb", "qkm", "rr", "vv", "st", "ots"]
        (tk, form, knt, qnt, kbt, nmx, ex, at_m, bd, blk, sol, upd, zs, gs, yl, qdt, kgt, kd, vb, qkm, rr, vv,
         st, ots) = plan(
            [("tk", [P, QKV_TILES, P], F32), ("form", [P, 2, HEADS, P], F32)]
            + [(n, [P, HEADS, P], F32) for n in names]
            + [("blk", [BLKS * HEADS, SUB * SUB], F32), ("sol", [BLKS * HEADS, SUB * SUB], F32),
               ("upd", [BLKS * HEADS, SUB * SUB // 4], F32),
               ("zs", [P, TO], F32), ("gs", [P, TO], F32), ("yl", [P, TO], F32)]
            + [(n, [P, HEADS, P], F32) for n in live])
        orx = vb
        tt_m = kbt
        bw = OBLOCKS[0][1]
        yz0, yo0, yg0, yz1, yg1, yo1, ht = plan(
            [(n, [P, KT, bw], F32) for n in ("yz0", "yo0", "yg0", "yz1", "yg1", "yo1")]
            + [("ht", [P, KT, TO], F32)])
        yz, yg, yo = (yz0, yz1), (yg0, yg1), (yo0, yo1)
        h2, h2m = plan([("h2", [P, KT, D], F32), ("h2m", [HALO, D], F32)])
        after_h2 = end[0]
        xg, xv, cg, cv, sg = plan([
            ("xg", [P, TO], F32), ("xv", [P, TO], F32), ("cg", [P, SEQ], F32), ("cv", [P, SEQ], F32),
            ("sg", [P, SEQ], F32)], after_h2)
        gffn = sg
        mlp_end = end[0]
        (hx,) = plan([("hx", [P, 2, D], F32)], mlp_end)
        a_hi, a_lo, fing, fino = plan([
            ("a_hi", [P, 2, SEQ], F32R), ("a_lo", [P, 2, SEQ], F32R), ("fing", [P, D], F32),
            ("fino", [P, OUT_SLOTS, D], F32)], mlp_end)

        gb = ctx.enter_context(nc.psum_tensor("gb", [P, 3, 512], F32))
        db = ctx.enter_context(nc.psum_tensor("db", [P, 4, 512], F32))
        mb = ctx.enter_context(nc.psum_tensor("mb", [P, 512], F32))

        qkv_d = nc.dram_tensor("qkv_d", [NCH * P, QKV_TILES * P], F32, kind="Internal").ap()
        yb_d = nc.dram_tensor("yb_d", [D, TO], F32, kind="Internal").ap()
        za_d = nc.dram_tensor("za_d", [D, TO], F32, kind="Internal").ap()
        yg_d = nc.dram_tensor("yg_d", [D, TO], F32, kind="Internal").ap()
        blk_d = nc.dram_tensor("blk_d", [BLKS * HEADS, SUB * SUB], F32, kind="Internal").ap()
        sol_d = nc.dram_tensor("sol_d", [BLKS * HEADS, SUB * SUB], F32, kind="Internal").ap()
        ot_d = nc.dram_tensor("ot_d", [D, PAD + T], F32, kind="Internal").ap()

        ident = cst[:, C_ID:C_ID + P]

        def lvl(n):
            return cst[:, C_LV + n * P:C_LV + (n + 1) * P]

        def over_heads(m, n=HEADS):
            return m.unsqueeze(1).broadcast_to([P, n, P])

        def per_head(f, n=HEADS):
            return f.unsqueeze(2).broadcast_to([P, n, P])

        def factor(kind, c):
            return fac[:, kind, bass.ds(c, 1), :].rearrange("p o h -> p (o h)")

        def first(n):
            return isinstance(n, int) and n == 0

        s_const = sem("s_const")
        s_zero = sem("s_zero")
        s_prow = sem("s_prow")
        s_hd = sem("s_hd")
        s_prmT = sem("s_prmT")
        s_prm = sem("s_prm")
        s_x = [sem(f"s_x{i}") for i in range(3)]
        s_nsq = sem("s_nsq")
        s_xs = sem("s_xs")
        s_nt = sem("s_nt")
        s_gmix = sem("s_gmix")
        s_uhi = sem("s_uhi")
        s_u = sem("s_u")
        s_w = [sem(f"s_w{i}") for i in range(SLOTS)]
        s_whi = sem("s_whi")
        s_wlo = sem("s_wlo")
        s_g = sem("s_g")
        s_gfree = sem("s_gfree")
        s_z = sem("s_z")
        s_zsig = sem("s_zsig")
        s_zfree = sem("s_zfree")
        s_na = sem("s_na")
        s_ab = sem("s_ab")
        s_abT = sem("s_abT")
        s_gtok = sem("s_gtok")
        s_gcum = sem("s_gcum")
        s_gsb = sem("s_gsb")
        s_exp = sem("s_exp")
        s_conv = sem("s_conv")
        s_sl = sem("s_sl")
        s_tmps = sem("s_tmps")
        s_tm = sem("s_tm")
        s_sq = sem("s_sq")
        s_ssq = sem("s_ssq")
        s_spill = sem("s_spill")
        s_fac = sem("s_fac")
        s_pw = sem("s_pw")
        s_phi = sem("s_phi")
        s_plo = sem("s_plo")
        s_yb = [sem(f"s_yb{i}") for i in range(2)]
        s_tk = sem("s_tk")
        s_form = {f: sem(f"s_form_{f}") for f in ("qn", "kn", "kb", "qd", "kg")}
        s_kd = sem("s_kd")
        s_vb = sem("s_vb")
        s_nm = sem("s_nm")
        s_gcp = sem("s_gcp")
        s_dec = sem("s_dec")
        s_ps = {n: sem(f"s_ps_{n}") for n in STEPS}
        s_ev = {n: sem(f"s_ev_{n}") for n in STEPS}
        s_bst = sem("s_bst")
        s_blk = sem("s_blk")
        s_sol = sem("s_sol")
        s_sst = sem("s_sst")
        s_bd = sem("s_bd")
        s_osq = sem("s_osq")
        s_oss = sem("s_oss")
        s_ort = sem("s_ort")
        s_on = sem("s_on")
        s_ot = sem("s_ot")
        s_za = sem("s_za")
        s_yg = sem("s_yg")
        s_yl = sem("s_yl")
        s_zg = sem("s_zg")
        s_gg = sem("s_gg")
        s_yin = [sem(f"s_yin{i}") for i in range(2)]
        s_ygin = [sem(f"s_ygin{i}") for i in range(2)]
        s_y1 = sem("s_y1")
        s_yhi = sem("s_yhi")
        s_y = sem("s_y")
        s_h2x = [sem(f"s_h2x{i}") for i in range(3)]
        s_h2T = sem("s_h2T")
        s_h2 = sem("s_h2")
        s_h2sq = sem("s_h2sq")
        s_hx = sem("s_hx")
        s_hnt = sem("s_hnt")
        s_gffn = sem("s_gffn")
        s_u2hi = sem("s_u2hi")
        s_u2 = sem("s_u2")
        s_cg = sem("s_cg")
        s_cv = sem("s_cv")
        s_sg = sem("s_sg")
        s_act = sem("s_act")
        s_ahi = sem("s_ahi")
        s_alo = sem("s_alo")
        s_dn = sem("s_dn")
        s_dnfree = sem("s_dnfree")
        s_fg = sem("s_fg")
        s_fsq = sem("s_fsq")
        s_fin = sem("s_fin")
        s_out = [sem(f"s_out{i}") for i in range(OUT_SLOTS)]

        def gain(row, n=KT):
            return prm[:, row:row + n]

        def gflat(kind):
            return fac[:, kind, :, :].rearrange("p c h -> p (c h)")

        def pool_out(g):
            return (pb, pa)[g % 2]

        def heads(m, h):
            return m[:, h * HEADS // 2:(h + 1) * HEADS // 2, :]

        def dbank(name, h):
            return db[:, 2 * (STEPS.index(name) % 2) + h, :].rearrange("p (m c) -> p m c", m=HEADS // 2)

        def tbank(b, n):
            return db[:, b, :].rearrange("p (k c) -> p k c", k=4)[:, :, 0:n]

        block = ctx.enter_context(nc.Block())

        @block.sync
        def _(sp):
            def load_w(n, src, i=0, per=3, wide=False):
                if n >= SLOTS:
                    sp.wait_ge(s_wlo, n - SLOTS + 1 + per * i)
                dst = w_raw[:, n % SLOTS, :]
                if not wide:
                    dst = dst.rearrange("p (k c) -> p k c", k=KT)
                sp.dma_start(dst, src).then_inc(s_w[n % SLOTS], 16)

            def cols(w, c0):
                return w[0, :, bass.ds(c0, P)].rearrange("(k p) c -> p k c", p=P)

            sp.dma_start(xt[0:META, 0, :], meta_tokens).then_inc(s_x[0], 16)
            sp.dma_start(gmix[0:META, :], norm_mix.broadcast_to([META, D])).then_inc(s_gmix, 16)
            sp.dma_start(cst[:, :], consts).then_inc(s_const, 16)
            sp.dma_start(xt[:, 1, :], x[0, 0:P, :]).then_inc(s_x[1], 16)
            sp.dma_start(gmix[META:, :], norm_mix.broadcast_to([P - META, D])).then_inc(s_gmix, 16)
            sp.dma_start(xt[:, 2, :], x[0, P:2 * P, :]).then_inc(s_x[2], 16)
            load_w(W_AB, cols(w_in, AB_COL))
            for j in range(3, KT + 1):
                sp.wait_ge(s_xs, j - 2)
                sp.dma_start(xt[:, j % 3, :], x[0, (j - 1) * P:j * P, :]).then_inc(s_x[j % 3], 16)
            for j in range(2):
                load_w(W_QKV + j, cols(w_in, j * P))
            with sp.Fori(0, QKV_TILES // 3 - 1) as i:
                for j in range(3):
                    load_w(W_QKV + 2 + j, cols(w_in, (2 + j) * P + 3 * P * i), i)
            load_w(W_QKV + QKV_TILES - 1, cols(w_in, (QKV_TILES - 1) * P))
            for q, g in enumerate(GROUPS):
                load_w(W_POOL + q, cols(w_in, POOL_COL + g * P))
            sp.wait_ge(s_wlo, W_WPOOL - SLOTS + 1)
            sp.dma_start(w_raw[:, W_WPOOL % SLOTS, :].rearrange("p (g d) -> p g d", g=4),
                         w_pool[0].rearrange("g p d -> p g d")).then_inc(s_w[W_WPOOL % SLOTS], 16)

            def load_tk(c):
                sp.dma_start(tk[:, :, :].rearrange("p t d -> p (t d)"),
                             qkv_d[bass.ds(c * P, P), :]).then_inc(s_tk, 16)

            def invert(c, n=BLKS):
                def block(b, m):
                    return m[SUB * b:SUB * (b + 1), :, SUB * b:SUB * (b + 1)]

                def rows(m, b):
                    return m[HEADS * b:HEADS * (b + 1), :].rearrange("h (r c) -> r h c", r=SUB)

                stored = 16 * c * BLKS if n < BLKS else 16 + 16 * BLKS * (c - 1)
                sp.wait_ge(s_ev["KK"], 2 * c + 2)
                for b in range(n):
                    sp.dma_start(rows(blk_d, b), block(BLKS - n + b, at_m)).then_inc(s_bst, 16)
                sp.wait_ge(s_bst, stored + 16 * n)
                sp.dma_start(blk[0:HEADS * n, :], blk_d[0:HEADS * n, :]).then_inc(s_blk, 16)
                sp.wait_ge(s_sol, c + 1)
                sp.dma_start(sol_d[0:HEADS * n, :], sol[0:HEADS * n, :]).then_inc(s_sst, 16)
                sp.wait_ge(s_sst, 16 * c + 16)
                if n < BLKS:
                    sp.wait_ge(s_zero, 4)
                for b in range(n):
                    sp.dma_start(block(BLKS - n + b, bd), rows(sol_d, b)).then_inc(s_bd, 16)

            for j, c0 in enumerate((Z_COL, GA_COL, GB_COL)):
                load_w(W_ZG + j, cols(w_in, c0))
            sp.wait_ge(s_spill, 16 * QKV_TILES)
            sp.wait_ge(s_conv, QKV_TILES)
            load_tk(0)
            invert(0, 1)
            sp.wait_ge(s_gfree, U_ZG)
            sp.wait_ge(s_yb[0], 16 * 4)
            sp.wait_ge(s_yb[1], 16 * 4)
            sp.dma_start(yl[:, :], yb_d[0:P, :]).then_inc(s_yl, 16)
            sp.wait_ge(s_form["qd"], 1)
            sp.wait_ge(s_vb, 1)
            load_tk(1)
            with sp.Fori(0, HEADS - 1) as i:
                for j, c0 in enumerate((Z_COL, GA_COL, GB_COL)):
                    load_w(W_ZG + 3 + j, cols(w_in, c0 + P + P * i), i)
                invert(i + 1)
                sp.wait_ge(s_form["qd"], i + 2)
                sp.wait_ge(s_vb, i + 2)
                load_tk(i + 2)
                sp.wait_ge(s_gg, i + 1)
                sp.dma_start(yl[:, :], yb_d[bass.ds(P + P * i, P), :]).then_inc(s_yl, 16)
            for n in range(3):
                load_w(W_OUT + n, cols(w_out, n * P))
            invert(NCH - 1)

            def load_y(b, src, dst):
                o, w = OBLOCKS[b]
                sp.dma_start(dst[b % 2][:, :, :], src[:, o:o + w].rearrange("(k p) t -> p k t", p=P)
                             ).then_inc((s_ygin if dst is yg else s_yin)[b % 2], 16)

            ot_from = ot_d[:, PAD + OFF:]
            sp.wait_ge(s_za, 16 * HEADS)
            sp.wait_ge(s_form["qd"], NCH)
            sp.wait_ge(s_vb, NCH)
            load_y(0, za_d, yz)
            sp.wait_ge(s_ev["QK"], 2 * NCH)
            sp.wait_ge(s_ps["TQD"], 2 * NCH)
            sp.wait_ge(s_ot, 16 * (NCH - 1))
            load_y(0, ot_from, yo)
            sp.wait_ge(s_yg, 16 * (HEADS + 1))
            sp.wait_ge(s_ps[LAST_Y], 2 * (NCH - 1))
            load_y(0, yg_d, yg)
            load_y(1, za_d, yz)
            load_y(1, yg_d, yg)
            sp.wait_ge(s_ps["O"], 2 * NCH)
            load_y(1, ot_from, yo)
            load_w(W_OUT + 3, cols(w_out, 3 * P))
            sp.wait_ge(s_y, 2)
            load_y(2, za_d, yz)
            load_y(2, yg_d, yg)
            sp.wait_ge(s_ot, 16 * NCH)
            load_y(2, ot_from, yo)
            for n in (4, 5):
                load_w(W_OUT + n, cols(w_out, n * P))
            sp.wait_ge(s_y, 6)
            sp.dma_start(gffn[:, :], norm_ffn.broadcast_to([P, D])).then_inc(s_gffn, 16)
            sp.dma_start(h2m[:, :], meta_tokens[OFF:META, :]).then_inc(s_h2x[0], 16)
            for g, (t0, t1) in enumerate(((0, 2), (2, 5), (5, KT))):
                sp.dma_start(h2[:, t0:t1, :], x[0, t0 * P:t1 * P, :].rearrange("(t p) d -> p t d", p=P)
                             ).then_inc(s_h2x[g], 16)
                if g < 2:
                    load_w(W_OUT + 6 + g, cols(w_out, (6 + g) * P))

            def up_cols(j):
                return (j % 2) * DFF + (j // 2) * P

            for j in range(4):
                load_w(W_UP0 + j, cols(w_up, up_cols(j)))
            with sp.Fori(0, FFN_ITERS - 1) as i:
                for j in range(6):
                    if j in (2, 3):
                        load_w(W_FFN + j, w_down[0, bass.ds(2 * P * i + (j - 2) * P, P), :], i, 6, wide=True)
                    else:
                        jj = j if j < 2 else j - 2
                        load_w(W_FFN + j, cols(w_up, up_cols(jj) + 2 * P + 2 * P * i), i, 6)
            for k in range(2):
                load_w(W_LAST + k, w_down[0, (FT - 2 + k) * P:(FT - 1 + k) * P, :], wide=True)
            sp.dma_start(fing[:, :], norm_final.rearrange("(o d) -> o d", o=1).broadcast_to([P, D])
                         ).then_inc(s_fg, 16)
            for t in range(KT):
                sp.wait_ge(s_fin, t + 1)
                sp.dma_start(out[0, t * P:(t + 1) * P, :], fino[:, t % OUT_SLOTS, :]
                             ).then_inc(s_out[t % OUT_SLOTS], 16)
            for slot in range(OUT_SLOTS):
                sp.wait_ge(s_out[slot], 16 * KT // OUT_SLOTS)

        @block.gpsimd
        def _(pool):
            pool.memset(tiny[:, :], 0.0)
            pool.drain()
            pool.memset(eps_t, EPS).then_inc(s_zero, 1)
            pool.memset(prow[:, :, :], 0.0)
            pool.memset(ab_beta[:, :], 0.0)
            pool.memset(ab_g[:, :], 0.0).then_inc(s_zero, 1)
            pool.wait_ge(s_zero, 2)
            with nc.allow_non_contiguous_dma(reason="sixteen words"):
                pool.dma_start(hdp[8:16, 0:1], dt_bias.rearrange("o h -> h o")).then_inc(s_hd, 16)
                pool.dma_start(hdp[8:16, 1:2], a_log.rearrange("o h -> h o")).then_inc(s_hd, 16)

            def rows(v):
                return v.rearrange("o (i p) -> (o i) p", p=P)

            cf = conv_ffn.rearrange("o j (i p) -> (o j i) p", p=P)
            for dst, src in ((prow[0:R_PSC, 0, :], conv_qkv.rearrange("o j (i p) -> (o j i) p", p=P)),
                             (prow[R_PSC:R_PSC + 8, 0, :], rows(pool_scale)),
                             (prow[R_HN:R_HN + 1, 0, :], head_norm),
                             (prow[0:88, 1, :], cf[0:88, :]), (prow[0:44, 2, :], cf[88:132, :])):
                pool.dma_start(dst, src).then_inc(s_prow, 16)

            def w_low(n, i=0, per=3):
                pool.wait_ge(s_whi, n + 1 + per * i)
                pool.tensor_tensor(w_lo[:, n % SLOTS, :], w_raw[:, n % SLOTS, :],
                                   w_hi[:, n % SLOTS, :].bitcast(F32), ALU.subtract).then_inc(s_wlo, 1)

            w_low(W_AB)
            w_low(W_QKV)
            w_low(W_QKV + 1)
            pool.wait_ge(s_u, 2 * (KT + 1))
            pool.memset(xb[:, :, 0:3], 0.0)
            pool.memset(sl[:, 0:PAD], 0.0)
            pool.memset(px[:, 0:16], 0.0)
            pool.memset(pa[:, 0:16], 0.0)
            pool.memset(pb[:, 0:16], 0.0).then_inc(s_zero, 1)

            def squares(j, i=0):
                w_low(W_QKV + 2 + j, i)
                pool.wait_ge(s_tm, 3 * i + j + 1)
                if j > 0:
                    pool.wait_ge(s_ssq, 3 * i + j)
                pool.tensor_tensor(sq[:, :, :], tm[:, :, :], tm[:, :, :], ALU.mult).then_inc(s_sq, 1)

            for j in range(3):
                squares(j)
            with pool.Fori(0, QKV_TILES // 3 - 1) as i:
                for j in range(3, 6):
                    squares(j, i)
            for n in range(W_QKV + QKV_TILES + 2, W_ZG):
                w_low(n)

            def mask(c):
                pool.tensor_tensor(nmx[:, :, :], per_head(factor(GCUM, c)),
                                   over_heads(cst[:, C_NEG:C_NEG + P]), ALU.add).then_inc(s_nm, 1)

            def state_parts(c):
                pool.tensor_tensor(kd[:, :, :], tk[:, HEADS:2 * HEADS, :], per_head(factor(FKD, c)),
                                   ALU.mult).then_inc(s_kd, 1)
                pool.tensor_tensor(vb[:, :, :], tk[:, 2 * HEADS:, :], per_head(factor(FV, c)),
                                   ALU.mult).then_inc(s_vb, 1)

            def substitute(c, n=BLKS):
                n *= HEADS
                low = blk[0:n, :].rearrange("p (r c) -> p r c", c=SUB)
                inv = sol[0:n, :].rearrange("p (r c) -> p r c", c=SUB)
                pool.memset(sol[0:n, :], 0.0)
                pool.drain()
                pool.memset(sol[0:n, ::SUB + 1], 1.0)
                pool.drain()
                pool.wait_ge(s_blk, 16 * c + 16)
                for j in range(SUB - 1):
                    rest = SUB - 1 - j
                    out = upd[0:n, 0:rest * (j + 1)].rearrange("p (r c) -> p r c", c=j + 1)
                    pool.tensor_tensor(out, low[:, j, j + 1:].unsqueeze(2).broadcast_to([n, rest, j + 1]),
                                       inv[:, j, 0:j + 1].unsqueeze(1).broadcast_to([n, rest, j + 1]), ALU.mult)
                    pool.drain()
                    t = pool.tensor_tensor(inv[:, j + 1:, 0:j + 1], inv[:, j + 1:, 0:j + 1], out, ALU.subtract)
                    if j < SUB - 2:
                        pool.drain()
                t.then_inc(s_sol, 1)

            pool.wait_ge(s_plo, 4)
            mask(0)
            pool.memset(bd[:, :, :], 0.0).then_inc(s_zero, 1)
            w_low(W_ZG)
            w_low(W_ZG + 1)
            substitute(0, 1)
            w_low(W_ZG + 2)
            pool.wait_ge(s_gfree, U_ZG)
            pool.wait_ge(s_yb[0], 16 * 4)
            pool.wait_ge(s_yb[1], 16 * 4)
            pool.memset(gs[:, 0:1], 0.0).then_inc(s_yg, 16)
            pool.wait_ge(s_tk, 16)
            state_parts(0)
            for h in range(2):
                pool.memset(heads(st, h), 0.0).then_inc(s_ev["SU"], 1)
            with pool.Fori(0, HEADS) as i:
                pool.wait_ge(s_ev[LAST_Y], 2 * i + 2)
                mask(i + 1)
                substitute(i + 1)
                pool.wait_ge(s_ps["SU"], 2 * i + 2)
                pool.wait_ge(s_ps["OT"], 2 * i + 2)
                pool.wait_ge(s_tk, 16 * i + 32)
                state_parts(i + 1)
                for j in range(3):
                    w_low(W_ZG + 3 + j, i)
            for n in range(3, KT):
                w_low(W_OUT + n)
            for j in range(4):
                w_low(W_UP0 + j)
            with pool.Fori(0, FFN_ITERS - 1) as i:
                for j in range(6):
                    w_low(W_FFN + j, i, 6)
            w_low(W_LAST)
            w_low(W_LAST + 1)

        @block.tensor
        def _(pe):
            def w_ready(n, i=0, per=3):
                pe.wait_ge(s_wlo, n + 1 + per * i)

            def unit(n, bank, o, w, k0=0, k1=KT):
                for k in range(k0, k1):
                    w1, w2 = (v[:, n % SLOTS, k * P:(k + 1) * P] for v in (w_hi, w_lo))
                    u1, u2 = (v[:, k, o:o + w] for v in (u_hi, u_lo))
                    for m, (wt, u) in enumerate(((w1, u1), (w1, u2), (w2, u1))):
                        mm = pe.matmul(gb[:, bank, 0:w], wt, u, start=(k == 0 and m == 0),
                                       stop=(k == KT - 1 and m == 2))
                return mm

            pe.wait_ge(s_const, 16)
            for j in range(KT + 1):
                pe.wait_ge(s_xs, j + 1)
                n = META if j == 0 else P
                for h in range(2):
                    if j >= 2:
                        pe.wait_ge(s_u, 2 * (j - 2) + h + 1)
                    for k in range(4 * h, 4 * h + 4):
                        t = pe.transpose(db[:, 2 * (j % 2) + h, k % 4 * P:k % 4 * P + n],
                                         xs[0:n, j % 2, k * P:(k + 1) * P], cst[0:n, C_ID:C_ID + n])
                    t.then_inc(s_nt, 1)
            pe.wait_ge(s_prow, 16 * 5)
            for r, n in enumerate((R_CF, 88, 44)):
                t = pe.transpose(mb[:, r * P:r * P + n], prow[0:n, r, :], cst[0:n, C_ID:C_ID + n])
            t.then_inc(s_prmT, 1)

            pe.wait_ge(s_u, 2 * (KT + 1))
            w_ready(W_AB)
            for b, (o, w) in enumerate(BLOCKS):
                unit(W_AB, b, o, w).then_inc(s_g, 1)

            def project(n, before, i=0):
                w_ready(n, i)
                for b, (o, w) in enumerate(BLOCKS):
                    pe.wait_ge(s_gfree, before + b - 2 + 3 * 3 * i)
                    unit(n, b, o, w).then_inc(s_g, 1)

            def turn(n, first=False):
                pe.wait_ge(s_sl, n + 1)
                if not first:
                    pe.wait_ge(s_tm, n)
                for r, (c0, c1) in enumerate(((0, 4), (4, 8), (8, NCH))):
                    for c in range(c0, c1):
                        t = pe.transpose(db[:, r, (c - c0) * P:(c - c0 + 1) * P], sl[:, c * P:(c + 1) * P], ident)
                    t.then_inc(s_tmps, 1)

            for n in range(3):
                project(W_QKV + n, U_QKV + 3 * n)
                if n:
                    turn(n - 1, n == 1)
            with pe.Fori(0, QKV_TILES // 3 - 1) as i:
                for j in range(3, 6):
                    project(W_QKV + j, U_QKV + 3 * j, i)
                    turn(3 * i + j - 1)
            for g in range(4):
                project(W_POOL + g, U_POOL + 3 * g)
                if g == 0:
                    turn(QKV_TILES - 1)
                    pe.wait_ge(s_ab, 1)
                    pe.wait_ge(s_prm, 3)
                    for c in range(NCH):
                        for m, src in enumerate((ab_beta, ab_g)):
                            t = pe.transpose(mb[:, (m * NCH + c) * 16:(m * NCH + c + 1) * 16],
                                             src[:, c * P:(c + 1) * P], cst[0:16, C_ID:C_ID + 16])
                    t.then_inc(s_abT, 1)
                elif g == 1:
                    pe.wait_ge(s_gtok, 1)
                    pe.matmul(mb[:, 288:288 + NCH * HEADS], cst[:, C_CUM:C_CUM + P], gtok[:, :], start=True, stop=True)
                    pe.matmul(mb[:, 360:360 + NCH * HEADS], cst[:, C_CUM + P - 1:C_CUM + P].broadcast_to([P, P]),
                              gtok[:, :], start=True, stop=True).then_inc(s_gcum, 1)

            def project_pool(q):
                g, j = GROUPS[q // 2], q
                w_ready(W_WPOOL)
                pe.wait_ge(s_plo, q // 2 + 1)
                ws = slice(g * 2 * P + (j % 2) * P, g * 2 * P + (j % 2 + 1) * P)
                w1, w2 = (v[:, W_WPOOL % SLOTS, ws] for v in (w_hi, w_lo))
                for b, (o, w) in enumerate(OBLOCKS):
                    pe.wait_ge(s_gfree, U_WPOOL - 3 + 3 * j + b + 1)
                    u1, u2 = (v[:, g, OFF + o:OFF + o + w] for v in (p_hi, p_lo))
                    for m, (wt, u) in enumerate(((w1, u1), (w1, u2), (w2, u1))):
                        mm = pe.matmul(gb[:, b, 0:w], wt, u, start=(m == 0), stop=(m == 2))
                    mm.then_inc(s_g, 1)

            def step(name, c, freed):
                bank = 2 * (STEPS.index(name) % 2)

                def each(inputs, op):
                    for h in range(2):
                        if freed:
                            pe.wait_ge(s_ev[freed[0]], freed[1] + h + 1)
                        for s, v in inputs:
                            pe.wait_ge(s, v + h + 1)
                        for m in range(4):
                            t = op(db[:, bank + h, m * P:(m + 1) * P], 4 * h + m)
                        t.then_inc(s_ps[name], 1)

                def turned(src):
                    return lambda o, m: pe.transpose(o, src[:, m, :], ident)

                def product(a, b):
                    return lambda o, m: pe.matmul(o, a[:, m, :], b[:, m, :], start=True, stop=True)

                done = {n: (s_ev[n], 2 * (c - 1) if n in DOUBLING and n != LAST_Y else 2 * c) for n in STEPS}
                if name in FORM:
                    f, n = FORM[name]
                    pe.wait_ge(s_form[f], c + 1)
                    each([], turned(form[:, n]))
                elif name == "GROW":
                    pe.wait_ge(s_gcp, c + 1)
                    each([], lambda o, m: pe.transpose(o, gcur[:, m:m + 1].broadcast_to([P, P]), ident))
                elif name == "KK":
                    each([done["TKN"], done["TKB"]], product(knt, kbt))
                elif name == "QK":
                    each([done["TQ"]], product(knt, qnt))
                elif name == "TT0":
                    pe.wait_ge(s_bd, 16 + 16 * BLKS * c)
                    each([], turned(bd))
                elif name[0] == "X":
                    each([done["KK" if name == "X0" else f"T{int(name[1]) - 1}"]],
                         product(at_m, bd if name == "X0" else tt_m))
                elif name == "Y0":
                    each([done["X0"], done["TT0"]], product(nmx, rr))
                elif name[0] == "Y":
                    each([done["X" + name[1]]], product(nmx, rr))
                elif name[0] == "T":
                    each([done["Y" + name[1]]], turned(rr))
                elif name == "P1":
                    pe.wait_ge(s_ev["SU"], 2 * c + 2)
                    each([done["TKG"]], product(kgt, st))
                elif name == "V":
                    each([done["P1"], done[LAST_Y]], product(rr, orx))
                elif name == "O":
                    def both(o, m):
                        pe.matmul(o, qdt[:, m, :], st[:, m, :], start=True, stop=False)
                        return pe.matmul(o, qkm[:, m, :], vv[:, m, :], start=False, stop=True)
                    each([done["V"], done["QK"], done["TQD"]], both)
                elif name == "SU":
                    pe.wait_ge(s_kd, c + 1)
                    each([done["V"]], product(kd, vv))
                elif name == "OT":
                    pe.wait_ge(s_on, c + 1)
                    each([], turned(orx))

            def same_banks(name, among):
                return [n for n in among if STEPS.index(n) % 2 == STEPS.index(name) % 2]

            pe.wait_ge(s_tm, QKV_TILES)
            for name in FIRST_PLAN:
                if name[0] == "pool":
                    project_pool(name[1])
                else:
                    held = same_banks(name, PREP_STEPS[:PREP_STEPS.index(name)])
                    step(name, 0, (held[-1], 0) if held else None)
            step("TT0", 0, (same_banks("TT0", PREP_STEPS)[-1], 0))
            pe.wait_ge(s_ev["QK"], 2)

            def piece(p, i):
                u, part = divmod(p, 3)
                t, b = divmod(u, 3)
                o, w = OBLOCKS[b]
                if part == 0:
                    if b == 0:
                        w_ready(W_ZG + t, i)
                    if t == 1:
                        pe.wait_ge(s_zfree, 3 * i + b + 1)
                    else:
                        pe.wait_ge(s_gfree, U_ZG - 3 + b + 1 + 6 * i + (3 if t == 2 else 0))
                mm = unit(W_ZG + t, b, OFF + o, w, *PIECES[part])
                if part == 2:
                    mm.then_inc(s_z if t == 0 else s_g, 1)

            with pe.Fori(0, HEADS) as i:
                for k, name in enumerate(STEPS):
                    held = same_banks(name, STEPS[:k])
                    c = i if name in REC else i + 1
                    if not held:
                        freed = (LAST_Y, 2 * i)
                    elif held[-1] in REC:
                        freed = (held[-1], 2 * i + 2 if held[-1] == "SU" else 2 * i)
                    else:
                        freed = (held[-1], 2 * i if held[-1] in DOUBLING else 2 * i + 2)
                    step(name, c, freed)
                    for p in pieces_after(name):
                        piece(p, i)
            for name, prev in (("P1", LAST_Y), ("V", "P1"), ("O", "V"), ("OT", "O")):
                step(name, NCH - 1, (prev, 2 * (NCH - 1)))

            def back(j):
                n, c0 = (HALO, 0) if j == 0 else (P, HALO + (j - 1) * P)
                for h in range(2):
                    if j >= 1:
                        pe.wait_ge(s_h2, 2 * (j - 1) + h + 1)
                    for k in range(4):
                        t = pe.transpose(db[0:n, h, k * P:(k + 1) * P], ht[:, 4 * h + k, c0:c0 + n], ident)
                    t.then_inc(s_h2T, 1)

            def forth(j):
                n = HALO if j == 0 else P
                pe.wait_ge(s_hx, j + 1)
                for h in range(2):
                    if j >= 1:
                        pe.wait_ge(s_u2, 2 * (j - 1) + h + 1)
                    for k in range(4 * h, 4 * h + 4):
                        t = pe.transpose(db[:, 2 + h, k % 4 * P:k % 4 * P + n], hx[0:n, j % 2, k * P:(k + 1) * P],
                                         cst[0:n, C_ID:C_ID + n])
                    t.then_inc(s_hnt, 1)

            q = 0
            for kind, *tile in OUT_PLAN:
                if kind == "unit":
                    n, b = tile
                    o, w = OBLOCKS[b]
                    w_ready(W_OUT + n)
                    pe.wait_ge(s_gfree, U_OUT - 3 + q + 1)
                    for hf in range(2):
                        if n == 0:
                            pe.wait_ge(s_y, 2 * b + hf + 1)
                        mm = unit(W_OUT + n, q % 3, o, w, 4 * hf, 4 * hf + 4)
                    mm.then_inc(s_g, 1)
                    q += 1
                elif kind == "up":
                    n, b = tile
                    o, w = OBLOCKS[b]
                    w_ready(W_UP0 + n)
                    pe.wait_ge(s_u2, 2 * NORMED[b])
                    pe.wait_ge(s_gfree, U_OUT - 3 + q + 1)
                    unit(W_UP0 + n, q % 3, o, w).then_inc(s_g, 1)
                    q += 1
                elif kind == "back":
                    if tile[0] == 0:
                        pe.wait_ge(s_ev["OT"], 2 * NCH)
                        pe.wait_ge(s_ev["O"], 2 * NCH)
                    pe.wait_ge(s_gfree, U_OUT + BACK_UNITS[tile[0]])
                    back(tile[0])
                else:
                    forth(tile[0])

            def up(n, before, i=0):
                w_ready(n, i, 6)
                for b, (o, w) in enumerate(OBLOCKS):
                    pe.wait_ge(s_gfree, before + b - 2 + 12 * i)
                    unit(n, b, o, w).then_inc(s_g, 1)

            def down_part(n, u, q):
                t, half = divmod(u, 2)
                a1, a2 = (v[:, q, t * P:(t + 1) * P] for v in (a_hi, a_lo))
                w1, w2 = (v[:, (n + q) % SLOTS, half * 512:(half + 1) * 512] for v in (w_hi, w_lo))
                for m, (a, wt) in enumerate(((a1, w1), (a1, w2), (a2, w1))):
                    mm = pe.matmul(db[:, u % 4, :], a, wt, start=(q == 0 and m == 0), stop=(q == 1 and m == 2))
                return mm

            def down(n, i):
                w_ready(n + 1, i, 6)
                pe.wait_ge(s_alo, 2 * i + 2)
                for u in range(2 * KT):
                    if u > 3:
                        pe.wait_ge(s_dnfree, 16 * i + u - 3)
                    down_part(n, u, 0)
                    down_part(n, u, 1).then_inc(s_dn, 1)

            for j in range(2, 4):
                up(W_UP0 + j, U_UP0 + 3 * j)
            with pe.Fori(0, FFN_ITERS - 1) as i:
                up(W_FFN, U_FFN, i)
                up(W_FFN + 1, U_FFN + 3, i)
                down(W_FFN + 2, i)
                up(W_FFN + 4, U_FFN + 6, i)
                up(W_FFN + 5, U_FFN + 9, i)
                pe.wait_ge(s_dnfree, 16 * i + 2 * KT)
            w_ready(W_LAST + 1)
            pe.wait_ge(s_alo, FT - 1)
            for u in range(4):
                down_part(W_LAST, u, 0)
            for u in range(2 * KT):
                if u % KT == 0:
                    pe.wait_ge(s_alo, FT + u // KT)
                if u > 3:
                    pe.wait_ge(s_dnfree, 16 * (FFN_ITERS - 1) + u - 3)
                    down_part(W_LAST, u, 0)
                down_part(W_LAST, u, 1).then_inc(s_dn, 1)

        @block.scalar
        def _(act):
            def w_high(n, i=0, per=3):
                act.wait_ge(s_w[n % SLOTS], 16 * (n // SLOTS + 1) + 16 * (per // 3) * i)
                act.activation(w_hi[:, n % SLOTS, :], w_raw[:, n % SLOTS, :], ACT.Copy).then_inc(s_whi, 1)

            def root(j, n, src, junk, done):
                act.activation(junk, src, ACT.Square, accum_out=nss[0:n, j:j + 1])
                act.drain()
                act.activation(nss[0:n, j:j + 1], nss[0:n, j:j + 1], ACT.Sqrt, bias=eps_t[0:n, :],
                               scale=1.0 / D).then_inc(done, 1)

            def norm_root(j):
                n = META if j == 0 else P
                act.wait_ge(s_x[j % 3], 16 * (j // 3 + 1))
                if j >= 2:
                    act.wait_ge(s_nt, 2 * (j - 1))
                root(j, n, xt[0:n, j % 3, :], xs[0:n, j % 2, :], s_nsq)

            act.wait_ge(s_zero, 1)
            norm_root(0)
            for j in range(KT + 1):
                if j < KT:
                    norm_root(j + 1)
                n, c0 = (META, 0) if j == 0 else (P, META + (j - 1) * P)
                for h in range(2):
                    act.wait_ge(s_nt, 2 * j + h + 1)
                    act.activation(u_hi[:, 4 * h:4 * h + 4, c0:c0 + n], tbank(2 * (j % 2) + h, n),
                                   ACT.Copy).then_inc(s_uhi, 1)
                if j >= KT - 2:
                    w_high(W_AB + j - (KT - 2))

            act.wait_ge(s_prmT, 1)
            for r, (p0, m) in enumerate(((0, R_CF), (R_CF, 88), (R_CF + 88, 44))):
                act.activation(prm[:, p0:p0 + m], mb[:, r * P:r * P + m], ACT.Copy).then_inc(s_prm, 1)

            act.wait_ge(s_hd, 32)
            act.wait_ge(s_zero, 2)
            for b, (o, w) in enumerate(BLOCKS):
                act.wait_ge(s_g, b + 1)
                act.activation(ab_beta[:, PAD + o:PAD + o + w], gb[0:16, b, 0:w], ACT.Sigmoid)
                act.activation(ab_t[:, PAD + o:PAD + o + w], gb[0:16, b, 0:w], ACT.Identity,
                               bias=hdp[:, 0:1]).then_inc(s_gfree, 1)
            w_high(W_QKV + 2)
            act.drain()
            act.activation(ab_g[:, PAD:], ab_t[:, PAD:], ACT.Abs)
            act.activation(hdp[:, 2:3], hdp[:, 1:2], ACT.Exp)
            act.drain()
            act.activation(ab_g[:, PAD:], ab_g[:, PAD:], ACT.Exp, scale=-1.0)
            act.activation(ab_t[:, PAD:], ab_t[:, PAD:], ACT.Relu)
            act.drain()
            act.activation(ab_g[:, PAD:], ab_g[:, PAD:], ACT.Ln, bias=1.0).then_inc(s_na, 1)

            def silu(n):
                act.wait_ge(s_conv, n + 1)
                if not first(n):
                    act.wait_ge(s_tmps, 3 * n)
                act.activation(sl[:, PAD:], cacc[:, :], ACT.Silu).then_inc(s_sl, 1)

            def by_tokens(n):
                if not first(n):
                    act.wait_ge(s_sq, n)
                    act.wait_ge(s_spill, 16 * n)
                for r, (c0, c1) in enumerate(((0, 4), (4, 8), (8, NCH))):
                    act.wait_ge(s_tmps, 3 * n + r + 1)
                    t = act.activation(tm[:, c0:c1, :].rearrange("p c d -> p (c d)"), db[:, r, 0:(c1 - c0) * P],
                                       ACT.Copy)
                t.then_inc(s_tm, 1)
                act.wait_ge(s_tm, n + 1)
                act.dma_start(qkv_d[:, bass.ds(n * P, P)].rearrange("(c p) d -> p c d", p=P),
                              tm[:, :, :]).then_inc(s_spill, 16)

            def qkv_tile(j, i=0):
                n = j + 3 * i
                if j > 0:
                    act.wait_ge(s_g, 3 * n + 3)
                    w_high(W_QKV + j + 2, i)
                for b, (o, w) in enumerate(BLOCKS):
                    if b == 0 and j >= 3:
                        act.wait_ge(s_conv, n - 2)
                    act.wait_ge(s_g, U_QKV + 3 * n + b + 1)
                    act.activation(xb[:, j % 3, 3 + o:3 + o + w], gb[:, b, 0:w], ACT.Copy).then_inc(s_gfree, 1)
                    if b == 1 and j > 0:
                        silu(n - 1)
                if j > 0:
                    by_tokens(n - 1)

            act.wait_ge(s_zero, 3)
            for j in range(3):
                qkv_tile(j)
            with act.Fori(0, QKV_TILES // 3 - 1) as i:
                for j in range(3, 6):
                    qkv_tile(j, i)

            def exponentials():
                act.wait_ge(s_gsb, 1)
                act.activation(gtmp[:, 1, :], gflat(GCUM), ACT.Exp)
                act.activation(gtmp[:, 2, :], gtmp[:, 0, :], ACT.Exp)
                act.activation(gflat(EGT), mb[:, 360:360 + NCH * HEADS], ACT.Exp)
                act.wait_ge(s_ssq, QKV_TILES)
                act.activation(ssq[:, 0:2 * HEADS, :], ssq[:, 0:2 * HEADS, :], ACT.Sqrt, bias=eps_t).then_inc(s_exp, 1)

            for g, group in enumerate(GROUPS):
                act.wait_ge(s_g, 3 * (W_POOL + g))
                w_high(W_POOL + g + 2)
                for b, (o, w) in enumerate(BLOCKS):
                    if g and b == 0:
                        act.wait_ge(s_pw, g)
                    act.wait_ge(s_g, U_POOL + 3 * g + b + 1)
                    act.activation(px[:, 16 + o:16 + o + w], gb[:, b, 0:w], ACT.Copy).then_inc(s_gfree, 1)
                    if g == 0 and b == 1:
                        silu(QKV_TILES - 1)
                if g == 0:
                    by_tokens(QKV_TILES - 1)
                act.wait_ge(s_pw, g + 1)
                act.activation(p_hi[:, group, :], pool_out(group)[:, 16:], ACT.Copy).then_inc(s_phi, 1)
                if g == 1:
                    exponentials()
            act.wait_ge(s_g, U_WPOOL)
            w_high(W_WPOOL + 2)

            def scale_pool(j):
                tile = 2 * GROUPS[j // 2] + j % 2
                if j >= 2:
                    act.wait_ge(s_yb[j % 2], 16 * (j // 2))
                for b, (o, w) in enumerate(OBLOCKS):
                    act.wait_ge(s_g, U_WPOOL + 3 * j + b + 1)
                    act.activation(ybs[:, j % 2, o:o + w], gb[:, b, 0:w], ACT.Copy,
                                   scale=gain(R_PSC + tile, 1)).then_inc(s_gfree, 1)
                act.wait_ge(s_gfree, U_WPOOL + 3 * j + 3)
                act.dma_start(yb_d[tile * P:(tile + 1) * P, :], ybs[:, j % 2, :]).then_inc(s_yb[j % 2], 16)
                if j == KT - 1:
                    w_high(W_ZG + 2)

            def copy_halves(name, dst, c, turns=None):
                for h in range(2):
                    act.wait_ge(s_ps[name], 2 * (c if turns is None else turns) + h + 1)
                    act.activation(heads(dst, h), dbank(name, h), ACT.Copy).then_inc(s_ev[name], 1)

            def act_step(name, c):
                if name == "TQ":
                    copy_halves(name, qnt, c)
                elif name == "TKN":
                    copy_halves(name, knt, c)
                elif name == "TQD":
                    copy_halves(name, qdt, c)
                elif name == "TKG":
                    copy_halves(name, kgt, c)
                elif name == "GROW":
                    for h in range(2):
                        act.wait_ge(s_ev[name], 2 * c + h + 1)
                        act.activation(heads(ex, h), heads(ex, h), ACT.Exp).then_inc(s_dec, 1)
                elif name == "TT0":
                    copy_halves(name, rr, c - 1, turns=c)
                elif name in DOUBLING and name[0] == "T":
                    copy_halves(name, tt_m, c - 1)
                elif name == "V":
                    copy_halves(name, vv, c)
                elif name == "O":
                    for h in range(2):
                        act.wait_ge(s_ps[name], 2 * c + h + 1)
                        act.activation(heads(ots, h), dbank(name, h), ACT.Square).then_inc(s_osq, 1)
                        act.activation(heads(orx, h), dbank(name, h), ACT.Copy).then_inc(s_ev[name], 1)
                elif name == "SU":
                    act.wait_ge(s_oss, c + 1)
                    act.activation(orr, oss, ACT.Sqrt, bias=eps_t, scale=1.0 / P).then_inc(s_ort, 1)
                elif name == "OT":
                    copy_halves(name, ots, c)
                    act.wait_ge(s_ev[name], 2 * c + 2)
                    act.dma_start(ot_d[:, bass.ds(c * P, P)].rearrange("(h d) t -> d h t", d=P),
                                  ots[:, :, :]).then_inc(s_ot, 16)

            act.wait_ge(s_spill, 16 * QKV_TILES)
            for name in FIRST_PLAN:
                if name[0] == "pool":
                    scale_pool(name[1])
                else:
                    act_step(name, 0)
            for h in range(2):
                act.wait_ge(s_ps["TT0"], h + 1)
                act.activation(heads(rr, h), dbank("TT0", h), ACT.Copy).then_inc(s_ev[LAST_Y], 1)

            def gates(u, i):
                t, b = divmod(u, 3)
                o, w = OBLOCKS[b]
                if t == 0:
                    act.wait_ge(s_z, 3 * i + b + 1)
                    act.activation(zs[:, o:o + w], gb[:, b, 0:w], ACT.Sigmoid).then_inc(s_zsig, 1)
                else:
                    if t == 1:
                        act.wait_ge(s_yg, 16 * i + 16)
                    elif b == 0:
                        act.wait_ge(s_zg, i + 1)
                        act.dma_start(za_d[bass.ds(i * P, P), :], zs[:, :]).then_inc(s_za, 16)
                    act.wait_ge(s_g, U_ZG + 6 * i + 3 * (t - 1) + b + 1)
                    act.activation(gs[:, o:o + w], gb[:, b, 0:w], ACT.Sigmoid).then_inc(s_gfree, 1)
                if b == 2:
                    w_high(W_ZG + 3 + t, i)
                if u == 8:
                    act.wait_ge(s_gg, i + 1)
                    act.dma_start(yg_d[bass.ds(i * P, P), :], gs[:, :]).then_inc(s_yg, 16)

            with act.Fori(0, HEADS) as i:
                for name in STEPS:
                    act_step(name, i if name in REC else i + 1)
                    for u in units_after(name):
                        gates(u, i)
                act.wait_ge(s_ot, 16 * i + 16)
                act.wait_ge(s_za, 16 * i + 16)
            for name in REC:
                act_step(name, NCH - 1)

            def y_high(b):
                o, w = OBLOCKS[b]
                for hf in range(2):
                    ks = slice(4 * hf, 4 * hf + 4)
                    act.wait_ge(s_y1, 2 * b + hf + 1)
                    act.activation(u_hi[:, ks, o:o + w], yo[b % 2][:, ks, :], ACT.Copy).then_inc(s_yhi, 1)

            def high2(j):
                n, c0 = (HALO, 0) if j == 0 else (P, HALO + (j - 1) * P)
                for h in range(2):
                    act.wait_ge(s_hnt, 2 * j + h + 1)
                    act.activation(u_hi[:, 4 * h:4 * h + 4, c0:c0 + n], tbank(2 + h, n), ACT.Copy).then_inc(s_u2hi, 1)

            y_high(0)
            q = 0
            for kind, *tile in OUT_PLAN:
                if kind == "unit":
                    n, b = tile
                    o, w = OBLOCKS[b]
                    if n == 0 and b < 2:
                        y_high(b + 1)
                    act.wait_ge(s_g, U_OUT + q + 1)
                    act.activation(ht[:, n, o:o + w], gb[:, q % 3, 0:w], ACT.Copy).then_inc(s_gfree, 1)
                    q += 1
                    if b == 2:
                        w_high(W_OUT + n + 3)
                elif kind == "up":
                    n, b = tile
                    o, w = OBLOCKS[b]
                    act.wait_ge(s_g, U_OUT + q + 1)
                    act.activation((xg, xv)[n][:, o:o + w], gb[:, q % 3, 0:w], ACT.Copy).then_inc(s_gfree, 1)
                    q += 1
                elif kind == "back":
                    j = tile[0]
                    n = HALO if j == 0 else P
                    act.wait_ge(s_h2, 2 * j + 2)
                    if j >= 2:
                        act.wait_ge(s_hnt, 2 * (j - 1))
                    root(j, n, h2m[:, :] if j == 0 else h2[:, j - 1, :], hx[0:n, j % 2, :], s_h2sq)
                else:
                    high2(tile[0])

            def take(j, before, i=0):
                dst = xg if j % 2 == 0 else xv
                for b, (o, w) in enumerate(OBLOCKS):
                    act.wait_ge(s_g, before + b + 1 + 12 * i)
                    act.activation(dst[:, o:o + w], gb[:, b, 0:w], ACT.Copy).then_inc(s_gfree, 1)

            def gate(p):
                act.wait_ge(s_cg, p + 1)
                if not first(p):
                    act.wait_ge(s_act, p)
                act.activation(sg[:, :], cg[:, :], ACT.Silu).then_inc(s_sg, 1)

            def high(p, q, turns=None):
                if turns is not None:
                    act.wait_ge(s_dn, 16 * turns)
                act.wait_ge(s_act, p + 1)
                act.activation(a_hi[:, q, :], cv[:, :], ACT.Copy).then_inc(s_ahi, 1)

            for q in range(2):
                if q == 0:
                    w_high(W_UP0 + 3)
                    w_high(W_UP0 + 4)
                else:
                    act.wait_ge(s_cg, 1)
                    take(0, U_UP0 + 6)
                    w_high(W_UP0 + 5)
                    act.wait_ge(s_cv, 1)
                    take(1, U_UP0 + 9)
                if q == 0:
                    gate(0)
                    high(0, 0)
            with act.Fori(0, FFN_ITERS - 1) as i:
                gate(2 * i + 1)
                high(2 * i + 1, 1)
                act.wait_ge(s_g, U_FFN + 12 * i)
                w_high(W_FFN + 2, i, 6)
                act.wait_ge(s_cg, 2 * i + 2)
                take(0, U_FFN, i)
                w_high(W_FFN + 3, i, 6)
                act.wait_ge(s_cv, 2 * i + 2)
                take(1, U_FFN + 3, i)
                w_high(W_FFN + 4, i, 6)
                gate(2 * i + 2)
                high(2 * i + 2, 0, i + 1)
                w_high(W_FFN + 5, i, 6)
                w_high(W_FFN + 6, i, 6)
                act.wait_ge(s_cg, 2 * i + 3)
                take(0, U_FFN + 6, i)
                w_high(W_FFN + 7, i, 6)
                act.wait_ge(s_cv, 2 * i + 3)
                take(1, U_FFN + 9, i)
            gate(FT - 1)
            for hf in range(2):
                cols = slice(hf * SEQ // 2, (hf + 1) * SEQ // 2)
                act.wait_ge(s_act, FT + hf)
                act.activation(a_hi[:, 1, cols], cv[:, cols], ACT.Copy).then_inc(s_ahi, 1)

            for t in range(KT):
                act.wait_ge(s_dnfree, 16 * (FFN_ITERS - 1) + 2 * t + 2)
                root(t, P, h2[:, t, :], sg[:, :], s_fsq)

        @block.vector
        def _(dve):
            def drain():
                dve.drain()

            def scale(j):
                n = META if j == 0 else P
                dve.wait_ge(s_nsq, j + 1)
                dve.reciprocal(nss[0:n, j:j + 1], nss[0:n, j:j + 1])
                drain()
                dve.scalar_tensor_tensor(xs[0:n, j % 2, :], xt[0:n, j % 3, :], nss[0:n, j:j + 1], gmix[0:n, :],
                                         ALU.mult, ALU.mult).then_inc(s_xs, 1)

            dve.wait_ge(s_gmix, 32)
            scale(0)
            for j in range(KT + 1):
                if j < KT:
                    scale(j + 1)
                n, c0 = (META, 0) if j == 0 else (P, META + (j - 1) * P)
                for h in range(2):
                    dve.wait_ge(s_uhi, 2 * j + h + 1)
                    dst = slice(4 * h, 4 * h + 4), slice(c0, c0 + n)
                    dve.tensor_tensor(u_lo[:, dst[0], dst[1]], tbank(2 * (j % 2) + h, n),
                                      u_hi[:, dst[0], dst[1]].bitcast(F32), ALU.subtract).then_inc(s_u, 1)
            dve.wait_ge(s_prm, 3)

            dve.wait_ge(s_na, 1)
            dve.tensor_tensor(ab_g[:, PAD:], ab_g[:, PAD:], ab_t[:, PAD:], ALU.add)
            drain()
            dve.tensor_scalar(ab_g[:, PAD:], ab_g[:, PAD:], hdp[:, 2:3], -1.0, ALU.mult, ALU.mult).then_inc(s_ab, 1)

            taps = 4

            def conv(n, slot):
                dve.wait_ge(s_gfree, U_QKV + 3 * n + 3)
                if not first(n):
                    dve.wait_ge(s_sl, n)

                def tap(j):
                    return prm[:, bass.ds(R_CONV + j * QKV_TILES + n, 1)]

                dve.tensor_scalar(cacc[:, :], xb[:, slot, 3:3 + T], tap(taps - 1), None, ALU.mult)
                for j in range(taps - 2, -1, -1):
                    drain()
                    t = dve.scalar_tensor_tensor(cacc[:, :], xb[:, slot, j:j + T], tap(j), cacc[:, :],
                                                 ALU.mult, ALU.add)
                t.then_inc(s_conv, 1)

            def sums(n):
                dve.wait_ge(s_sq, n + 1)
                dve.tensor_reduce(ssq[:, bass.ds(n, 1), :].rearrange("p o c -> p (o c)"), sq[:, :, :], AX_X,
                                  ALU.add).then_inc(s_ssq, 1)

            dve.wait_ge(s_zero, 3)
            conv(0, 0)
            with dve.Fori(0, QKV_TILES // 3 - 1) as i:
                for j in range(3):
                    conv(1 + 3 * i + j, (1 + j) % 3)
                    sums(3 * i + j)
            for n in (QKV_TILES - 2, QKV_TILES - 1):
                conv(n, n % 3)
                sums(n - 1)

            def by_chunk(m):
                return mb[:, m * NCH * 16:(m + 1) * NCH * 16].rearrange("p (c k) -> p c k", k=16)

            def cumulate():
                dve.wait_ge(s_abT, 1)
                dve.tensor_copy(fac[:, FV, :, :], by_chunk(0)[:, :, 0:8])
                dve.tensor_copy(gtok[:, :].rearrange("p (c h) -> p c h", h=HEADS), by_chunk(1)[:, :, 8:16]).then_inc(s_gtok, 1)
                dve.wait_ge(s_gcum, 1)
                dve.tensor_copy(gflat(GCUM), mb[:, 288:288 + NCH * HEADS])
                drain()
                dve.tensor_tensor(gtmp[:, 0, :], mb[:, 360:360 + NCH * HEADS], gflat(GCUM), ALU.subtract).then_inc(s_gsb, 1)

            def factors():
                dve.wait_ge(s_exp, 1)
                dve.reciprocal(ssq[:, 0:2 * HEADS, :], ssq[:, 0:2 * HEADS, :])
                drain()
                rq = ssq[:, 0:HEADS, :].rearrange("p h c -> p c h")
                rk = ssq[:, HEADS:2 * HEADS, :].rearrange("p h c -> p c h")
                eg = gtmp[:, 1, :].rearrange("p (c h) -> p c h", h=HEADS)
                el = gtmp[:, 2, :].rearrange("p (c h) -> p c h", h=HEADS)
                dve.tensor_scalar(fac[:, FQ], rq, float(P) ** -0.5, None, ALU.mult)
                dve.tensor_copy(fac[:, FK], rk)
                dve.tensor_tensor(fac[:, FKD], rk, el, ALU.mult)
                dve.tensor_tensor(fac[:, FKB], rk, fac[:, FV], ALU.mult)
                drain()
                dve.tensor_tensor(fac[:, FQD], fac[:, FQ], eg, ALU.mult)
                dve.tensor_tensor(fac[:, FKG], fac[:, FKB], eg, ALU.mult).then_inc(s_fac, 1)
                drain()

            def scaled(f, n, src, kind, c):
                dve.tensor_tensor(form[:, n], tk[:, src * HEADS:(src + 1) * HEADS, :], per_head(factor(kind, c)),
                                  ALU.mult).then_inc(s_form[f], 1)

            def forms_first(c):
                dve.tensor_copy(gcur, factor(GCUM, c)).then_inc(s_gcp, 1)
                dve.wait_ge(s_tk, 16 * c + 16)
                scaled("kn", 0, 1, FK, c)
                scaled("kb", 1, 1, FKB, c)

            for q, g in enumerate(GROUPS):
                if q:
                    dve.wait_ge(s_phi, q)
                dve.wait_ge(s_gfree, U_POOL + 3 * q + 3)
                src = px
                for k in range(g + 1):
                    dst = (pa, pb)[k % 2]
                    dve.tensor_tensor(dst[:, 16:], src[:, 16:], src[:, 16 - 2 ** k:16 + T - 2 ** k], ALU.add)
                    drain()
                    src = dst
                dst = pool_out(g)
                dve.tensor_scalar(dst[:, 16:], src[:, 16:], 1.0 / WINDOWS[g], None, ALU.mult)
                drain()
                dve.tensor_tensor(dst[:, 16:32], dst[:, 16:32], cst[:, C_INV + 16 * g:C_INV + 16 * g + 16], ALU.mult)
                drain()
                dve.tensor_tensor(dst[:, 16:], dst[:, 16:], px[:, 16:], ALU.subtract).then_inc(s_pw, 1)
                dve.wait_ge(s_phi, q + 1)
                dve.tensor_tensor(p_lo[:, g, :], dst[:, 16:], p_hi[:, g, :].bitcast(F32),
                                  ALU.subtract).then_inc(s_plo, 1)
                drain()
                if q == 0:
                    sums(QKV_TILES - 1)
                    cumulate()
                elif q == 1:
                    factors()
                elif q == 2:
                    forms_first(0)

            def halves(name, turns, op, out_sem):
                for h in range(2):
                    dve.wait_ge(s_ps[name], 2 * turns + h + 1)
                    op(h).then_inc(out_sem, 1)

            def dve_step(name, c):
                if name == "TKN":
                    dve.wait_ge(s_ps[name], 2 * c + 2)
                elif name == "TKB":
                    halves(name, c, lambda h: dve.tensor_copy(heads(kbt, h), dbank(name, h)), s_ev[name])
                elif name == "GROW":
                    dve.wait_ge(s_nm, c + 1)
                    halves(name, c, lambda h: dve.tensor_tensor(heads(ex, h), dbank(name, h), heads(nmx, h),
                                                                ALU.subtract), s_ev[name])
                elif name == "KK":
                    for h in range(2):
                        dve.wait_ge(s_dec, 2 * c + h + 1)
                        dve.wait_ge(s_ps[name], 2 * c + h + 1)
                        dve.tensor_tensor(heads(at_m, h), dbank(name, h), heads(ex, h), ALU.mult).then_inc(s_ev[name], 1)
                    scaled("qn", 0, 0, FQ, c)
                    scaled("kg", 1, 1, FKG, c)
                elif name == "TQ":
                    dve.wait_ge(s_ps[name], 2 * c + 2)
                    scaled("qd", 0, 0, FQD, c)
                elif name == "QK":
                    halves(name, c, lambda h: dve.tensor_tensor(heads(qkm, h), dbank(name, h), heads(ex, h),
                                                                ALU.mult), s_ev[name])
                elif name[0] == "X":
                    halves(name, c - 1, lambda h: dve.tensor_tensor(
                        heads(nmx, h), dbank(name, h), over_heads(lvl(int(name[1])), HEADS // 2), ALU.mult), s_ev[name])
                elif name[0] == "Y":
                    halves(name, c - 1, lambda h: dve.tensor_tensor(heads(rr, h), heads(rr, h), dbank(name, h),
                                                                    ALU.subtract), s_ev[name])
                elif name == "P1":
                    dve.wait_ge(s_vb, c + 1)
                    halves(name, c, lambda h: dve.tensor_tensor(heads(orx, h), heads(vb, h), dbank(name, h),
                                                                ALU.subtract), s_ev[name])
                elif name == "O":
                    dve.wait_ge(s_ps[name], 2 * c + 2)
                    dve.tensor_tensor(st[:, :, :], st[:, :, :], per_head(factor(EGT, c)), ALU.mult)
                    dve.wait_ge(s_osq, 2 * c + 2)
                    dve.tensor_reduce(oss, ots[:, :, :], AX_X, ALU.add).then_inc(s_oss, 1)
                elif name == "SU":
                    drain()
                    halves(name, c, lambda h: dve.tensor_tensor(heads(st, h), heads(st, h), dbank(name, h),
                                                                ALU.add), s_ev[name])
                elif name == "TQD":
                    output_scale(c - 1)

            def output_scale(c):
                dve.wait_ge(s_ort, c + 1)
                dve.reciprocal(orr, orr)
                drain()
                dve.wait_ge(s_ev["O"], 2 * c + 2)
                dve.tensor_tensor(orx[:, :, :], orx[:, :, :], per_head(orr), ALU.mult).then_inc(s_on, 1)

            for name in PREP_STEPS:
                if name != "TQD":
                    dve_step(name, 0)

            def gated(u, i):
                t, b = divmod(u, 3)
                o, w = OBLOCKS[b]
                if t == 0:
                    dve.wait_ge(s_zsig, 3 * i + b + 1)
                    dve.scalar_tensor_tensor(zs[:, o:o + w], zs[:, o:o + w], gain(R_HN, 1), gb[:, b, 0:w],
                                             ALU.mult, ALU.mult).then_inc(s_zfree, 1)
                elif u == 5:
                    dve.wait_ge(s_gfree, U_ZG + 6 * i + 3)
                    dve.tensor_tensor(zs[:, :], zs[:, :], gs[:, :], ALU.mult).then_inc(s_zg, 1)
                elif u == 8:
                    dve.wait_ge(s_gfree, U_ZG + 6 * i + 6)
                    dve.wait_ge(s_yl, 16 * i + 16)
                    dve.tensor_tensor(gs[:, :], gs[:, :], yl[:, :], ALU.mult).then_inc(s_gg, 1)

            dve.wait_ge(s_ev["SU"], 2)
            with dve.Fori(0, HEADS) as i:
                dve_step("P1", i)
                forms_first(i + 1)
                for name in STEPS[1:]:
                    dve_step(name, i if name in REC else i + 1)
                    for u in units_after(name):
                        gated(u, i)
            def y_product(b):
                s = b % 2
                dve.wait_ge(s_yin[s], 32 * (b // 2 + 1))
                for ks in FEATURE_HALVES:
                    dve.tensor_tensor(yo[s][:, ks, :], yo[s][:, ks, :], yz[s][:, ks, :], ALU.mult)

            dve_step("P1", NCH - 1)
            y_product(0)
            dve.wait_ge(s_osq, 2 * NCH)
            dve.tensor_reduce(oss, ots[:, :, :], AX_X, ALU.add).then_inc(s_oss, 1)
            output_scale(NCH - 1)

            def y_low(b):
                o, w = OBLOCKS[b]
                s = b % 2
                dve.wait_ge(s_ygin[s], 16 * (b // 2 + 1))
                if b:
                    y_product(b)
                drain()
                for ks in FEATURE_HALVES:
                    dve.tensor_tensor(yo[s][:, ks, :], yo[s][:, ks, :], yg[s][:, ks, :], ALU.add).then_inc(s_y1, 1)
                for hf, ks in enumerate(FEATURE_HALVES):
                    dve.wait_ge(s_yhi, 2 * b + hf + 1)
                    dve.tensor_tensor(u_lo[:, ks, o:o + w], yo[s][:, ks, :], u_hi[:, ks, o:o + w].bitcast(F32),
                                      ALU.subtract).then_inc(s_y, 1)

            for b in range(len(OBLOCKS)):
                y_low(b)

            def residual(j):
                n = HALO if j == 0 else P
                for h in range(2):
                    dst = h2m[:, h * 512:(h + 1) * 512] if j == 0 else h2[:, j - 1, h * 512:(h + 1) * 512]
                    dve.wait_ge(s_h2x[j // 3], 32 if j < 3 else 16)
                    dve.wait_ge(s_h2T, 2 * j + h + 1)
                    dve.tensor_tensor(dst, dst, db[0:n, h, :], ALU.add).then_inc(s_h2, 1)

            def scale2(j):
                n = HALO if j == 0 else P
                dve.wait_ge(s_h2sq, j + 1)
                dve.reciprocal(nss[0:n, j:j + 1], nss[0:n, j:j + 1])
                drain()
                dve.scalar_tensor_tensor(hx[0:n, j % 2, :], h2m[:, :] if j == 0 else h2[:, j - 1, :], nss[0:n, j:j + 1],
                                         gffn[0:n, :], ALU.mult, ALU.mult).then_inc(s_hx, 1)

            dve.wait_ge(s_gffn, 16)

            def low2(j):
                n, c0 = (HALO, 0) if j == 0 else (P, HALO + (j - 1) * P)
                for h in range(2):
                    dve.wait_ge(s_u2hi, 2 * j + h + 1)
                    dst = slice(4 * h, 4 * h + 4), slice(c0, c0 + n)
                    dve.tensor_tensor(u_lo[:, dst[0], dst[1]], tbank(2 + h, n),
                                      u_hi[:, dst[0], dst[1]].bitcast(F32), ALU.subtract).then_inc(s_u2, 1)

            for kind, *tile in OUT_PLAN:
                if kind == "back":
                    residual(tile[0])
                    if tile[0]:
                        low2(tile[0] - 1)
                elif kind == "forth":
                    scale2(tile[0])
            low2(KT)

            def conv3(dst, src, f, done, c0=0, c1=SEQ):
                def tap(j):
                    return prm[:, bass.ds(R_CF + j * 2 * FT + f, 1)]
                dve.tensor_scalar(dst[:, c0:c1], src[:, c0 + 2:c1 + 2], tap(2), None, ALU.mult)
                drain()
                dve.scalar_tensor_tensor(dst[:, c0:c1], src[:, c0 + 1:c1 + 1], tap(1), dst[:, c0:c1], ALU.mult, ALU.add)
                drain()
                dve.scalar_tensor_tensor(dst[:, c0:c1], src[:, c0:c1], tap(0), dst[:, c0:c1], ALU.mult,
                                         ALU.add).then_inc(done, 1)

            def hidden(p, taken, more=3, downs=None):
                dve.wait_ge(s_gfree, taken)
                if not first(p):
                    dve.wait_ge(s_sg, p)
                conv3(cg, xg, p, s_cg)
                dve.wait_ge(s_gfree, taken + more)
                conv3(cv, xv, FT + p, s_cv)
                if downs is not None:
                    add_down(downs, 0, 2)
                drain()
                dve.wait_ge(s_sg, p + 1)
                dve.tensor_tensor(cv[:, :], cv[:, :], sg[:, :], ALU.mult).then_inc(s_act, 1)

            def low(p, q):
                dve.wait_ge(s_ahi, p + 1)
                dve.tensor_tensor(a_lo[:, q, :], cv[:, :], a_hi[:, q, :].bitcast(F32), ALU.subtract).then_inc(s_alo, 1)

            def add_down(i, u0, u1):
                for u in range(u0, u1):
                    t, half = divmod(u, 2)
                    dve.wait_ge(s_dn, 16 * i + u + 1)
                    dst = h2[:, t, half * 512:(half + 1) * 512]
                    dve.tensor_tensor(dst, dst, db[:, u % 4, :], ALU.add).then_inc(s_dnfree, 1)

            hidden(0, U_UP0 + 5, 1)
            low(0, 0)
            with dve.Fori(0, FFN_ITERS - 1) as i:
                hidden(2 * i + 1, U_FFN - 3 + 12 * i)
                low(2 * i + 1, 1)
                hidden(2 * i + 2, U_FFN + 3 + 12 * i, downs=i)
                add_down(i, 2, 2 * KT)
                low(2 * i + 2, 0)
            dve.wait_ge(s_gfree, U_FFN - 3 + 12 * (FFN_ITERS - 1))
            dve.wait_ge(s_sg, FT - 1)
            conv3(cg, xg, FT - 1, s_cg)
            for hf in range(2):
                c0, c1 = hf * SEQ // 2, (hf + 1) * SEQ // 2
                dve.wait_ge(s_gfree, U_FFN - 1 + hf + 12 * (FFN_ITERS - 1))
                conv3(cv, xv, 2 * FT - 1, s_cv, c0, c1)
                drain()
                dve.wait_ge(s_sg, FT)
                dve.tensor_tensor(cv[:, c0:c1], cv[:, c0:c1], sg[:, c0:c1], ALU.mult).then_inc(s_act, 1)
            for hf in range(2):
                c0, c1 = hf * SEQ // 2, (hf + 1) * SEQ // 2
                dve.wait_ge(s_ahi, FT + hf)
                dve.tensor_tensor(a_lo[:, 1, c0:c1], cv[:, c0:c1], a_hi[:, 1, c0:c1].bitcast(F32),
                                  ALU.subtract).then_inc(s_alo, 1)

            def final(t):
                dve.wait_ge(s_fsq, t + 1)
                dve.reciprocal(nss[:, t:t + 1], nss[:, t:t + 1])
                drain()
                if t >= OUT_SLOTS:
                    dve.wait_ge(s_out[t % OUT_SLOTS], 16 * (t // OUT_SLOTS))
                dve.scalar_tensor_tensor(fino[:, t % OUT_SLOTS, :], h2[:, t, :], nss[:, t:t + 1], fing[:, :],
                                         ALU.mult, ALU.mult).then_inc(s_fin, 1)

            dve.wait_ge(s_fg, 16)
            for t in range(KT):
                add_down(FFN_ITERS - 1, 2 * t, 2 * t + 2)
                if t:
                    final(t - 1)
            final(KT - 1)


def kernel(**inputs):
    import concourse.bacc as bacc
    from concourse.bass_utils import run_bass_kernel_spmd

    names = ["x", "meta_tokens", "norm_mix", "w_in", "conv_qkv", "a_log", "dt_bias", "head_norm", "w_pool",
             "pool_scale", "w_out", "norm_ffn", "w_up", "conv_ffn", "w_down", "norm_final"]
    nc = bacc.Bacc("TRN2", target_bir_lowering=False, num_devices=1)
    arrays = {f"in_{n}": np.ascontiguousarray(inputs[n]) for n in names}
    arrays["in_constants"] = constants()
    args = [nc.dram_tensor(n, a.shape, mybir.dt.from_np(a.dtype), kind="ExternalInput").ap()
            for n, a in arrays.items()]
    args.append(nc.dram_tensor("out_h", (1, SEQ, D), F32, kind="ExternalOutput").ap())
    hybrid_block(nc, *args)
    r = run_bass_kernel_spmd(nc, [arrays], core_ids=[0])
    return r.results[0]["out_h"]
```
